# Optimizing a Trainium2 kernel written in Bass

```python
import math
import jax
import jax.numpy as jnp
from jax import lax
import numpy as np

D_MODEL = 1024
BATCH = 1
SEQ = 512
DEPTH = 2

MIX_WIDTH = D_MODEL
N_MIXERS = 4
GROUP_WIDTH = MIX_WIDTH // N_MIXERS
HEAD_DIM = 64
N_HEADS_GROUP = GROUP_WIDTH // HEAD_DIM
ROPE_THETA = 10000.0
NORM_EPS = 1e-6
Q_BLOCK = 128
NEG_INF = -1e30

NSA_CMP_LEN = 32
NSA_CMP_STRIDE = 16
NSA_CMP_HIDDEN = 2 * HEAD_DIM
NSA_SEL_LEN = 64
NSA_TOP_N = 16
NSA_WINDOW = 512
NSA_FORCE_BONUS = 1e3

GDN_CONV = 4
GDN_CHUNK = 64

MLSTM_QK_DIM = HEAD_DIM // 2
MLSTM_CHUNK = 64
MLSTM_GATE_CAP = 15.0

DIFF_SUB_DIM = HEAD_DIM // 2

MEM_TOKENS = 256
MEM_HEADS = 4
MEM_HEAD_DIM = 64

MOE_GROUPS = 4
MOE_EXPERTS_PER_GROUP = 8
MOE_N_EXPERTS = MOE_GROUPS * MOE_EXPERTS_PER_GROUP
MOE_TOP_K = 2
MOE_FF = D_MODEL // 4
MOE_TOKEN_BLOCK = 128

IN_WIDTHS = (
    GROUP_WIDTH, HEAD_DIM, HEAD_DIM, HEAD_DIM, HEAD_DIM, HEAD_DIM, HEAD_DIM, 3 * N_HEADS_GROUP,
    GROUP_WIDTH, GROUP_WIDTH, GROUP_WIDTH, N_HEADS_GROUP, N_HEADS_GROUP, GROUP_WIDTH,
    N_HEADS_GROUP * MLSTM_QK_DIM, N_HEADS_GROUP * MLSTM_QK_DIM, GROUP_WIDTH, N_HEADS_GROUP, N_HEADS_GROUP, GROUP_WIDTH,
    GROUP_WIDTH, GROUP_WIDTH, GROUP_WIDTH,
)
IN_COLS = sum(IN_WIDTHS)

kernel_name = 'hybrid_nsa_gdn_mlstm_diffattn_hmoe'

def rms_norm(x, g):
    xf = x.astype(jnp.float32)
    y = xf * lax.rsqrt(jnp.mean(xf * xf, axis=-1, keepdims=True) + NORM_EPS)
    return (y * g.astype(jnp.float32)).astype(x.dtype)

def l2_normalize(x):
    return x * lax.rsqrt(jnp.sum(x * x, axis=-1, keepdims=True) + NORM_EPS)

def rope_tables(pos, dim):
    inv_freq = 1.0 / (ROPE_THETA ** (jnp.arange(0, dim, 2, dtype=jnp.float32) / dim))
    ang = pos.astype(jnp.float32)[:, None] * inv_freq[None, :]
    return jnp.cos(ang), jnp.sin(ang)

def apply_rope(x, cos, sin):
    x1, x2 = jnp.split(x.astype(jnp.float32), 2, axis=-1)
    return jnp.concatenate([x1 * cos - x2 * sin, x2 * cos + x1 * sin], axis=-1).astype(x.dtype)

def masked_softmax(s, mask):
    p = jax.nn.softmax(jnp.where(mask, s, NEG_INF), axis=-1)
    return jnp.where(mask, p, 0.0)

def soft_cap(x, cap):
    return cap * jnp.tanh(x / cap)

def causal_depthwise_conv(x, w):
    k_len, ch = w.shape
    return lax.conv_general_dilated(
        x, w[:, None, :].astype(x.dtype), window_strides=(1,), padding=[(k_len - 1, 0)],
        dimension_numbers=('NWC', 'WIO', 'NWC'), feature_group_count=ch)

def nsa_overlap(n_cmp, n_sel):
    c0 = NSA_CMP_STRIDE * np.arange(n_cmp)[:, None]
    s0 = NSA_SEL_LEN * np.arange(n_sel)[None, :]
    ov = np.clip(np.minimum(c0 + NSA_CMP_LEN, s0 + NSA_SEL_LEN) - np.maximum(c0, s0), 0, None)
    return (ov / NSA_CMP_STRIDE).astype(np.float32)

def nsa_mixer(q, kc, vc, ks, vs, kw, vw, gates, qk_gain, cmp_pe, cmp_w1, cmp_w2, cos, sin):
    B, S, _ = q.shape
    H, Dh = N_HEADS_GROUP, HEAD_DIM
    scale = Dh ** -0.5
    nb = S // Q_BLOCK
    n_cmp = (S - NSA_CMP_LEN) // NSA_CMP_STRIDE + 1
    n_sel = S // NSA_SEL_LEN
    n_top = min(NSA_TOP_N, n_sel)

    q = apply_rope(rms_norm(q.reshape(B, S, H, Dh), qk_gain[0]).transpose(0, 2, 1, 3), cos, sin)

    cmp_idx = NSA_CMP_STRIDE * np.arange(n_cmp)[:, None] + np.arange(NSA_CMP_LEN)[None, :]
    cmp_end = NSA_CMP_STRIDE * np.arange(n_cmp) + NSA_CMP_LEN - 1

    def compress(t, j):
        blocks = t[:, cmp_idx] + cmp_pe[j]
        hid = jax.nn.gelu(blocks.reshape(B, n_cmp, -1) @ cmp_w1[j])
        return hid @ cmp_w2[j]

    kc = apply_rope(rms_norm(compress(kc, 0), qk_gain[1]), cos[cmp_end], sin[cmp_end])
    vc = compress(vc, 1)
    ks = apply_rope(rms_norm(ks, qk_gain[2]), cos, sin)
    ks_blocks = ks.reshape(B, n_sel, NSA_SEL_LEN, Dh)
    vs_blocks = vs.reshape(B, n_sel, NSA_SEL_LEN, Dh)
    kw = apply_rope(rms_norm(kw, qk_gain[3]), cos, sin)
    kw_pad = jnp.pad(kw, ((0, 0), (NSA_WINDOW, 0), (0, 0)))
    vw_pad = jnp.pad(vw, ((0, 0), (NSA_WINDOW, 0), (0, 0)))
    gates = jax.nn.sigmoid(gates.reshape(B, S, H, 3).transpose(0, 2, 1, 3))
    overlap = jnp.asarray(nsa_overlap(n_cmp, n_sel))
    sel_ids = jnp.arange(n_sel)
    win_offs = jnp.arange(Q_BLOCK + NSA_WINDOW)

    def block(i):
        t0 = i * Q_BLOCK
        t = t0 + jnp.arange(Q_BLOCK)
        qb = lax.dynamic_slice_in_dim(q, t0, Q_BLOCK, axis=2)
        gb = lax.dynamic_slice_in_dim(gates, t0, Q_BLOCK, axis=2)
        s = jnp.einsum('bhqd,bcd->bhqc', qb, kc).astype(jnp.float32) * scale
        p_c = masked_softmax(s, cmp_end[None, :] <= t[:, None])
        o_c = jnp.einsum('bhqc,bcd->bhqd', p_c.astype(vc.dtype), vc)
        imp = jnp.einsum('bhqc,cn->bqn', p_c, overlap)
        cur = t // NSA_SEL_LEN
        valid = sel_ids[None, :] <= cur[:, None]
        forced = (sel_ids[None, :] == 0) | (sel_ids[None, :] == cur[:, None]) | (sel_ids[None, :] == cur[:, None] - 1)
        score = jnp.where(valid, imp + jnp.where(forced, NSA_FORCE_BONUS, 0.0), NEG_INF)
        _, idx = lax.top_k(score, n_top)
        kg = jax.vmap(lambda kb, ix: kb[ix])(ks_blocks, idx)
        vg = jax.vmap(lambda vb, ix: vb[ix])(vs_blocks, idx)
        s = jnp.einsum('bhqd,bqnrd->bhqnr', qb, kg).astype(jnp.float32) * scale
        kpos = idx[..., None] * NSA_SEL_LEN + jnp.arange(NSA_SEL_LEN)
        sel_mask = (kpos <= t[None, :, None, None]).reshape(B, 1, Q_BLOCK, -1)
        p_s = masked_softmax(s.reshape(B, H, Q_BLOCK, -1), sel_mask)
        o_s = jnp.einsum('bhqk,bqkd->bhqd', p_s.astype(vg.dtype), vg.reshape(B, Q_BLOCK, -1, Dh))
        kwb = lax.dynamic_slice_in_dim(kw_pad, t0, Q_BLOCK + NSA_WINDOW, axis=1)
        vwb = lax.dynamic_slice_in_dim(vw_pad, t0, Q_BLOCK + NSA_WINDOW, axis=1)
        spos = t0 - NSA_WINDOW + win_offs
        dist = t[:, None] - spos[None, :]
        w_mask = (dist >= 0) & (dist < NSA_WINDOW) & (spos[None, :] >= 0)
        s = jnp.einsum('bhqd,bkd->bhqk', qb, kwb).astype(jnp.float32) * scale
        p_w = masked_softmax(s, w_mask)
        o_w = jnp.einsum('bhqk,bkd->bhqd', p_w.astype(vwb.dtype), vwb)
        return gb[..., 0:1] * o_c + gb[..., 1:2] * o_s + gb[..., 2:3] * o_w

    out = lax.map(block, jnp.arange(nb))
    return out.transpose(1, 0, 3, 2, 4).reshape(B, S, H * Dh)

def gated_delta_chunked(q, k, v, g, beta):
    B, H, S, Dk = q.shape
    Dv = v.shape[-1]
    C = GDN_CHUNK
    N = S // C
    q = q.reshape(B, H, N, C, Dk)
    k = k.reshape(B, H, N, C, Dk)
    v = v.reshape(B, H, N, C, Dv)
    g = g.reshape(B, H, N, C)
    beta = beta.reshape(B, H, N, C)
    gc = jnp.cumsum(g, axis=-1)
    incl = jnp.tril(jnp.ones((C, C), bool))
    strict = jnp.tril(jnp.ones((C, C), bool), -1)
    decay = jnp.exp(jnp.where(incl, gc[..., :, None] - gc[..., None, :], NEG_INF))
    k_beta = k * beta[..., None]
    a_low = jnp.where(strict, jnp.einsum('bhnid,bhnjd->bhnij', k_beta, k) * decay, 0.0)
    system = a_low + jnp.eye(C, dtype=jnp.float32)
    rhs = jnp.concatenate([v * beta[..., None], k_beta * jnp.exp(gc)[..., None]], axis=-1)
    sol = lax.linalg.triangular_solve(system, rhs, left_side=True, lower=True)
    u, w = sol[..., :Dv], sol[..., Dv:]
    qd = q * jnp.exp(gc)[..., None]
    attn = jnp.einsum('bhnid,bhnjd->bhnij', q, k) * decay
    g_last = gc[..., -1]
    k_end = k * jnp.exp(g_last[..., None] - gc)[..., None]

    def step(state, xs):
        qd_c, w_c, u_c, a_c, ke_c, gl_c = xs
        v_new = u_c - jnp.einsum('bhck,bhkv->bhcv', w_c, state)
        o_c = jnp.einsum('bhck,bhkv->bhcv', qd_c, state) + jnp.einsum('bhcj,bhjv->bhcv', a_c, v_new)
        state = state * jnp.exp(gl_c)[..., None, None] + jnp.einsum('bhck,bhcv->bhkv', ke_c, v_new)
        return state, o_c

    xs = tuple(jnp.moveaxis(t, 2, 0) for t in (qd, w, u, attn, k_end, g_last))
    _, o = lax.scan(step, jnp.zeros((B, H, Dk, Dv), jnp.float32), xs)
    return jnp.moveaxis(o, 0, 2).reshape(B, H, S, Dv)

def gdn_mixer(q, k, v, a, b, z, conv_w, a_log, dt_bias, norm_g):
    B, S, _ = q.shape
    H, Dh = N_HEADS_GROUP, HEAD_DIM
    dtype = q.dtype
    qkv = jax.nn.silu(causal_depthwise_conv(jnp.concatenate([q, k, v], axis=-1), conv_w))
    q, k, v = jnp.split(qkv, 3, axis=-1)
    heads = lambda t: t.reshape(B, S, H, Dh).transpose(0, 2, 1, 3).astype(jnp.float32)
    q = l2_normalize(heads(q)) * Dh ** -0.5
    k = l2_normalize(heads(k))
    v = heads(v)
    beta = jax.nn.sigmoid(b.astype(jnp.float32)).transpose(0, 2, 1)
    g = -jnp.exp(a_log.astype(jnp.float32)) * jax.nn.softplus(a.astype(jnp.float32) + dt_bias.astype(jnp.float32))
    o = gated_delta_chunked(q, k, v, g.transpose(0, 2, 1), beta)
    o = rms_norm(o.transpose(0, 2, 1, 3), norm_g) * jax.nn.silu(z.astype(jnp.float32).reshape(B, S, H, Dh))
    return o.reshape(B, S, H * Dh).astype(dtype)

def mlstm_chunked(q, k, v, i_g, log_f):
    B, H, S, Dk = q.shape
    Dv = v.shape[-1]
    C = MLSTM_CHUNK
    N = S // C
    q = q.reshape(B, H, N, C, Dk)
    k = k.reshape(B, H, N, C, Dk)
    v = v.reshape(B, H, N, C, Dv)
    i_g = i_g.reshape(B, H, N, C)
    b = jnp.cumsum(log_f.reshape(B, H, N, C), axis=-1)
    causal = jnp.tril(jnp.ones((C, C), bool))
    d_log = jnp.where(causal, b[..., :, None] - b[..., None, :] + i_g[..., None, :], NEG_INF)
    a_end = b[..., -1:] - b + i_g
    m_loc = jnp.max(a_end, axis=-1)
    w_end = jnp.exp(a_end - m_loc[..., None])
    c_loc = jnp.einsum('bhncd,bhnce,bhnc->bhnde', k, v, w_end)
    n_loc = jnp.einsum('bhncd,bhnc->bhnd', k, w_end)
    b_last = b[..., -1]

    def step(carry, xs):
        c_st, n_st, m_st = carry
        c_l, n_l, m_l, b_l = xs
        m_new = jnp.maximum(b_l + m_st, m_l)
        s_prev = jnp.exp(b_l + m_st - m_new)
        s_loc = jnp.exp(m_l - m_new)
        c_new = s_prev[..., None, None] * c_st + s_loc[..., None, None] * c_l
        n_new = s_prev[..., None] * n_st + s_loc[..., None] * n_l
        return (c_new, n_new, m_new), (c_st, n_st, m_st)

    init = (jnp.zeros((B, H, Dk, Dv), jnp.float32), jnp.zeros((B, H, Dk), jnp.float32), jnp.zeros((B, H), jnp.float32))
    xs = tuple(jnp.moveaxis(t, 2, 0) for t in (c_loc, n_loc, m_loc, b_last))
    _, (c_in, n_in, m_in) = lax.scan(step, init, xs)
    c_in = jnp.moveaxis(c_in, 0, 2)
    n_in = jnp.moveaxis(n_in, 0, 2)
    m_in = jnp.moveaxis(m_in, 0, 2)
    inter_log = b + m_in[..., None]
    m_t = jnp.maximum(inter_log, jnp.max(d_log, axis=-1))
    w_inter = jnp.exp(inter_log - m_t)
    w_intra = jnp.exp(d_log - m_t[..., None]) * jnp.einsum('bhncd,bhnsd->bhncs', q, k)
    num = w_inter[..., None] * jnp.einsum('bhncd,bhnde->bhnce', q, c_in) + jnp.einsum('bhncs,bhnse->bhnce', w_intra, v)
    den = w_inter * jnp.einsum('bhncd,bhnd->bhnc', q, n_in) + jnp.sum(w_intra, axis=-1)
    h = num / jnp.maximum(jnp.abs(den), jnp.exp(-m_t))[..., None]
    return h.reshape(B, H, S, Dv)

def mlstm_mixer(q, k, v, i_pre, f_pre, o_pre, i_bias, f_bias, norm_g):
    B, S, _ = q.shape
    H = N_HEADS_GROUP
    dtype = q.dtype
    heads = lambda t, d: t.reshape(B, S, H, d).transpose(0, 2, 1, 3).astype(jnp.float32)
    q = heads(q, MLSTM_QK_DIM)
    k = heads(k, MLSTM_QK_DIM) * MLSTM_QK_DIM ** -0.5
    v = heads(v, HEAD_DIM)
    i_g = soft_cap(i_pre.astype(jnp.float32) + i_bias.astype(jnp.float32), MLSTM_GATE_CAP).transpose(0, 2, 1)
    log_f = jax.nn.log_sigmoid(soft_cap(f_pre.astype(jnp.float32) + f_bias.astype(jnp.float32), MLSTM_GATE_CAP)).transpose(0, 2, 1)
    h = mlstm_chunked(q, k, v, i_g, log_f)
    h = rms_norm(h.transpose(0, 2, 1, 3), norm_g) * jax.nn.sigmoid(o_pre.astype(jnp.float32).reshape(B, S, H, HEAD_DIM))
    return h.reshape(B, S, H * HEAD_DIM).astype(dtype)

def diff_mixer(q, k, v, qk_gain, lam, norm_g, lambda_init, cos, sin):
    B, S, _ = q.shape
    H, d = N_HEADS_GROUP, DIFF_SUB_DIM
    nb = S // Q_BLOCK
    q = apply_rope(rms_norm(q.reshape(B, S, H, 2, d).transpose(0, 2, 3, 1, 4), qk_gain[0]), cos, sin)
    k = apply_rope(rms_norm(k.reshape(B, S, H, 2, d).transpose(0, 2, 3, 1, 4), qk_gain[1]), cos, sin)
    v = v.reshape(B, S, H, HEAD_DIM).transpose(0, 2, 1, 3)
    lam = lam.astype(jnp.float32)
    lam_full = jnp.exp(jnp.sum(lam[0] * lam[1])) - jnp.exp(jnp.sum(lam[2] * lam[3])) + lambda_init
    scale = d ** -0.5
    kpos = jnp.arange(S)

    def block(i):
        t0 = i * Q_BLOCK
        qb = lax.dynamic_slice_in_dim(q, t0, Q_BLOCK, axis=3)
        s = jnp.einsum('bhcqd,bhckd->bhcqk', qb, k).astype(jnp.float32) * scale
        p = masked_softmax(s, kpos[None, :] <= (t0 + jnp.arange(Q_BLOCK))[:, None])
        a = p[:, :, 0] - lam_full * p[:, :, 1]
        return jnp.einsum('bhqk,bhkd->bhqd', a.astype(v.dtype), v)

    o = lax.map(block, jnp.arange(nb))
    o = o.transpose(1, 0, 3, 2, 4).reshape(B, S, H, HEAD_DIM)
    o = rms_norm(o, norm_g) * (1.0 - lambda_init)
    return o.reshape(B, S, H * HEAD_DIM)

def memory_cross_attention(hn, memn, wq, wkv, qk_gain, wo):
    B, S, _ = hn.shape
    M = memn.shape[1]
    q = (hn @ wq).reshape(B, S, MEM_HEADS, MEM_HEAD_DIM).transpose(0, 2, 1, 3)
    k, v = jnp.split(memn @ wkv, 2, axis=-1)
    k = k.reshape(B, M, MEM_HEADS, MEM_HEAD_DIM).transpose(0, 2, 1, 3)
    v = v.reshape(B, M, MEM_HEADS, MEM_HEAD_DIM).transpose(0, 2, 1, 3)
    q = rms_norm(q, qk_gain[0])
    k = rms_norm(k, qk_gain[1])
    s = jnp.einsum('bhsd,bhmd->bhsm', q, k).astype(jnp.float32) * MEM_HEAD_DIM ** -0.5
    p = jax.nn.softmax(s, axis=-1)
    o = jnp.einsum('bhsm,bhmd->bhsd', p.astype(v.dtype), v)
    return o.transpose(0, 2, 1, 3).reshape(B, S, MEM_HEADS * MEM_HEAD_DIM) @ wo

def hierarchical_moe(hn, w_group, b_group, w_expert, b_expert, w1, w3, w2):
    B, S, D = hn.shape
    xt = hn.reshape(-1, D)
    T = xt.shape[0]
    grp_prob = jax.nn.softmax((xt @ w_group).astype(jnp.float32) + b_group.astype(jnp.float32), axis=-1)
    grp_p, grp_idx = lax.top_k(grp_prob, 1)
    exp_logits = ((xt @ w_expert).astype(jnp.float32) + b_expert.astype(jnp.float32)).reshape(T, MOE_GROUPS, MOE_EXPERTS_PER_GROUP)
    exp_logits = jnp.take_along_axis(exp_logits, grp_idx[:, :, None], axis=1)[:, 0]
    top_p, top_idx = lax.top_k(jax.nn.softmax(exp_logits, axis=-1), MOE_TOP_K)
    top_w = top_p / jnp.sum(top_p, axis=-1, keepdims=True) * grp_p
    w_in_group = jnp.sum(jax.nn.one_hot(top_idx, MOE_EXPERTS_PER_GROUP, dtype=jnp.float32) * top_w[..., None], axis=1)
    combine = (jax.nn.one_hot(grp_idx[:, 0], MOE_GROUPS, dtype=jnp.float32)[:, :, None] * w_in_group[:, None, :])
    combine = combine.reshape(T, MOE_N_EXPERTS).astype(xt.dtype)
    nblk = T // MOE_TOKEN_BLOCK

    def block(args):
        xb, cb = args
        hg = jnp.einsum('td,edf->tef', xb, w1)
        hu = jnp.einsum('td,edf->tef', xb, w3)
        act = jax.nn.silu(hg) * hu * cb[:, :, None]
        return jnp.einsum('tef,efd->td', act, w2)

    y = lax.map(block, (xt.reshape(nblk, MOE_TOKEN_BLOCK, D), combine.reshape(nblk, MOE_TOKEN_BLOCK, MOE_N_EXPERTS)))
    return y.reshape(B, S, D)

def setup_inputs(seed: int = 0) -> dict:
    key = jax.random.key(seed)
    keys = iter(jax.random.split(key, 64))
    L, H, D = DEPTH, N_HEADS_GROUP, D_MODEL

    def normal(shape, scale):
        return jax.random.normal(next(keys), shape, jnp.float32) * scale

    def gain(shape):
        return 1.0 + normal(shape, 0.02)

    dt = jnp.exp(jax.random.uniform(next(keys), (L, H), jnp.float32, math.log(1e-3), math.log(1e-1)))
    return {
        'x': normal((BATCH, SEQ, D), 1.0),
        'mem': normal((BATCH, MEM_TOKENS, D), 1.0),
        'ln_mix': gain((L, D)),
        'w_in': normal((L, D, IN_COLS), D ** -0.5),
        'w_out': normal((L, MIX_WIDTH, D), MIX_WIDTH ** -0.5),
        'nsa_qk_gain': gain((L, 4, HEAD_DIM)),
        'nsa_cmp_pe': normal((L, 2, NSA_CMP_LEN, HEAD_DIM), 0.02),
        'nsa_cmp_w1': normal((L, 2, NSA_CMP_LEN * HEAD_DIM, NSA_CMP_HIDDEN), (NSA_CMP_LEN * HEAD_DIM) ** -0.5),
        'nsa_cmp_w2': normal((L, 2, NSA_CMP_HIDDEN, HEAD_DIM), NSA_CMP_HIDDEN ** -0.5),
        'gdn_conv': normal((L, GDN_CONV, 3 * GROUP_WIDTH), GDN_CONV ** -0.5),
        'gdn_a_log': jnp.log(jax.random.uniform(next(keys), (L, H), jnp.float32, 1.0, 16.0)),
        'gdn_dt_bias': dt + jnp.log(-jnp.expm1(-dt)),
        'gdn_norm': gain((L, HEAD_DIM)),
        'mlstm_i_bias': normal((L, H), 0.1),
        'mlstm_f_bias': jnp.linspace(3.0, 6.0, H, dtype=jnp.float32)[None, :] + normal((L, H), 0.1),
        'mlstm_norm': gain((L, HEAD_DIM)),
        'diff_qk_gain': gain((L, 2, DIFF_SUB_DIM)),
        'diff_lambda': normal((L, 4, DIFF_SUB_DIM), 0.1),
        'diff_norm': gain((L, HEAD_DIM)),
        'ln_xattn': gain((L, D)),
        'ln_mem': gain((L, D)),
        'xattn_wq': normal((L, D, MEM_HEADS * MEM_HEAD_DIM), D ** -0.5),
        'xattn_wkv': normal((L, D, 2 * MEM_HEADS * MEM_HEAD_DIM), D ** -0.5),
        'xattn_qk_gain': gain((L, 2, MEM_HEAD_DIM)),
        'xattn_wo': normal((L, MEM_HEADS * MEM_HEAD_DIM, D), (MEM_HEADS * MEM_HEAD_DIM) ** -0.5),
        'ln_moe': gain((L, D)),
        'moe_w_group': normal((L, D, MOE_GROUPS), D ** -0.5),
        'moe_b_group': normal((L, MOE_GROUPS), 0.01),
        'moe_w_expert': normal((L, D, MOE_N_EXPERTS), D ** -0.5),
        'moe_b_expert': normal((L, MOE_N_EXPERTS), 0.01),
        'moe_w1': normal((L, MOE_N_EXPERTS, D, MOE_FF), D ** -0.5),
        'moe_w3': normal((L, MOE_N_EXPERTS, D, MOE_FF), D ** -0.5),
        'moe_w2': normal((L, MOE_N_EXPERTS, MOE_FF, D), MOE_FF ** -0.5),
    }

def reference(x, mem, ln_mix, w_in, w_out, nsa_qk_gain, nsa_cmp_pe, nsa_cmp_w1, nsa_cmp_w2,
              gdn_conv, gdn_a_log, gdn_dt_bias, gdn_norm, mlstm_i_bias, mlstm_f_bias, mlstm_norm,
              diff_qk_gain, diff_lambda, diff_norm, ln_xattn, ln_mem, xattn_wq, xattn_wkv,
              xattn_qk_gain, xattn_wo, ln_moe, moe_w_group, moe_b_group, moe_w_expert,
              moe_b_expert, moe_w1, moe_w3, moe_w2):
    S = x.shape[1]
    pos = jnp.arange(S)
    cos_a, sin_a = rope_tables(pos, HEAD_DIM)
    cos_d, sin_d = rope_tables(pos, DIFF_SUB_DIM)
    split_at = np.cumsum(IN_WIDTHS)[:-1].tolist()
    h = x
    for l in range(DEPTH):
        hn = rms_norm(h, ln_mix[l])
        parts = jnp.split(hn @ w_in[l], split_at, axis=-1)
        y_a = nsa_mixer(*parts[0:8], nsa_qk_gain[l], nsa_cmp_pe[l], nsa_cmp_w1[l], nsa_cmp_w2[l], cos_a, sin_a)
        y_b = gdn_mixer(*parts[8:14], gdn_conv[l], gdn_a_log[l], gdn_dt_bias[l], gdn_norm[l])
        y_c = mlstm_mixer(*parts[14:20], mlstm_i_bias[l], mlstm_f_bias[l], mlstm_norm[l])
        lambda_init = 0.8 - 0.6 * math.exp(-0.3 * l)
        y_d = diff_mixer(*parts[20:23], diff_qk_gain[l], diff_lambda[l], diff_norm[l], lambda_init, cos_d, sin_d)
        h = h + jnp.concatenate([y_a, y_b, y_c, y_d], axis=-1) @ w_out[l]
        h = h + memory_cross_attention(rms_norm(h, ln_xattn[l]), rms_norm(mem, ln_mem[l]),
                                       xattn_wq[l], xattn_wkv[l], xattn_qk_gain[l], xattn_wo[l])
        h = h + hierarchical_moe(rms_norm(h, ln_moe[l]), moe_w_group[l], moe_b_group[l], moe_w_expert[l],
                                 moe_b_expert[l], moe_w1[l], moe_w3[l], moe_w2[l])
    return h


_drawn_inputs = setup_inputs


def setup_inputs(seed=0):
    import zlib

    import numpy as np

    out = dict(_drawn_inputs(seed))
    spreads = {}
    factors = {'nsa_qk_gain': 4.17,
     'nsa_cmp_pe': 3.999,
     'mlstm_i_bias': 28.888,
     'ln_xattn': 4.221,
     'ln_mem': 2.828,
     'xattn_qk_gain': 3.795,
     'moe_b_group': 9.881,
     'moe_b_expert': 3.514,
     'diff_lambda': 2.684}
    for name, (base, spread) in spreads.items():
        noise = np.random.default_rng([zlib.crc32(name.encode()), seed]).standard_normal(out[name].shape)
        drawn = base * np.exp(spread * noise) if base else spread * noise
        out[name] = jnp.asarray(drawn.astype(out[name].dtype))
    for name, factor in factors.items():
        out[name] = (out[name] * factor).astype(out[name].dtype)
    return out
```

```python
from contextlib import ExitStack

import numpy as np

import concourse.bass as bass
from concourse import mybir

F32 = mybir.dt.float32
BF16 = mybir.dt.bfloat16
U32 = mybir.dt.uint32
I32 = mybir.dt.int32
ALU = mybir.AluOpType
ACT = mybir.ActivationFunctionType
AXX = mybir.AxisListType.X

P = 128
L = 2
S = 512
NT = S // P
D = 1024
KD = D // P
H = 4
DH = 64
GW = H * DH
MEM = 256
NMT = MEM // P
NCMP = (S - 32) // 16 + 1
EPS = 1e-6
E_GROUPS, E_PER = 4, 8
NE = E_GROUPS * E_PER
FF = D // 4
NEG = -1e30
LEVELS = 7
SLOT = 2048
R = 6
CAP = 64
ROUNDS = S // CAP
NPAIR = NE // 2
QE = 4
NSMALL = 156

C_Q, C_KCVC, C_KSVS, C_KW, C_GQ = 0, 256, 384, 512, 652
C_AB, C_Z, C_MQ, C_MV, C_IF, C_MO, C_DQ, C_DK, C_DV = 1420, 1428, 1684, 1940, 2196, 2204, 2460, 2716, 2972

ROW = {}
_at = 0
for _n, _w in (("nsa_gain", 384), ("cmp_gain", 64), ("diff_gain", 512), ("xq_gain", 256), ("xk_gain", 256), ("gdn_norm", 64),
               ("mlstm_norm", 64), ("diff_norm", 64), ("i_bias", 4), ("f_bias", 4), ("a_log", 4),
               ("dt_bias", 4), ("lam", 128), ("b_group", 4), ("b_expert", 32), ("lam_init", 2)):
    ROW[_n] = (_at, _at + _w)
    _at += _w
NROW = _at
NCOL = 4 * KD + 24

CONST_F = {}
_at = 0
for _n, _w in (("ident", 128), ("triu", 128), ("ones", 128), ("sel4", 512), ("cosA", 128), ("sinA", 128),
               ("cosD", 64), ("sinD", 64), ("cosC", 32), ("sinC", 32), ("valid", 1), ("eps", 1), ("striu", 128), ("place", 32), ("c64", 7)):
    CONST_F[_n] = (_at, _at + _w)
    _at += _w
NCF = _at
CONST_B = {}
_at = 0
for _n, _w in (("identb", 128), ("mask", 128), ("maskT", 128), ("maskC", 4 * 32), ("lvl", LEVELS * 128)):
    CONST_B[_n] = (_at, _at + _w)
    _at += _w
NCB = _at


def const_tables():
    f = np.zeros((P, NCF), np.float32)
    b = np.zeros((P, NCB), np.float32)
    p = np.arange(P)

    def put(a, table, name, v):
        lo, hi = table[name]
        a[:v.shape[0], lo:lo + v.shape[1]] = v
    put(f, CONST_F, "ident", np.eye(P, dtype=np.float32))
    put(f, CONST_F, "triu", (p[:, None] <= p[None, :]).astype(np.float32))
    put(f, CONST_F, "ones", np.ones((P, P), np.float32))
    put(f, CONST_F, "sel4", np.repeat(np.eye(4, dtype=np.float32), P, axis=1))

    def rope(pos, dim):
        inv = (1.0 / (np.float32(10000.0) ** (np.arange(0, dim, 2, dtype=np.float32) / np.float32(dim)))).astype(np.float32)
        ang = pos.astype(np.float32)[:, None] * inv[None, :]
        return np.cos(ang).astype(np.float32), np.sin(ang).astype(np.float32)
    for d, c, s in ((DH, "cosA", "sinA"), (DH // 2, "cosD", "sinD")):
        cos, sin = rope(np.arange(S), d)
        put(f, CONST_F, c, cos.reshape(NT, P, -1).transpose(1, 0, 2).reshape(P, -1))
        put(f, CONST_F, s, sin.reshape(NT, P, -1).transpose(1, 0, 2).reshape(P, -1))
    end = 16 * np.arange(NCMP) + 31
    cos, sin = rope(end, DH)
    put(f, CONST_F, "cosC", cos)
    put(f, CONST_F, "sinC", sin)
    put(f, CONST_F, "valid", (p[:, None] >= 31).astype(np.float32))
    put(f, CONST_F, "eps", np.full((P, 1), EPS, np.float32))
    put(f, CONST_F, "striu", (p[:, None] < p[None, :]).astype(np.float32))
    ex = np.arange(NE)
    put(f, CONST_F, "place", np.tile((ex % 2) * CAP * NPAIR + ex // 2, (P, 1)).astype(np.float32))
    put(f, CONST_F, "c64", np.tile(CAP * np.arange(1, ROUNDS), (P, 1)).astype(np.float32))
    put(b, CONST_B, "identb", np.eye(P))
    put(b, CONST_B, "mask", np.where(p[None, :] > p[:, None], NEG, 0.0))
    put(b, CONST_B, "maskT", np.where(p[None, :] < p[:, None], NEG, 0.0))
    tok = np.arange(S).reshape(NT, P)
    mc = np.zeros((P, 4, 32))
    mc[:, :, :NCMP] = np.where(end[None, None, :] <= tok.T[:, :, None], 0.0, NEG)
    put(b, CONST_B, "maskC", mc.reshape(P, -1))
    lv = np.zeros((P, LEVELS, P))
    for n in range(LEVELS):
        w = 1 << n
        j, i = p[:, None], p[None, :]
        lv[:, n] = (j // (2 * w) == i // (2 * w)) & (j // w % 2 == 0) & (i // w % 2 == 1)
    put(b, CONST_B, "lvl", lv.reshape(P, -1))
    return f, b


def job_list():
    jobs = []

    def add(name, banks, eng):
        jobs.append((name, banks, eng))
    for k in range(KD):
        add(("hT", "mix", k), 1, "AD"[k % 2])
    for c in range(6):
        add(("gp", c), 1, "AD"[c % 2])
    for tp in range(2):
        add(("small", tp), 1, "D")
    for tp in range(2):
        add(("z", tp), 1, "A")
    for w in range(3):
        for tp in range(2):
            add(("gn", w, tp), 1, "AD"[tp])
    add(("gc",), 1, "A")
    for w in range(4):
        for hp in range(2):
            add(("gT", w, hp), 1, "AD"[hp])
    for h in range(H):
        add(("gD", h), 1, "A")
        add(("gA", h), 1, "D")
        add(("gQ", h), 1, "D")
    for h in range(H):
        add(("T0", h), 1, "A")
    for n in range(1, LEVELS):
        for h in range(H):
            add(("X", n, h), 1, "A")
        for h in range(H):
            if n < LEVELS - 1:
                add(("T", n, h), 1, "D")
            add(("U", n, h), 1, "D")
    for hp in range(2):
        add(("wT", hp), 1, "A")
    for t in range(NT):
        add(("vn", t), 1, "A")
        add(("go", t), 1, "A")
        add(("gS", t), 1, "D")
    for tp in range(2):
        add(("nq", tp), 1, "AD"[tp])
    add(("kcvc",), 1, "D")
    for tp in range(2):
        add(("ksvs", tp), 1, "D")
    for j in range(2):
        add(("hid", j), 1, "D")
    for j in range(2):
        add(("cmp", j), 1, "D")
    add(("kcT",), 1, "D")
    for pr in range(4):
        add(("nT", pr), 1, "AD"[pr % 2])
    for w in range(3):
        for tp in range(2):
            add(("dp", w, tp), 1, "AD"[tp])
    for pr in range(4):
        add(("dT", pr), 1, "AD"[pr % 2])
    items = attention_items()
    for n, it in enumerate(items):
        attention_jobs(add, n, it)
    for w in range(2):
        add(("mqk", w), 1, "AD"[w])
    for tp in range(2):
        add(("mv", tp), 1, "D")
    for tp in range(2):
        add(("mo", tp), 1, "A")
    add(("mF",), 1, "D")
    add(("aT",), 1, "D")
    add(("MT",), 1, "A")
    for h in range(H):
        add(("mB", h), 1, "A")
        add(("mD", h), 1, "A")
        for j in range(NT):
            add(("mS", h, j), 1, "D")
        add(("mO", h), 1, "D")
    for k in range(KD):
        add(("yT", k), 1, "AD"[k % 2])
    for u in range(4):
        for tp in range(2):
            add(("wo", u, tp), 1, "D")
    for k in range(KD):
        add(("memT", k), 1, "AD"[k % 2])
    add(("xk",), 1, "D")
    add(("xv",), 1, "A")
    for k in range(KD):
        add(("hT", "xa", k), 1, "AD"[k % 2])
    for tp in range(2):
        add(("xq", tp), 1, "AD"[tp])
    for hp in range(2):
        add(("xqT", hp), 1, "A")
        add(("xkT", hp), 1, "D")
    for n, it in enumerate(cross_items()):
        attention_jobs(add, 100 + n, it)
    for hp in range(2):
        add(("xoT", hp), 1, "AD"[hp])
    for t in range(NT):
        for c in range(2):
            add(("xo", t, c), 1, "D")
    for k in range(KD):
        add(("hT", "moe", k), 1, "AD"[k % 2])
    for t in range(NT):
        add(("route", t), 1, "D")
    add(("rank",), 1, "D")
    return jobs


def attention_items():
    items = []
    for br in ("cmp", "sel", "win"):
        for t in range(NT):
            for pr in range(2):
                items.append((br, pr, t, NCMP if br == "cmp" else (t + 1) * P))
    for t in range(NT):
        for h in range(H):
            items.append(("diff", h, t, (t + 1) * P))
    return items


def cross_items():
    return [("cross", pr, t, MEM) for t in range(NT) for pr in range(2)]


def attention_jobs(add, n, item):
    add(("S", n), 2, "A")
    add(("PT", n), 2, "AD"[n % 2])
    add(("O", n), 1, "D")


class Jobs:

    def __init__(self, full, free):
        self.full, self.free = full, free
        self.info = {}
        owner = [None] * 8
        at = 0
        count = {"A": 0, "D": 0}
        for n, (name, banks, eng) in enumerate(job_list()):
            if banks == 2 and at % 2:
                at = (at + 1) % 8
            before = {owner[at + j] for j in range(banks)} - {None}
            count[eng] += 1
            assert name not in self.info, name
            self.info[name] = (n + 1, at, banks, eng, count[eng], before)
            for j in range(banks):
                owner[at + j] = name
            at = (at + banks) % 8

    def number(self, name):
        return self.info[name][0]

    def freed(self, name):
        _, _, _, eng, c, _ = self.info[name]
        return self.free[eng], c


def build(nc, t_in, out, dbg=None):
    ctx = ExitStack()
    with ctx:
        def sb(name, shape, dt=F32):
            return ctx.enter_context(nc.sbuf_tensor(name, shape, dt))

        sems = {}

        def sem(name):
            if name not in sems:
                sems[name] = ctx.enter_context(nc.semaphore(name))
            return sems[name]

        psum = ctx.enter_context(nc.psum_tensor("psum", [P, 8, 512], F32))
        h_res = sb("h_res", [P, NT, D])
        hnT = sb("hnT", [P, KD, S])
        y = sb("y", [P, NT, D])
        ring = sb("ring", [P, R, SLOT])
        cf = sb("cf", [P, NCF])
        cb = sb("cb", [P, NCB], BF16)
        row = sb("row", [P, NROW])
        col = sb("col", [P, NCOL])
        cw2 = sb("cw2", [P, 2, DH])
        pe_c = sb("pe_c", [P, 32])
        wr = sb("wr", [P, KD, 36])
        small = sb("small", [P, NT, NSMALL])
        st = sb("st", [P, 2100])
        rounds = sb("rounds", [P, 1], I32)
        pos = sb("pos", [P, 2 * NT], U32)
        tok = sb("tok", [P, 2 * NT, 2], U32)
        unused = sb("unused", [P, NPAIR, 2], U32)
        AW = 20000
        arena = sb("arena", [P, AW])

        def cst(name):
            lo, hi = CONST_F[name]
            return cf[:, lo:hi]

        def cbt(name):
            lo, hi = CONST_B[name]
            return cb[:, lo:hi]

        def rowp(name):
            lo, hi = ROW[name]
            return row[:, lo:hi]

        def col_ln(n):
            return {"mix": 0, "xa": 1, "moe": 2, "mem": 3}[n] * KD

        stat_at = {}
        used = [0]

        def stat(name, n):
            if name not in stat_at:
                stat_at[name] = (used[0], n)
                used[0] += n
                assert used[0] <= 2100, used[0]
            lo, k = stat_at[name]
            assert k == n
            return st[:, lo:lo + n]

        def view(off, *dims):
            n = int(np.prod(dims))
            assert off + n <= AW, (off, n)
            v = arena[:, off:off + n]
            if len(dims) == 1:
                return v
            names = "abcd"[:len(dims)]
            return v.rearrange(f"p ({' '.join(names)}) -> p {' '.join(names)}", **dict(zip(names, dims)))

        raw = view(0, 6, 515)
        conv = view(3090, 6, 512)
        gT_, gU, gX = view(0, H, NT, P), view(2048, H, NT, P), view(4096, H, NT, P)
        G0 = 6162
        gnat = view(G0, 4, NT, H, DH)
        gtr = view(G0 + 4096, 4, 2, S)
        AT = view(G0 + 8192, H, NT, P)
        atT = view(G0 + 10240, H, NT, P)
        vnew = view(G0 + 12288, 2, H, DH)
        state = view(G0 + 12800, H, DH)
        assert G0 + 13056 <= AW
        ycol = lambda a: y[:, :, a * GW:(a + 1) * GW]
        zgate = ycol(2)
        dec = ycol(0)
        Bm = ycol(3)
        dec_v = dec.rearrange("p t (b i) -> p b t i", b=2)
        Bm_v = Bm.rearrange("p t (b i) -> p b t i", b=2)
        nX = view(0, NT, 6, DH)
        nY = view(1536, NT, 8, DH)
        nV = view(3584, NT, 2, DH)
        nTr = view(4096, 4, S)
        kcvcT = view(6144, S)
        blk = view(6656, 32, NCMP)
        ckn = view(7648, 2, DH)
        cvn = view(7776, DH)
        kcT = view(7840, 32)
        hidb = view(7872, 2, 32)
        hidt = view(7936, 2, 32)
        ckr = view(8000, 2, DH)
        Pm = view(8128, 2, 2, 512)
        PTm = view(10176, 2, 2, 512)
        dX = view(12224, NT, 512)
        dY = view(14272, NT, 512)
        dV = view(16320, NT, GW)
        dTr = view(17344, 4, S)
        assert 17344 + 2048 <= AW
        tmpA, tmpB = view(14272, 1024), view(15296, 1024)
        mqT, mkT = view(0, S), view(512, S)
        mV = view(1024, NT, H, 65)
        mO = view(2064, NT, GW)
        Em = view(3088, 2, NT, S)
        aT = view(7184, S)
        nMT = view(7696, S)
        memn = view(0, NMT, D)
        memT = view(2048, KD, MEM)
        xK = view(4096, NMT, GW)
        xV = view(4608, NMT, GW)
        xQ = view(5120, NT, GW)
        xqT = view(6144, 2, S)
        xkT = view(7168, 2, MEM)
        xtmp = view(12224, 2048)
        xoT = view(14272, 2, S)
        xO = y[:, :, 0:GW]
        ring2 = view(0, 6, SLOT)
        X2 = view(12288, 2, D)
        X2T = view(14336, 2, KD, P)
        sgl = view(16384, 2, 2, CAP)
        aTm = view(16640, 2, 2, CAP)
        Ye = view(16896, D)
        gmoe = view(17920, D)
        ids = view(18944, NPAIR, 2).bitcast(U32)
        Yg = view(0, NT, 2, D)
        idx = sb("idx", [P, 3], U32)
        table = nc.dram_tensor("table", (ROUNDS * P * NPAIR, 2), U32, kind="Internal").ap()
        hn_rows = nc.dram_tensor("hn_rows", (S, D), F32, kind="Internal").ap()
        y_rows = nc.dram_tensor("y_rows", (2 * S + P, D), F32, kind="Internal").ap()

        def expert_slot(q, n):
            return ring[:, 3 * q + n, :] if q < 2 else ring2[:, 3 * (q - 2) + n, :]

        J = Jobs(sem("psum_full"), {"A": sem("psum_free_act"), "D": sem("psum_free_dve")})
        ATT = [(n, it) for n, it in enumerate(attention_items())]
        XATT = [(100 + n, it) for n, it in enumerate(cross_items())]
        block = ctx.enter_context(nc.Block())

        psum_full = J.full

        def bank(name):
            _, at, banks, _, _, _ = J.info[name]
            return psum[:, at, :] if banks == 1 else psum[:, at:at + 2, :]

        class Waits:

            def __init__(self, e):
                self.e, self.seen = e, {}

            def new_layer(self):
                self.seen = {}

            def wait_ge(self, s, v):
                if self.seen.get(s.name, 0) < v:
                    self.e.wait_ge(s, v)
                    self.seen[s.name] = v

        class Steps:

            def __init__(self, s):
                self.sem, self.count = s, 0

            def __call__(self, ins):
                ins.then_inc(self.sem, 1)
                self.count += 1
                return self.count

        def phase(e, need, n):
            e.drain().then_inc(sem(f"phase{n}"), 1)
            need.wait_ge(sem(f"phase{n}"), 4)

        def layer_end(e, name):
            e.drain().then_inc(sem("layer_done"), 1)
            e.wait_ge(sem("layer_go_" + name), 1)
            e.sem_clear(sem("layer_go_" + name))

        units = ["gq", "gk", "gv", "small", "z", "nq", "kv", "cw1a", "cw1b", "dq", "dk", "dv",
                 "mqk", "mv", "mo", "wo0", "wo1", "wo2", "wo3", "xkw", "xvw", "xqw", "xow", "pad"]
        upos = {u: n for n, u in enumerate(units)}
        assert len(units) % R == 0
        last_job = {"gq": ("gp", 1), "gk": ("gp", 3), "gv": ("gp", 5), "small": ("small", 1), "z": ("z", 1),
                    "nq": ("nq", 1), "kv": ("ksvs", 1), "cw1a": ("hid", 1), "cw1b": ("hid", 1),
                    "dq": ("dp", 0, 1), "dk": ("dp", 1, 1), "dv": ("dp", 2, 1), "mqk": ("mqk", 1),
                    "mv": ("mv", 1), "mo": ("mo", 1), "wo0": ("wo", 0, 1), "wo1": ("wo", 1, 1),
                    "wo2": ("wo", 2, 1), "wo3": ("wo", 3, 1), "xkw": ("xk",), "xvw": ("xv",),
                    "xqw": ("xq", 1), "xow": ("xo", 3, 1)}
        ndma = {u: 1 for u in units}
        ndma.update(kv=1, small=3, cw1a=2, cw1b=2, pad=0)
        landed = {}
        tot = [0] * R
        for n, u in enumerate(units):
            tot[n % R] += 16 * ndma[u]
            landed[u] = tot[n % R]
        slot_base = list(tot)

        def slot(u):
            return ring[:, upos[u] % R, :]

        def weights_in(u):
            return sem(f"weights{upos[u] % R}"), landed[u]

        def operands(it):
            br, pr, t, kl = it
            q = slice(t * P, (t + 1) * P)
            nk = -(-kl // P)
            lo, hi = slice(0, DH), slice(DH, P)
            if br == "cmp":
                return [nTr[s, pr, q] for s in (lo, hi)], [kcT[s, 0:NCMP] for s in (lo, hi)], [[cvn[0:NCMP, :]]] * 2, None
            if br in ("sel", "win"):
                w = ("sel", "win").index(br)
                return ([nTr[s, pr, q] for s in (lo, hi)], [nTr[s, 2 + w, 0:kl] for s in (lo, hi)],
                        [[nV[:, k, w, :] for k in range(nk)]] * 2, None)
            if br == "diff":
                ss = [slice(32 * (2 * (pr % 2) + m), 32 * (2 * (pr % 2) + m) + 32) for m in range(2)]
                return ([dTr[s, pr // 2, q] for s in ss], [dTr[s, 2 + pr // 2, 0:kl] for s in ss],
                        [[dV[:, k, pr * DH:(pr + 1) * DH] for k in range(nk)]] * 2, None)
            return ([xqT[s, pr, q] for s in (lo, hi)], [xkT[s, pr, :] for s in (lo, hi)],
                    [[xV[:, k, (2 * pr + m) * DH:(2 * pr + m + 1) * DH] for k in range(nk)] for m in range(2)], None)

        def item_count(n):
            return n + 1 if n < 100 else len(ATT) + n - 100 + 1

        def prev_item(n):
            seq = [k for k, _ in ATT] + [k for k, _ in XATT]
            return seq[seq.index(n) - 2]

        @block.sync
        def _(e):
            e.dma_start(cf[:], t_in["const_f"]).then_inc(sem("const_in"), 16)
            e.dma_start(cb[:], t_in["const_b"]).then_inc(sem("const_in"), 16)
            e.dma_start(h_res[:], t_in["x"].rearrange("b (t p) d -> p (b t) d", p=P)).then_inc(sem("const_in"), 16)
            need = Waits(e)
            with e.Fori(0, L) as l:
                need.new_layer()

                def lay(name, pat, **kw):
                    return t_in[name][bass.ds(l, 1)].rearrange(pat, **kw)
                e.dma_start(row[:], lay("rows", "a p n -> p (a n)")).then_inc(sem("params_in"), 16)
                e.dma_start(col[:], lay("cols", "a p n -> p (a n)")).then_inc(sem("params_in"), 16)
                e.dma_start(cw2[:], lay("nsa_cmp_w2", "a j p n -> p (a j) n")).then_inc(sem("params_in"), 16)
                e.dma_start(pe_c[:], lay("pe_t", "a p n -> p (a n)")).then_inc(sem("params_in"), 16)
                e.dma_start(wr[:], lay("w_route", "a (p k) n -> p (a k) n", p=P)).then_inc(sem("params_in"), 16)
                win = lay("w_in", "a (p k) n -> p (a k) n", p=P)
                wout = lay("w_out", "a (k p) n -> p (a k) n", p=P)
                for n, u in enumerate(units):
                    if u == "pad":
                        continue
                    if n >= R:
                        need.wait_ge(psum_full, J.number(last_job[units[n - R]]))
                    s = sem(f"weights{n % R}")
                    sl = slot(u)
                    s8 = sl.rearrange("p (k n) -> p k n", k=KD)

                    def cols(c0, dst=s8):
                        e.dma_start(dst, win[:, :, c0:c0 + 256]).then_inc(s, 16)
                    if u in ("gq", "gk", "gv"):
                        cols(C_GQ + 256 * ("gq", "gk", "gv").index(u))
                    elif u == "small":
                        sm = sl[:, 0:KD * NSMALL].rearrange("p (k n) -> p k n", k=KD)
                        e.dma_start(sm[:, :, 0:140], win[:, :, C_KW:C_KW + 140]).then_inc(s, 16)
                        e.dma_start(sm[:, :, 140:148], win[:, :, C_AB:C_AB + 8]).then_inc(s, 16)
                        e.dma_start(sm[:, :, 148:156], win[:, :, C_IF:C_IF + 8]).then_inc(s, 16)
                    elif u in ("cw1a", "cw1b"):
                        half = ("cw1a", "cw1b").index(u)
                        for j in range(2):
                            src = t_in["nsa_cmp_w1"][bass.ds(l, 1), j].rearrange("a (l d) m -> d (a l) m", d=DH)
                            e.dma_start(sl[j * DH:(j + 1) * DH, :].rearrange("p (l m) -> p l m", m=P),
                                        src[:, 16 * half:16 * half + 16, :]).then_inc(s, 16)
                    elif u.startswith("wo"):
                        e.dma_start(s8, wout[:, :, int(u[2]) * 256:int(u[2]) * 256 + 256]).then_inc(s, 16)
                    elif u in ("xkw", "xvw"):
                        w = lay("xattn_wkv", "a (p k) n -> p (a k) n", p=P)
                        c0 = 0 if u == "xkw" else 256
                        e.dma_start(s8, w[:, :, c0:c0 + 256]).then_inc(s, 16)
                    elif u == "xqw":
                        e.dma_start(s8, lay("xattn_wq", "a (p k) n -> p (a k) n", p=P)).then_inc(s, 16)
                    elif u == "xow":
                        e.dma_start(sl.rearrange("p (k n) -> p k n", k=2),
                                    lay("xattn_wo", "a (k p) n -> p (a k) n", p=P)).then_inc(s, 16)
                    else:
                        cols({"z": C_Z, "nq": C_Q, "kv": C_KCVC, "mqk": C_MQ, "mv": C_MV, "mo": C_MO,
                              "dq": C_DQ, "dk": C_DK, "dv": C_DV}[u])
                need.wait_ge(sem("phase3"), 4)
                e.dma_start(memn[:], t_in["mem"].rearrange("b (t p) d -> p (b t) d", p=P)).then_inc(sem("mem_in"), 16)
                e.dma_start(gmoe, lay("ln_moe_rows", "a p n -> p (a n)")).then_inc(sem("gmoe_in"), 16)
                w1, w3, w2 = (t_in[n][bass.ds(l, 1)] for n in ("moe_w1", "moe_w3", "moe_w2"))

                def load_expert(ex, q):
                    for n, wt in enumerate((w1, w3)):
                        e.dma_start(expert_slot(q, n).rearrange("p (k f) -> p k f", k=KD),
                                    wt[:, ex].rearrange("a b (p k) f -> p (a b k) f", p=P))\
                         .then_inc(sem(f"expert_in{q}"), 16)
                    e.dma_start(expert_slot(q, 2).rearrange("p (k n) -> p k n", k=2),
                                w2[:, ex].rearrange("a b (k p) n -> p (a b k) n", p=P))\
                     .then_inc(sem(f"expert_in{q}"), 16)

                for q in range(QE):
                    e.wait_ge(sem("place_free"), q + 1)
                    load_expert(bass.ds(q, 1), q)
                    if q == 1:
                        for t in range(NT):
                            e.wait_ge(sem("hn_moe"), t + 1)
                            e.dma_start(hn_rows[t * P:(t + 1) * P, :], y[:, t, :]).then_inc(sem("hn_rows_out"), 16)
                with e.Fori(0, NE // QE - 1) as i:
                    for q in range(QE):
                        e.wait_ge(sem("moe_down"), QE * i + q + 1)
                        load_expert(bass.ds(QE * i + QE + q, 1), q)
                e.wait_ge(sem("routed"), 1)
                nr = e.value_load(rounds[0:1, 0:1], min_val=1, max_val=ROUNDS)
                with e.If(nr > 1):
                    with e.Fori(1, nr) as r:
                        with e.Fori(0, NE // QE) as i:
                            for q in range(QE):
                                e.wait_ge(sem("moe_down"), NE * r + QE * i + q + 1 - QE)
                                load_expert(bass.ds(QE * i + q, 1), q)
                layer_end(e, "sp")
            e.dma_start(out.rearrange("b (t p) d -> p (b t) d", p=P), h_res[:]).then_inc(sem("out_done"), 16)
            if dbg is not None:
                e.dma_start(dbg["y"], y[:]).then_inc(sem("out_done"), 16)
            e.wait_ge(sem("out_done"), 16 if dbg is None else 32)

        @block.tensor
        def _(e):
            need = Waits(e)

            def begin(name):
                _, at, banks, _, _, before = J.info[name]
                for b in sorted(before, key=str):
                    need.wait_ge(*J.freed(b))
                return psum[:, at, :] if banks == 1 else psum[:, at:at + 2, :]

            def tpose(out_, in_, n=P):
                return e.transpose(out_, in_, cst("ident")[0:n, 0:n])

            def transposed_norm(nm):
                for k in range(KD):
                    o = begin(("hT", nm, k))
                    for t in range(NT):
                        need.wait_ge(sem(f"hn_{nm}"), t + 1)
                        ins = tpose(o[:, t * P:(t + 1) * P], y[:, t, :].rearrange("p (c k) -> p k c", k=KD)[:, k, :])
                    ins.then_inc(psum_full, 1)

            def got_hnT(nm):
                for k in (KD - 2, KD - 1):
                    need.wait_ge(*J.freed(("hT", nm, k)))

            def proj_T(name, u, c0):
                need.wait_ge(*weights_in(u))
                o = begin(name)
                w = slot(u).rearrange("p (k n) -> p k n", k=KD)
                for k in range(KD):
                    ins = e.matmul(o, w[:, k, c0:c0 + P], hnT[:, k, :], start=(k == 0), stop=(k == KD - 1))
                ins.then_inc(psum_full, 1)

            def proj_N(name, u, tp, n, c0=0, lhs=None, nk=KD, width=None):
                need.wait_ge(*weights_in(u))
                o = begin(name)
                w = slot(u)[:, 0:nk * (width or n)].rearrange("p (k n) -> p k n", k=nk)
                src = hnT if lhs is None else lhs
                for q in range(2):
                    t = 2 * tp + q
                    for k in range(nk):
                        ins = e.matmul(o[:, q * n:(q + 1) * n], src[:, k, t * P:(t + 1) * P], w[:, k, c0:c0 + n],
                                       start=(k == 0), stop=(k == nk - 1))
                ins.then_inc(psum_full, 1)

            def attention(items):
                def scores(n, it):
                    br, pr, t, kl = it
                    qs, ks, vs, used = operands(it)
                    o = begin(("S", n))
                    for m in range(2):
                        e.matmul(o[:, m, 0:kl], qs[m], ks[m], start=True, stop=(br == "cross"),
                                 skip_group_check=True)
                        if br == "cmp":
                            ins = e.matmul(o[:, m, 0:kl], cbt("identb"), cbt("maskC")[:, t * 32:t * 32 + kl],
                                           start=False, stop=True, skip_group_check=True)
                        elif br != "cross":
                            ins = e.matmul(o[:, m, t * P:kl], cbt("identb"), cbt("mask"),
                                           start=False, stop=True, skip_group_check=True)
                        else:
                            ins = None
                    if ins is None:
                        return n, it
                    ins.then_inc(psum_full, 1)

                def scores_x(n, it):
                    br, pr, t, kl = it
                    qs, ks, vs, used = operands(it)
                    o = begin(("S", n))
                    for m in range(2):
                        ins = e.matmul(o[:, m, 0:kl], qs[m], ks[m], start=True, stop=True)
                    ins.then_inc(psum_full, 1)

                def weighted(n, it):
                    br, pr, t, kl = it
                    qs, ks, vs, used = operands(it)
                    nk = -(-kl // P)
                    need.wait_ge(*J.freed(("S", n)))
                    o = begin(("PT", n))
                    for m in range(2):
                        for k in range(nk):
                            w = min(P, kl - k * P)
                            ins = tpose(o[0:w, m, k * P:(k + 1) * P], Pm[:, n % 2, m, k * P:k * P + w])
                    ins.then_inc(psum_full, 1)

                def product(n, it):
                    br, pr, t, kl = it
                    qs, ks, vs, used = operands(it)
                    nk = -(-kl // P)
                    need.wait_ge(*J.freed(("PT", n)))
                    o = begin(("O", n))
                    for m in range(2):
                        for k in range(nk):
                            w = min(P, kl - k * P)
                            ins = e.matmul(o[:, m * DH:(m + 1) * DH], PTm[0:w, n % 2, m, k * P:(k + 1) * P],
                                           vs[m][k], start=(k == 0), stop=(k == nk - 1))
                    ins.then_inc(psum_full, 1)

                for n, it in items:
                    (scores_x if it[0] == "cross" else scores)(n, it)
                    weighted(n, it)
                    product(n, it)

            def gdn():
                for c in range(6):
                    proj_T(("gp", c), ("gq", "gk", "gv")[c // 2], (c % 2) * P)
                for tp in range(2):
                    proj_N(("small", tp), "small", tp, NSMALL)
                for tp in range(2):
                    proj_N(("z", tp), "z", tp, GW)
                for w in range(3):
                    need.wait_ge(sem("g_silu"), 2 * w + 2)
                    for tp in range(2):
                        o = begin(("gn", w, tp))
                        for q in range(2):
                            for c in range(2):
                                ins = tpose(o[:, q * GW + c * P:q * GW + (c + 1) * P],
                                            conv[:, 2 * w + c, (2 * tp + q) * P:(2 * tp + q + 1) * P])
                        ins.then_inc(psum_full, 1)
                need.wait_ge(sem("g_logdecay"), 1)
                o = begin(("gc",))
                g = stat("g", 16)
                e.matmul(o[:, 0:16], cst("triu"), g, start=True, stop=True)
                e.matmul(o[:, 16:32], cst("ones"), g, start=True, stop=True).then_inc(psum_full, 1)
                for w in range(4):
                    need.wait_ge(sem(("g_qk", "g_qk", "g_kbeta", "g_qd")[w]), 1)
                    src = (0, 1, 3, 0)[w]
                    for hp in range(2):
                        o = begin(("gT", w, hp))
                        for t in range(NT):
                            ins = tpose(o[:, t * P:(t + 1) * P],
                                        gnat[:, src, t, 2 * hp:2 * hp + 2, :].rearrange("p a b -> p (a b)"))
                        ins.then_inc(psum_full, 1)
                for hh in range(H):
                    pp = slice(DH * (hh % 2), DH * (hh % 2) + DH)
                    o = begin(("gD", hh))
                    for t in range(NT):
                        e.matmul(o[:, t * P:(t + 1) * P], g[:, t * H + hh:t * H + hh + 1].broadcast_to([P, P]),
                                 cst("triu"), start=True, stop=False, skip_group_check=True)
                        ins = e.matmul(o[:, t * P:(t + 1) * P], cbt("identb"), cbt("maskT"), start=False, stop=True,
                                       skip_group_check=True)
                    ins.then_inc(psum_full, 1)
                    if hh == 0:
                        for w in range(3):
                            for hp in range(2):
                                need.wait_ge(*J.freed(("gT", w, hp)))
                    for nm, r in (("gA", 2), ("gQ", 0)):
                        o = begin((nm, hh))
                        for t in range(NT):
                            c = slice(t * P, (t + 1) * P)
                            ins = e.matmul(o[:, c], gtr[pp, 1, hh // 2, c], gtr[pp, r, hh // 2, c],
                                           start=True, stop=True)
                        ins.then_inc(psum_full, 1)
                for hh in range(H):
                    need.wait_ge(sem("g_U0"), hh + 1)
                    o = begin(("T0", hh))
                    for t in range(NT):
                        ins = tpose(o[:, t * P:(t + 1) * P], gU[:, hh, t, :])
                    ins.then_inc(psum_full, 1)
                for n in range(1, LEVELS):
                    for hh in range(H):
                        need.wait_ge(sem("g_B"), (n - 1) * H + hh + 1)
                        need.wait_ge(*J.freed(("T0", hh) if n == 1 else ("T", n - 1, hh)))
                        o = begin(("X", n, hh))
                        for t in range(NT):
                            ins = e.matmul(o[:, t * P:(t + 1) * P], Bm_v[:, hh % 2, t, :], gT_[:, hh, t, :],
                                           start=True, stop=True)
                        ins.then_inc(psum_full, 1)
                    for hh in range(H):
                        need.wait_ge(*J.freed(("X", n, hh)))
                        if n > 1:
                            need.wait_ge(*J.freed(("U", n - 1, hh)))
                        if n < LEVELS - 1:
                            o = begin(("T", n, hh))
                            for t in range(NT):
                                ins = e.matmul(o[:, t * P:(t + 1) * P], gU[:, hh, t, :], gX[:, hh, t, :],
                                               start=True, stop=True)
                            ins.then_inc(psum_full, 1)
                        o = begin(("U", n, hh))
                        for t in range(NT):
                            ins = e.matmul(o[:, t * P:(t + 1) * P], gX[:, hh, t, :], gU[:, hh, t, :],
                                           start=True, stop=True)
                        ins.then_inc(psum_full, 1)
                need.wait_ge(sem("g_kbe"), 1)
                for hh in range(H):
                    need.wait_ge(*J.freed(("U", LEVELS - 1, hh)))
                for hp in range(2):
                    o = begin(("wT", hp))
                    for q in range(2):
                        for t in range(NT):
                            ins = e.matmul(o[q * DH:(q + 1) * DH, t * P:(t + 1) * P], gnat[:, 3, t, 2 * hp + q, :],
                                           gU[:, 2 * hp + q, t, :], start=True, stop=True)
                    ins.then_inc(psum_full, 1)
                need.wait_ge(sem("g_vbeta"), 1)
                need.wait_ge(sem("g_kend"), 1)
                for hp in range(2):
                    need.wait_ge(*J.freed(("wT", hp)))
                    need.wait_ge(*J.freed(("gT", 3, hp)))
                for t in range(NT):
                    c = slice(t * P, (t + 1) * P)
                    if t:
                        need.wait_ge(*J.freed(("gS", t - 1)))
                    o = begin(("vn", t))
                    for hh in range(H):
                        pp = slice(DH * (hh % 2), DH * (hh % 2) + DH)
                        oo = o[:, hh * DH:(hh + 1) * DH]
                        ins = e.matmul(oo, gU[:, hh, t, :], gnat[:, 2, t, hh, :], start=True, stop=(t == 0))
                        if t:
                            ins = e.matmul(oo, gtr[:, 2, hh // 2, c], state[:, hh, :], start=False, stop=True)
                    ins.then_inc(psum_full, 1)
                    need.wait_ge(*J.freed(("vn", t)))
                    o = begin(("go", t))
                    for hh in range(H):
                        pp = slice(DH * (hh % 2), DH * (hh % 2) + DH)
                        oo = o[:, hh * DH:(hh + 1) * DH]
                        ins = e.matmul(oo, atT[:, hh, t, :], vnew[:, t % 2, hh, :], start=True, stop=(t == 0))
                        if t:
                            ins = e.matmul(oo, gtr[:, 3, hh // 2, c], state[:, hh, :], start=False, stop=True)
                    ins.then_inc(psum_full, 1)
                    o = begin(("gS", t))
                    for hh in range(H):
                        q = hh % 2
                        ins = e.matmul(o[q * DH:(q + 1) * DH, (hh // 2) * DH:(hh // 2 + 1) * DH],
                                       gnat[:, 1, t, hh, :], vnew[:, t % 2, hh, :], start=True, stop=True)
                    ins.then_inc(psum_full, 1)

            def nsa_diff():
                for tp in range(2):
                    proj_N(("nq", tp), "nq", tp, GW)
                proj_T(("kcvc",), "kv", 0)
                for tp in range(2):
                    proj_N(("ksvs", tp), "kv", tp, P, c0=P, width=256)
                need.wait_ge(*weights_in("cw1a"))
                need.wait_ge(*weights_in("cw1b"))
                need.wait_ge(sem("blocks"), 2)
                for j in range(2):
                    pp = slice(j * DH, (j + 1) * DH)
                    o = begin(("hid", j))
                    for i in range(32):
                        w = slot("cw1a" if i < 16 else "cw1b").rearrange("p (l m) -> p l m", m=P)[pp, i % 16, :]
                        ins = e.matmul(o[:, 0:NCMP], w, blk[pp, i, :], start=(i == 0), stop=(i == 31))
                    ins.then_inc(psum_full, 1)
                for j in range(2):
                    need.wait_ge(sem("cmp_hidden"), j + 1)
                    o = begin(("cmp", j))
                    e.matmul(o[0:NCMP, 0:DH], hidb[:, j, 0:NCMP], cw2[:, j, :], start=True, stop=True).then_inc(psum_full, 1)
                need.wait_ge(sem("cmp_k"), 1)
                o = begin(("kcT",))
                tpose(o[:, 0:NCMP], ckr[0:NCMP, :, :].rearrange("p a b -> p (a b)"), NCMP).then_inc(psum_full, 1)
                need.wait_ge(sem("nsa_rope"), 1)
                for pr in range(4):
                    o = begin(("nT", pr))
                    for t in range(NT):
                        ins = tpose(o[:, t * P:(t + 1) * P], nY[:, t, 2 * pr:2 * pr + 2, :].rearrange("p a b -> p (a b)"))
                    ins.then_inc(psum_full, 1)
                for w in range(3):
                    for tp in range(2):
                        proj_N(("dp", w, tp), ("dq", "dk", "dv")[w], tp, GW)
                need.wait_ge(sem("diff_rope"), 1)
                for pr in range(4):
                    o = begin(("dT", pr))
                    for t in range(NT):
                        ins = tpose(o[:, t * P:(t + 1) * P], dY[:, t, pr * P:(pr + 1) * P])
                    ins.then_inc(psum_full, 1)
                need.wait_ge(*J.freed(("kcT",)))
                need.wait_ge(*J.freed(("cmp", 1)))
                for pr in range(4):
                    need.wait_ge(*J.freed(("nT", pr)))
                    need.wait_ge(*J.freed(("dT", pr)))
                for w in range(3):
                    for tp in range(2):
                        need.wait_ge(*J.freed(("dp", w, tp)))
                attention(ATT)

            def mlstm():
                for w in range(2):
                    proj_T(("mqk", w), "mqk", w * P)
                for tp in range(2):
                    proj_N(("mv", tp), "mv", tp, GW)
                for tp in range(2):
                    proj_N(("mo", tp), "mo", tp, GW)
                need.wait_ge(sem("m_logf"), 1)
                lf = stat("lf", 16).rearrange("p (t h) -> p t h", h=H)
                o = begin(("mF",))
                for t in range(NT):
                    for s in range(t + 1):
                        ins = e.matmul(o[:, t * H:(t + 1) * H], cst("triu" if s == t else "ones"), lf[:, s, :],
                                       start=(s == 0), stop=(s == t))
                ins.then_inc(psum_full, 1)
                need.wait_ge(sem("m_a"), 1)
                a = stat("ma", 16).rearrange("p (t h) -> p t h", h=H)
                o = begin(("aT",))
                for t in range(NT):
                    ins = tpose(o[0:H, t * P:(t + 1) * P], a[:, t, :])
                ins.then_inc(psum_full, 1)
                need.wait_ge(sem("m_negM"), 1)
                o = begin(("MT",))
                for t in range(NT):
                    ins = tpose(o[:, t * H:(t + 1) * H], nMT[0:H, t * P:(t + 1) * P], H)
                ins.then_inc(psum_full, 1)
                for w in range(2):
                    need.wait_ge(*J.freed(("mqk", w)))
                need.wait_ge(*J.freed(("mv", 1)))
                for hh in range(H):
                    pp = slice(32 * hh, 32 * hh + 32)
                    sl = cst("sel4")[0:H, hh * P:(hh + 1) * P]
                    o = begin(("mB", hh))
                    e.matmul(o, sl, nMT[0:H, :], start=True, stop=True).then_inc(psum_full, 1)
                    o = begin(("mD", hh))
                    e.matmul(o, sl, nMT[0:H, :], start=True, stop=False, skip_group_check=True)
                    for t in range(NT):
                        ins = e.matmul(o[:, t * P:(t + 1) * P], cbt("identb"), cbt("maskT"), start=False,
                                       stop=(t == NT - 1), skip_group_check=True)
                    ins.then_inc(psum_full, 1)
                    for j in range(NT):
                        o = begin(("mS", hh, j))
                        e.matmul(o[:, j * P:S], mkT[pp, j * P:(j + 1) * P], mqT[pp, j * P:S],
                                      start=True, stop=True).then_inc(psum_full, 1)
                    for j in range(NT):
                        need.wait_ge(*J.freed(("mS", hh, j)))
                    o = begin(("mO", hh))
                    for t in range(NT):
                        for j in range(t + 1):
                            ins = e.matmul(o[:, t * 65:(t + 1) * 65], Em[:, hh % 2, j, t * P:(t + 1) * P],
                                           mV[:, j, hh, :], start=(j == 0), stop=(j == t))
                    ins.then_inc(psum_full, 1)

            def out_proj():
                need.wait_ge(sem("y_done"), 4)
                for k in range(KD):
                    o = begin(("yT", k))
                    for t in range(NT):
                        ins = tpose(o[:, t * P:(t + 1) * P], y[:, t, k * P:(k + 1) * P])
                    ins.then_inc(psum_full, 1)
                for k in (KD - 2, KD - 1):
                    need.wait_ge(*J.freed(("yT", k)))
                for u in range(4):
                    for tp in range(2):
                        proj_N(("wo", u, tp), f"wo{u}", tp, 256)

            def cross():
                need.wait_ge(sem("mem_norm"), 2)
                for k in range(KD):
                    o = begin(("memT", k))
                    for t in range(NMT):
                        ins = tpose(o[:, t * P:(t + 1) * P], memn[:, t, :].rearrange("p (c k) -> p k c", k=KD)[:, k, :])
                    ins.then_inc(psum_full, 1)
                for k in (KD - 2, KD - 1):
                    need.wait_ge(*J.freed(("memT", k)))
                proj_N(("xk",), "xkw", 0, GW, lhs=memT)
                proj_N(("xv",), "xvw", 0, GW, lhs=memT)
                e.drain().then_inc(sem("place_free"), 1)
                transposed_norm("xa")
                got_hnT("xa")
                for tp in range(2):
                    proj_N(("xq", tp), "xqw", tp, GW)
                need.wait_ge(sem("x_qk"), 2)
                for hp in range(2):
                    o = begin(("xqT", hp))
                    for t in range(NT):
                        ins = tpose(o[:, t * P:(t + 1) * P], xQ[:, t, hp * P:(hp + 1) * P])
                    ins.then_inc(psum_full, 1)
                    o = begin(("xkT", hp))
                    for t in range(NMT):
                        ins = tpose(o[:, t * P:(t + 1) * P], xK[:, t, hp * P:(hp + 1) * P])
                    ins.then_inc(psum_full, 1)
                for hp in range(2):
                    need.wait_ge(*J.freed(("xqT", hp)))
                    need.wait_ge(*J.freed(("xkT", hp)))
                need.wait_ge(*J.freed(("xv",)))
                attention(XATT)
                need.wait_ge(*J.freed(("O", 107)))
                for hp in range(2):
                    o = begin(("xoT", hp))
                    for t in range(NT):
                        ins = tpose(o[:, t * P:(t + 1) * P], xO[:, t, hp * P:(hp + 1) * P])
                    ins.then_inc(psum_full, 1)
                for hp in range(2):
                    need.wait_ge(*J.freed(("xoT", hp)))
                need.wait_ge(*weights_in("xow"))
                w = slot("xow").rearrange("p (k n) -> p k n", k=2)
                for t in range(NT):
                    for c in range(2):
                        o = begin(("xo", t, c))
                        for k in range(2):
                            ins = e.matmul(o, xoT[:, k, t * P:(t + 1) * P], w[:, k, c * 512:(c + 1) * 512],
                                           start=(k == 0), stop=(k == 1))
                        ins.then_inc(psum_full, 1)

            def moe():
                transposed_norm("moe")
                got_hnT("moe")
                for t in range(NT):
                    o = begin(("route", t))
                    for k in range(KD):
                        ins = e.matmul(o[:, 0:36], hnT[:, k, t * P:(t + 1) * P], wr[:, k, :],
                                       start=(k == 0), stop=(k == KD - 1))
                    ins.then_inc(psum_full, 1)
                need.wait_ge(sem("chosen"), 1)
                ch = stat("chosen", NT * NE).rearrange("p (t n) -> p t n", t=NT)
                o = begin(("rank",))
                for t in range(NT):
                    for a in range(t + 1):
                        e.matmul(o[:, t * NE:(t + 1) * NE], cst("striu" if a == t else "ones"), ch[:, a, :],
                                 start=(a == 0), stop=(a == t))
                for a in range(NT):
                    ins = e.matmul(o[:, NT * NE:(NT + 1) * NE], cst("ones"), ch[:, a, :],
                                   start=(a == 0), stop=(a == NT - 1))
                ins.then_inc(psum_full, 1)
                for b in [n for n in J.info if n[0] in ("hT", "xo", "route", "rank")]:
                    need.wait_ge(*J.freed(b))
                need.wait_ge(sem("routed"), 1)
                nr = e.value_load(rounds[0:1, 0:1], min_val=1, max_val=ROUNDS)
                e.drain().then_inc(sem("moe_T"), 2)
                with e.Fori(0, nr) as r:
                    with e.Fori(0, NE // QE) as i:
                        for b in range(2):
                            e.wait_ge(sem(f"rows_in{b}"), 128 * r + 16 * i + 16)
                            e.wait_ge(sem("rowsT_act"), 16 * r + 2 * i + b + 1)
                            e.wait_ge(sem("rowsT_dve"), 16 * r + 2 * i + b + 1)
                            for k in range(KD):
                                ins = tpose(psum[:, 2 + k // 4, (k % 4) * P:(k % 4 + 1) * P],
                                            X2[:, b, :].rearrange("p (c k) -> p k c", k=KD)[:, k, :])
                            ins.then_inc(sem("moe_T"), 1)
                            e.wait_ge(sem("rowsT_act"), 16 * r + 2 * i + b + 2)
                            e.wait_ge(sem("rowsT_dve"), 16 * r + 2 * i + b + 2)
                            for x in range(2):
                                q = 2 * b + x
                                w1, w3 = (expert_slot(q, n).rearrange("p (k f) -> p k f", k=KD) for n in range(2))
                                e.wait_ge(sem(f"expert_in{q}"), 384 * r + 48 * i + 48)
                                e.wait_ge(sem("moe_gated"), 32 * r + 4 * i + q + 1)
                                for g, wt in enumerate((w1, w3)):
                                    for m in range(2):
                                        c0 = (2 * g + m) * CAP
                                        for k in range(KD):
                                            ins = e.matmul(psum[:, x, c0:c0 + CAP], wt[:, k, m * P:(m + 1) * P],
                                                           X2T[:, b, k, x * CAP:(x + 1) * CAP],
                                                           start=(k == 0), stop=(k == KD - 1))
                                ins.then_inc(sem("moe_up"), 1)
                            e.wait_ge(sem("y_act"), 16 * r + 2 * i + b + 1)
                            e.wait_ge(sem("y_dve"), 16 * r + 2 * i + b + 1)
                            for x in range(2):
                                q = 2 * b + x
                                w2 = expert_slot(q, 2).rearrange("p (m n) -> p m n", m=2)
                                e.wait_ge(sem("moe_gated"), 32 * r + 4 * i + q + 3)
                                for c in range(2):
                                    for m in range(2):
                                        ins = e.matmul(psum[x * CAP:(x + 1) * CAP, 4 + 2 * b + c, :],
                                                       aTm[:, x, m, :], w2[:, m, c * 512:(c + 1) * 512],
                                                       start=(m == 0), stop=(m == 1))
                                ins.then_inc(sem("moe_down"), 1)

            e.wait_ge(sem("const_in"), 48)
            with e.Fori(0, L) as l:
                need.new_layer()
                transposed_norm("mix")
                got_hnT("mix")
                gdn()
                phase(e, need, 1)
                nsa_diff()
                phase(e, need, 2)
                mlstm()
                phase(e, need, 3)
                out_proj()
                cross()
                e.drain().then_inc(sem("place_free"), 1)
                phase(e, need, 4)
                e.drain().then_inc(sem("place_free"), 2)
                moe()
                layer_end(e, "pe")

        @block.scalar
        def _(e):
            need = Waits(e)
            stepped = sem("act_stepped")
            step = Steps(stepped)
            psum_free = J.free["A"]
            act = e.activation
            epsc = cst("eps")

            def take(name, dst, scale=None, src=None, func=ACT.Copy):
                need.wait_ge(psum_full, J.number(name))
                ps = bank(name)
                ins = act(dst, ps if src is None else src(ps), func, **({} if scale is None else {"scale": scale}))
                ins.then_inc(psum_free, 1)

            def rsqrt(src, dst, n, signal, scale=None):
                p = src.shape[0]
                tmp = stat("rsq_tmp", 64)[0:p, 0:src.shape[1]]
                need.wait_ge(stepped, step(act(tmp, src, ACT.Ln, scale=1.0 / n, bias=epsc[0:p])))
                act(dst, tmp, ACT.Exp, scale=-0.5).then_inc(sem(signal), 1)

            def norm_stats(nm):
                ss = stat("h_ss", NT)
                for t in range(NT):
                    if nm == "xa":
                        for u in range(4):
                            need.wait_ge(*J.freed(("wo", u, t // 2)))
                    if nm == "moe":
                        for c in range(2):
                            need.wait_ge(*J.freed(("xo", t, c)))
                    need.wait_ge(stepped, step(act(junk, h_res[:, t, :], ACT.Square, accum_out=ss[:, t:t + 1])))
                need.wait_ge(stepped, step.count)
                rsqrt(ss, stat("h_rstd", NT), D, f"rstd_{nm}")

            def hT(nm):
                for k in range(0, KD, 2):
                    take(("hT", nm, k), hnT[:, k, :],
                         scale=None if nm == "moe" else col[:, col_ln(nm) + k:col_ln(nm) + k + 1])

            def exps(items):
                for n, (br, pr, t, kl) in items:
                    need.wait_ge(psum_full, J.number(("S", n)))
                    ps = bank(("S", n))
                    need.wait_ge(sem("neg_max"), item_count(n))
                    if n % 100 >= 2 or n >= 100:
                        need.wait_ge(psum_full, J.number(("PT", prev_item(n))))
                    for m in range(2):
                        ins = act(Pm[:, n % 2, m, 0:kl], ps[:, m, 0:kl], ACT.Exp,
                                  bias=stat("nmax", 8)[:, 2 * (n % 4) + m:2 * (n % 4) + m + 1],
                                  accum_out=stat("psums", 8)[:, 2 * (n % 4) + m:2 * (n % 4) + m + 1])
                        if m == 0:
                            step(ins)
                    ins.then_inc(psum_free, 1)
                    if n % 2 == 0:
                        w = (-(-kl // P)) * P
                        pk = min(P, kl)
                        need.wait_ge(psum_full, J.number(("PT", n)))
                        pt = bank(("PT", n))
                        if n % 100 >= 2 or n >= 100:
                            need.wait_ge(psum_full, J.number(("O", prev_item(n))))
                        act(PTm[0:pk, n % 2, :, 0:w], pt[0:pk, :, 0:w], ACT.Copy).then_inc(psum_free, 1)

            e.wait_ge(sem("const_in"), 48)
            with e.Fori(0, L) as l:
                need.new_layer()
                step.count = 0
                junk = view(0, 1024)
                need.wait_ge(sem("params_in"), 80)
                norm_stats("mix")
                hT("mix")
                for c in range(0, 6, 2):
                    if c == 0:
                        need.wait_ge(sem("raw_zero"), 1)
                    take(("gp", c), raw[:, c, 3:515])
                for tp in range(2):
                    need.wait_ge(psum_full, J.number(("z", tp)))
                    ps = bank(("z", tp))
                    act(zgate[:, 2 * tp:2 * tp + 2, :], ps.rearrange("p (t n) -> p t n", t=2), ACT.Silu).then_inc(psum_free, 1)
                for c in range(6):
                    need.wait_ge(sem("g_conv"), c + 1)
                    act(conv[:, c, :], conv[:, c, :], ACT.Silu).then_inc(sem("g_silu"), 1)
                for w in range(3):
                    take(("gn", w, 0), gnat[:, w, 0:2].rearrange("p t h d -> p t (h d)"),
                         src=lambda ps: ps.rearrange("p (t n) -> p t n", t=2))
                need.wait_ge(sem("g_gates"), 1)
                t1, t2, t3 = stat("t1", 16), stat("t2", 16), stat("t3", 4)
                act(t1, t1, ACT.Exp, scale=-1.0).then_inc(sem("g_exp"), 1)
                bcol = small[:, :, 144:148]
                act(t2.rearrange("p (t h) -> p t h", h=H), bcol, ACT.Exp, scale=-1.0).then_inc(sem("g_exp"), 1)
                act(t3, rowp("a_log"), ACT.Exp).then_inc(sem("g_exp"), 1)
                need.wait_ge(sem("g_one_plus"), 1)
                act(stat("t4", 16), stat("t4", 16), ACT.Ln).then_inc(sem("g_ln"), 1)
                need.wait_ge(sem("g_ss"), 1)
                rsqrt(stat("g_ss", 32), stat("g_rs", 32), 1.0, "g_rs")
                need.wait_ge(psum_full, J.number(("gc",)))
                ps = bank(("gc",))
                act(stat("gcgl", 32), ps[:, 0:32], ACT.Copy).then_inc(psum_free, 1)
                need.wait_ge(*J.freed(("gc",)))
                act(stat("egcgl", 32), stat("gcgl", 32), ACT.Exp).then_inc(sem("g_egc"), 1)
                need.wait_ge(sem("g_gend"), 1)
                act(stat("gend", 16), stat("gend", 16), ACT.Exp).then_inc(sem("g_egend"), 1)
                for w in range(4):
                    take(("gT", w, 0), gtr[:, w, 0, :])
                for hh in range(H):
                    need.wait_ge(psum_full, J.number(("gD", hh)))
                    ps = bank(("gD", hh))
                    if hh >= 2:
                        need.wait_ge(*J.freed(("gQ", hh - 2)))
                    for t in range(NT):
                        ins = act(dec_v[:, hh % 2, t, :], ps[:, t * P:(t + 1) * P], ACT.Exp,
                                  bias=stat("ngc", 16)[:, t * H + hh:t * H + hh + 1])
                    ins.then_inc(psum_free, 1)
                for hh in range(H):
                    take(("T0", hh), gT_[:, hh].rearrange("p t n -> p (t n)"))
                for n in range(1, LEVELS):
                    for hh in range(H):
                        if n > 1:
                            need.wait_ge(psum_full, J.number(("U", n - 1, hh)))
                        take(("X", n, hh), gX[:, hh].rearrange("p t n -> p (t n)"))
                for hp in range(2):
                    need.wait_ge(psum_full, J.number(("gQ", H - 1)))
                    take(("wT", hp), gtr[:, 2, hp, :], scale=-1.0)
                for t in range(NT):
                    if t >= 2:
                        need.wait_ge(psum_full, J.number(("gS", t - 2)))
                    take(("vn", t), vnew[:, t % 2].rearrange("p h d -> p (h d)"), src=lambda ps: ps[:, 0:GW])
                    take(("go", t), y[:, t, GW:2 * GW], src=lambda ps: ps[:, 0:GW])
                need.wait_ge(sem("post_ss_gdn"), 1)
                rsqrt(stat("post_ss", 16), stat("post_rs", 16), DH, "post_rs_gdn")
                phase(e, need, 1)
                take(("nq", 0), nX[:, 0:2, 0:4, :].rearrange("p t h d -> p t (h d)"),
                     src=lambda ps: ps.rearrange("p (t n) -> p t n", t=2))
                for j in range(2):
                    need.wait_ge(sem("gelu_arg"), j + 1)
                    act(hidt[:, j, 0:NCMP], hidt[:, j, 0:NCMP], ACT.Exp, scale=-1.0).then_inc(sem("gelu_exp"), 1)
                need.wait_ge(sem("ck_ss"), 1)
                rsqrt(stat("ck_ss", 1)[0:NCMP], stat("ck_rs", 1)[0:NCMP], DH, "ck_rs")
                act(small[:, :, 128:140], small[:, :, 128:140], ACT.Exp, scale=-1.0).then_inc(sem("gate_exp"), 1)
                need.wait_ge(sem("n_ss"), 1)
                rsqrt(stat("n_ss", 24), stat("n_rs", 24), DH, "n_rs")
                need.wait_ge(sem("lam_dots"), 1)
                act(stat("lamv", 2), stat("lamv", 2), ACT.Exp).then_inc(sem("lam_exp"), 1)
                for pr in (0, 2):
                    take(("nT", pr), nTr[:, pr, :], scale=0.125 if pr == 0 else None)
                for w in range(3):
                    dst = dV[:, 0:2, :] if w == 2 else dX[:, 0:2, w * GW:(w + 1) * GW]
                    take(("dp", w, 0), dst, src=lambda ps: ps.rearrange("p (t n) -> p t n", t=2))
                need.wait_ge(sem("d_ss"), 1)
                rsqrt(stat("d_ss", 64), stat("d_rs", 64), DH // 2, "d_rs")
                for pr in (0, 2):
                    take(("dT", pr), dTr[:, pr, :], scale=float(32 ** -0.5) if pr == 0 else None)
                exps(ATT)
                need.wait_ge(sem("post_ss_diff"), 1)
                rsqrt(stat("post_ss", 16), stat("post_rs", 16), DH, "post_rs_diff")
                phase(e, need, 2)
                take(("mqk", 0), mqT[:, :], scale=float(32 ** -0.5))
                need.wait_ge(sem("m_gates"), 1)
                mt1 = stat("mt1", 32)
                act(mt1, mt1, ACT.Exp, scale=-2.0).then_inc(sem("m_exp"), 1)
                need.wait_ge(sem("m_capped"), 1)
                mt2 = stat("mt2", 16)
                act(mt2, mt2, ACT.Exp, scale=-1.0).then_inc(sem("m_exp"), 1)
                need.wait_ge(sem("m_one_plus"), 1)
                act(mt2, mt2, ACT.Ln).then_inc(sem("m_ln"), 1)
                for tp in range(2):
                    need.wait_ge(psum_full, J.number(("mo", tp)))
                    ps = bank(("mo", tp))
                    act(mO[:, 2 * tp:2 * tp + 2, :], ps.rearrange("p (t n) -> p t n", t=2), ACT.Exp,
                               scale=-1.0).then_inc(psum_free, 1)
                need.wait_ge(psum_full, J.number(("MT",)))
                ps = bank(("MT",))
                act(stat("nM", 16), ps[:, 0:16], ACT.Copy).then_inc(psum_free, 1)
                need.wait_ge(sem("m_negm"), 1)
                act(stat("enm", 16), stat("enm", 16), ACT.Exp).then_inc(sem("m_expm"), 1)
                a = stat("ma", 16)
                for hh in range(H):
                    if hh >= 2:
                        need.wait_ge(psum_full, J.number(("mO", hh - 2)))
                    need.wait_ge(psum_full, J.number(("mB", hh)))
                    ps = bank(("mB", hh))
                    for j in range(NT - 1):
                        ins = act(Em[:, hh % 2, j, (j + 1) * P:S], ps[:, (j + 1) * P:S], ACT.Exp,
                                  bias=a[:, j * H + hh:j * H + hh + 1])
                    ins.then_inc(psum_free, 1)
                    need.wait_ge(psum_full, J.number(("mD", hh)))
                    ps = bank(("mD", hh))
                    for j in range(NT):
                        ins = act(Em[:, hh % 2, j, j * P:(j + 1) * P], ps[:, j * P:(j + 1) * P], ACT.Exp,
                                  bias=a[:, j * H + hh:j * H + hh + 1])
                    ins.then_inc(psum_free, 1)
                need.wait_ge(sem("post_ss_mlstm"), 1)
                rsqrt(stat("post_ss", 16), stat("post_rs", 16), DH, "post_rs_mlstm")
                phase(e, need, 3)
                for k in range(0, KD, 2):
                    take(("yT", k), hnT[:, k, :])
                need.wait_ge(sem("mem_in"), 16)
                xj = xtmp[:, 0:1024]
                for t in range(NMT):
                    need.wait_ge(stepped, step(act(xj, memn[:, t, :], ACT.Square, accum_out=stat("mem_ss", 2)[:, t:t + 1])))
                need.wait_ge(stepped, step.count)
                rsqrt(stat("mem_ss", 2), stat("mem_rs", 2), D, "mem_rs")
                for k in range(0, KD, 2):
                    take(("memT", k), memT[:, k, :], scale=col[:, col_ln("mem") + k:col_ln("mem") + k + 1],
                         src=lambda ps: ps[:, 0:MEM])
                take(("xv",), xV, src=lambda ps: ps.rearrange("p (t n) -> p t n", t=2))
                junk = xtmp[:, 0:1024]
                norm_stats("xa")
                hT("xa")
                take(("xq", 0), xQ[:, 0:2, :], src=lambda ps: ps.rearrange("p (t n) -> p t n", t=2))
                need.wait_ge(sem("xk_ss"), 1)
                rsqrt(stat("xk_ss", 8), stat("xk_rs", 8), DH, "xk_rs")
                need.wait_ge(sem("xq_ss"), 1)
                rsqrt(stat("xq_ss", 16), stat("xq_rs", 16), DH, "xq_rs")
                for hp in range(2):
                    take(("xqT", hp), xqT[:, hp, :], scale=0.125)
                exps(XATT)
                take(("xoT", 0), xoT[:, 0, :])
                norm_stats("moe")
                phase(e, need, 4)
                hT("moe")
                need.wait_ge(sem("route_arg"), 1)
                act(stat("r_exp", 20), stat("r_exp", 20), ACT.Exp).then_inc(sem("route_exp"), 1)
                need.wait_ge(sem("routed"), 1)
                nr = e.value_load(rounds[0:1, 0:1], min_val=1, max_val=ROUNDS)
                e.drain().then_inc(sem("rowsT_act"), 1)
                e.drain().then_inc(sem("y_act"), 2)
                with e.Fori(0, nr) as r:
                    with e.Fori(0, NE // QE) as i:
                        for b in range(2):
                            e.wait_ge(sem("moe_T"), 16 * r + 2 * i + b + 3)
                            act(X2T[:, b, 0:4, :], psum[:, 2, :], ACT.Copy).then_inc(sem("rowsT_act"), 1)
                            for x in range(2):
                                e.wait_ge(sem("moe_up"), 32 * r + 4 * i + 2 * b + x + 1)
                                e.wait_ge(sem("moe_gated"), 32 * r + 4 * i + 2 * b + x + 1)
                                act(sgl[:, x], psum[:, x, 0:2 * CAP], ACT.Silu).then_inc(sem("moe_silu"), 1)
                            e.wait_ge(sem("moe_down"), 32 * r + 4 * i + 2 * b + 2)
                            e.wait_ge(sem("y_out"), 256 * r + 32 * i + 16 * b + 16)
                            act(Ye[:, 0:512], psum[:, 4 + 2 * b, :], ACT.Copy).then_inc(sem("y_act"), 1)
                e.wait_ge(sem("y_out"), 256 * nr + 16)
                for t in range(NT):
                    e.dma_start(Yg[:, t], y_rows[2 * P * t:2 * P * (t + 1), :].rearrange("(p n) d -> p n d", n=2))\
                        .then_inc(sem("y_rows_in"), 16)
                layer_end(e, "act")

        @block.vector
        def _(e):
            need = Waits(e)
            stepped = sem("dve_stepped")
            step = Steps(stepped)
            psum_free = J.free["D"]
            tt, ts, stt = e.tensor_tensor, e.tensor_scalar, e.scalar_tensor_tensor
            rsum = e.reduce_sum

            def take(name, dst, src=None, mul=None):
                need.wait_ge(psum_full, J.number(name))
                ps = bank(name)
                ps = ps if src is None else src(ps)
                ins = e.tensor_copy(dst, ps) if mul is None else ts(dst, ps, mul, None, ALU.mult)
                ins.then_inc(psum_free, 1)

            two = lambda ps: ps.rearrange("p (t n) -> p t n", t=2)

            def scale_norm(nm):
                need.wait_ge(sem(f"rstd_{nm}"), 1)
                for t in range(NT):
                    rstd = stat("h_rstd", NT)[:, t:t + 1]
                    if nm == "moe":
                        need.wait_ge(sem("gmoe_in"), 16)
                        ins = stt(y[:, t, :], h_res[:, t, :], rstd, gmoe, ALU.mult, ALU.mult)
                    else:
                        ins = ts(y[:, t, :], h_res[:, t, :], rstd, None, ALU.mult)
                    ins.then_inc(sem(f"hn_{nm}"), 1)

            def hT(nm):
                for k in range(1, KD, 2):
                    take(("hT", nm, k), hnT[:, k, :],
                         mul=None if nm == "moe" else col[:, col_ln(nm) + k:col_ln(nm) + k + 1])

            def rope(X, Y, cos, sin, tA, tB, half, outs):
                x1, x2 = X[..., 0:half], X[..., half:2 * half]
                step(tt(tA, x1, cos, ALU.mult))
                step(tt(tB, x2, sin, ALU.mult))
                need.wait_ge(stepped, step.count)
                for a, b in outs:
                    step(tt(Y[b + (slice(0, half),)], tA[a], tB[a], ALU.subtract))
                need.wait_ge(stepped, step.count)
                step(tt(tA, x2, cos, ALU.mult))
                step(tt(tB, x1, sin, ALU.mult))
                need.wait_ge(stepped, step.count)
                for a, b in outs:
                    ins = tt(Y[b + (slice(half, 2 * half),)], tA[a], tB[a], ALU.add)
                    if (a, b) != outs[-1]:
                        step(ins)
                need.wait_ge(stepped, step.count)
                return ins

            def attention_out(items):
                for n, (br, pr, t, kl) in items:
                    need.wait_ge(psum_full, J.number(("S", n)))
                    ps = bank(("S", n))
                    k4 = 2 * (n % 4)
                    e.tensor_reduce(stat("nmax", 8)[:, k4:k4 + 2], ps[:, :, 0:kl], AXX, ALU.max, negate=True)\
                        .then_inc(sem("neg_max"), 1)
                    if n % 2:
                        w = (-(-kl // P)) * P
                        pk = min(P, kl)
                        need.wait_ge(psum_full, J.number(("PT", n)))
                        pt = bank(("PT", n))
                        if n % 100 >= 2 or n >= 100:
                            need.wait_ge(psum_full, J.number(("O", prev_item(n))))
                        e.tensor_copy(PTm[0:pk, n % 2, :, 0:w], pt[0:pk, :, 0:w]).then_inc(psum_free, 1)
                    need.wait_ge(*J.freed(("S", n)))
                    rs = stat("rsum", 8)[:, k4:k4 + 2]
                    need.wait_ge(stepped, step(e.reciprocal(rs, stat("psums", 8)[:, k4:k4 + 2])))
                    if br in ("cmp", "sel", "win"):
                        b = ("cmp", "sel", "win").index(br)
                        g = small[:, t, 128:140].rearrange("p (h b) -> p b h", b=3)[:, b, 2 * pr:2 * pr + 2]
                        need.wait_ge(stepped, step(tt(rs, rs, g, ALU.mult)))
                    if br == "diff":
                        need.wait_ge(stepped, step(tt(rs, rs, stat("lamw", 2), ALU.mult)))
                    need.wait_ge(psum_full, J.number(("O", n)))
                    ps = bank(("O", n))
                    if br == "diff":
                        o = y[:, t, 3 * GW + pr * DH:3 * GW + (pr + 1) * DH]
                        need.wait_ge(stepped, step(ts(o, ps[:, 0:DH], rs[:, 0:1], None, ALU.mult)))
                        stt(o, ps[:, DH:2 * DH], rs[:, 1:2], o, ALU.mult, ALU.add).then_inc(psum_free, 1)
                        continue
                    for m in range(2):
                        o = (xO if br == "cross" else y)[:, t, (2 * pr + m) * DH:(2 * pr + m + 1) * DH]
                        src = ps[:, m * DH:(m + 1) * DH]
                        if br in ("cmp", "cross"):
                            ins = ts(o, src, rs[:, m:m + 1], None, ALU.mult)
                        else:
                            if m == 0:
                                need.wait_ge(*J.freed(("O", n - 8)))
                            ins = stt(o, src, rs[:, m:m + 1], o, ALU.mult, ALU.add)
                        if m == 0:
                            step(ins)
                    ins.then_inc(psum_free, 1)

            def post(nm, g, gain):
                yg = y[:, :, g * GW:(g + 1) * GW].rearrange("p t (h d) -> p t h d", h=H)
                tmp = view({"gdn": 0, "diff": 14272, "mlstm": 3088}[nm], NT, H, DH)
                need.wait_ge(stepped, step.count)
                need.wait_ge(stepped, step(tt(tmp, yg, yg, ALU.mult)))
                rsum(stat("post_ss", 16).rearrange("p (t h) -> p t h", h=H), tmp, AXX)\
                    .then_inc(sem("post_ss_" + nm), 1)
                need.wait_ge(sem("post_rs_" + nm), 1)
                rs = stat("post_rs", 16).rearrange("p (t h) -> p t h", h=H)
                need.wait_ge(stepped, step(tt(yg, yg, rs.unsqueeze(3).broadcast_to([P, NT, H, DH]), ALU.mult)))
                gn = rowp(gain).unsqueeze(1).broadcast_to([P, NT * H, DH])
                ygf = y[:, :, g * GW:(g + 1) * GW].rearrange("p t (h d) -> p t h d", h=H)
                need.wait_ge(stepped, step(tt(ygf, ygf, rowp(gain).unsqueeze(1).unsqueeze(1).broadcast_to([P, NT, H, DH]), ALU.mult)))

            e.wait_ge(sem("const_in"), 48)
            with e.Fori(0, L) as l:
                need.new_layer()
                step.count = 0
                need.wait_ge(sem("params_in"), 80)
                scale_norm("mix")
                hT("mix")
                for c in range(1, 6, 2):
                    if c == 1:
                        need.wait_ge(sem("raw_zero"), 1)
                    take(("gp", c), raw[:, c, 3:515])
                for tp in range(2):
                    take(("small", tp), small[:, 2 * tp:2 * tp + 2, :],
                         src=lambda ps: ps[:, 0:2 * NSMALL].rearrange("p (t n) -> p t n", t=2))
                taps = col[:, 4 * KD:4 * KD + 24].rearrange("p (c j) -> p c j", j=4)
                for c in range(6):
                    need.wait_ge(*J.freed(("gp", c)))
                for c in range(0, 6, 2):
                    for j in range(4):
                        for cc in (c, c + 1):
                            src = raw[:, cc, j:j + 512]
                            if j == 0:
                                ins = ts(conv[:, cc, :], src, taps[:, cc, 0:1], None, ALU.mult)
                            else:
                                ins = stt(conv[:, cc, :], src, taps[:, cc, j:j + 1], conv[:, cc, :], ALU.mult, ALU.add)
                            if j < 3:
                                step(ins)
                            else:
                                ins.then_inc(sem("g_conv"), 1)
                        need.wait_ge(stepped, step.count)
                need.wait_ge(*J.freed(("small", 1)))
                t1, t2, t3, t4, t5 = stat("t1", 16), stat("t2", 16), stat("t3", 4), stat("t4", 16), stat("t5", 16)
                v3 = lambda s: s.rearrange("p (t h) -> p t h", h=H)
                rb = lambda n: rowp(n).unsqueeze(1).broadcast_to([P, NT, H])
                need.wait_ge(stepped, step(tt(v3(t5), small[:, :, 140:144], rb("dt_bias"), ALU.add)))
                step(ts(t4, t5, -1.0, None, ALU.mult))
                need.wait_ge(stepped, step.count)
                tt(t1, t5, t4, ALU.max).then_inc(sem("g_gates"), 1)
                need.wait_ge(sem("g_gates"), 1)
                need.wait_ge(sem("g_exp"), 3)
                step(ts(t5, t5, 0.0, None, ALU.max))
                need.wait_ge(stepped, step.count)
                ts(t4, t1, 1.0, None, ALU.add).then_inc(sem("g_one_plus"), 1)
                beta = stat("beta", 16)
                need.wait_ge(stepped, step(ts(t2, t2, 1.0, None, ALU.add)))
                need.wait_ge(stepped, step(e.reciprocal(beta, t2)))
                need.wait_ge(sem("g_ln"), 1)
                need.wait_ge(stepped, step(tt(t5, t5, t4, ALU.add)))
                need.wait_ge(stepped, step(ts(t3, t3, -1.0, None, ALU.mult)))
                g = stat("g", 16)
                tt(v3(g), v3(t5), t3.unsqueeze(1).broadcast_to([P, NT, H]), ALU.mult).then_inc(sem("g_logdecay"), 1)
                for w in range(3):
                    take(("gn", w, 1), gnat[:, w, 2:4].rearrange("p t h d -> p t (h d)"), src=two)
                for w in range(3):
                    need.wait_ge(*J.freed(("gn", w, 0)))
                    need.wait_ge(*J.freed(("gn", w, 1)))
                sq = view(0, 2 * NT * H, DH)
                gf = gnat[:, 0:2].rearrange("p w t h d -> p (w t h) d")
                need.wait_ge(sem("g_silu"), 6)
                need.wait_ge(stepped, step(tt(sq, gf, gf, ALU.mult)))
                rsum(stat("g_ss", 32), sq, AXX).then_inc(sem("g_ss"), 1)
                need.wait_ge(sem("g_rs"), 1)
                rs = stat("g_rs", 32)
                need.wait_ge(stepped, step(ts(rs[:, 0:16], rs[:, 0:16], DH ** -0.5, None, ALU.mult)))
                tt(gf, gf, rs.unsqueeze(2).broadcast_to([P, 32, DH]), ALU.mult).then_inc(sem("g_qk"), 1)
                need.wait_ge(sem("g_qk"), 1)

                def heads(w):
                    return gnat[:, w].rearrange("p t h d -> p (t h) d")

                def per(s):
                    return s.unsqueeze(2).broadcast_to([P, 16, DH])
                tt(heads(3), heads(1), per(beta), ALU.mult).then_inc(sem("g_kbeta"), 1)
                tt(heads(2), heads(2), per(beta), ALU.mult).then_inc(sem("g_vbeta"), 1)
                need.wait_ge(*J.freed(("gc",)))
                gcgl = stat("gcgl", 32)
                tt(stat("gend", 16), gcgl[:, 16:32], gcgl[:, 0:16], ALU.subtract).then_inc(sem("g_gend"), 1)
                step(ts(stat("ngc", 16), gcgl[:, 0:16], -1.0, None, ALU.mult))
                need.wait_ge(stepped, step.count)
                e.sem_inc(sem("g_ngc"), 1)
                need.wait_ge(sem("g_egc"), 1)
                take(("gT", 0, 1), gtr[:, 0, 1, :])
                tt(heads(0), heads(0), per(stat("egcgl", 32)[:, 0:16]), ALU.mult).then_inc(sem("g_qd"), 1)
                take(("gT", 1, 1), gtr[:, 1, 1, :])
                need.wait_ge(sem("g_egend"), 1)
                tt(heads(1), heads(1), per(stat("gend", 16)), ALU.mult).then_inc(sem("g_kend"), 1)
                take(("gT", 2, 1), gtr[:, 2, 1, :])
                tt(heads(3), heads(3), per(stat("egcgl", 32)[:, 0:16]), ALU.mult).then_inc(sem("g_kbe"), 1)
                take(("gT", 3, 1), gtr[:, 3, 1, :])
                for hh in range(H):
                    need.wait_ge(*J.freed(("gD", hh)))
                    dd = dec_v[:, hh % 2]
                    for nm, dst in (("gA", AT), ("gQ", atT)):
                        need.wait_ge(psum_full, J.number((nm, hh)))
                        ps = bank((nm, hh))
                        tt(dst[:, hh], ps.rearrange("p (t i) -> p t i", t=NT), dd, ALU.mult).then_inc(psum_free, 1)
                lv = lambda n: cbt("lvl")[:, n * P:(n + 1) * P].unsqueeze(1).broadcast_to([P, NT, P])
                ident = cst("ident").unsqueeze(1).broadcast_to([P, NT, P])
                for hh in range(H):
                    need.wait_ge(*J.freed(("gA", hh)))
                    need.wait_ge(stepped, step(tt(Bm_v[:, hh % 2], AT[:, hh], lv(0), ALU.mult)))
                    tt(gU[:, hh], ident, Bm_v[:, hh % 2], ALU.subtract).then_inc(sem("g_U0"), 1)
                for n in range(1, LEVELS):
                    for hh in range(H):
                        if n == 1 and hh < 2:
                            need.wait_ge(sem("g_U0"), 4)
                        if n > 1 or hh >= 2:
                            k = (n - 1) * H + hh - 2
                            need.wait_ge(psum_full, J.number(("X", k // H + 1, k % H)))
                        tt(Bm_v[:, hh % 2], AT[:, hh], lv(n), ALU.mult).then_inc(sem("g_B"), 1)
                    for hh in range(H):
                        for nm, dst in (("T", gT_), ("U", gU)):
                            if nm == "T" and n == LEVELS - 1:
                                continue
                            need.wait_ge(psum_full, J.number((nm, n, hh)))
                            ps = bank((nm, n, hh)).rearrange("p (t i) -> p t i", t=NT)
                            if nm == "T":
                                need.wait_ge(*J.freed(("T0", hh)))
                            tt(dst[:, hh], dst[:, hh], ps, ALU.subtract).then_inc(psum_free, 1)
                egl = stat("egcgl", 32)[:, 16:32]
                need.wait_ge(stepped, step(e.memset(state, 0.0)))
                for t in range(NT):
                    need.wait_ge(psum_full, J.number(("gS", t)))
                    ps = bank(("gS", t))
                    for hh in range(H):
                        q = hh % 2
                        pp = slice(q * DH, (q + 1) * DH)
                        s_ = state[pp, hh, :]
                        src = ps[pp, (hh // 2) * DH:(hh // 2 + 1) * DH]
                        if t == 0:
                            ins = e.tensor_copy(s_, src)
                        else:
                            if hh == 0:
                                need.wait_ge(*J.freed(("gS", t - 1)))
                            ins = stt(s_, s_, egl[pp, t * H + hh:t * H + hh + 1], src, ALU.mult, ALU.add)
                        if hh < H - 1:
                            step(ins)
                    need.wait_ge(stepped, step.count)
                    ins.then_inc(psum_free, 1)
                for t in range(NT):
                    need.wait_ge(*J.freed(("go", t)))
                post("gdn", 1, "gdn_norm")
                yb = ycol(1)
                tt(yb, yb, zgate, ALU.mult).then_inc(sem("y_done"), 1)
                phase(e, need, 1)
                take(("nq", 1), nX[:, 2:4, 0:4, :].rearrange("p t h d -> p t (h d)"), src=two)
                take(("kcvc",), kcvcT)
                need.wait_ge(*J.freed(("kcvc",)))
                for half in range(2):
                    i0 = 16 * half
                    src = kcvcT[:, i0:i0 + 16 * NCMP].rearrange("p (n i) -> p i n", i=16)
                    tt(blk[:, i0:i0 + 16, :], src,
                       pe_c[:, i0:i0 + 16].unsqueeze(2).broadcast_to([P, 16, NCMP]), ALU.add)\
                        .then_inc(sem("blocks"), 1)
                for tp in range(2):
                    need.wait_ge(psum_full, J.number(("ksvs", tp)))
                    ps = bank(("ksvs", tp))[:, 0:256].rearrange("p (t n) -> p t n", t=2)
                    step(e.tensor_copy(nX[:, 2 * tp:2 * tp + 2, 4, :], ps[:, :, 0:DH]))
                    e.tensor_copy(nV[:, 2 * tp:2 * tp + 2, 0, :], ps[:, :, DH:P]).then_inc(psum_free, 1)
                step(e.tensor_copy(nX[:, :, 5, :], small[:, :, 0:DH]))
                step(e.tensor_copy(nV[:, :, 1, :], small[:, :, DH:P]))
                c2 = 2.0 * float(np.sqrt(2.0 / np.pi))
                for j in range(2):
                    need.wait_ge(psum_full, J.number(("hid", j)))
                    ps = bank(("hid", j))[:, 0:NCMP]
                    hb, ht = hidb[:, j, 0:NCMP], hidt[:, j, 0:NCMP]
                    e.tensor_copy(hb, ps).then_inc(psum_free, 1)
                    need.wait_ge(*J.freed(("hid", j)))
                    need.wait_ge(stepped, step(tt(ht, hb, hb, ALU.mult)))
                    need.wait_ge(stepped, step(ts(ht, ht, 0.044715 * c2, c2, ALU.mult, ALU.add)))
                    tt(ht, ht, hb, ALU.mult).then_inc(sem("gelu_arg"), 1)
                    need.wait_ge(sem("gelu_exp"), j + 1)
                    need.wait_ge(stepped, step(ts(ht, ht, 1.0, None, ALU.add)))
                    need.wait_ge(stepped, step(e.reciprocal(ht, ht)))
                    tt(hb, hb, ht, ALU.mult).then_inc(sem("cmp_hidden"), 1)
                take(("cmp", 0), ckn[0:NCMP, 0, :], src=lambda ps: ps[0:NCMP, 0:DH])
                take(("cmp", 1), cvn[0:NCMP, :], src=lambda ps: ps[0:NCMP, 0:DH])
                need.wait_ge(*J.freed(("cmp", 0)))
                ck = ckn[0:NCMP, 0, :]
                need.wait_ge(stepped, step(tt(ckn[0:NCMP, 1, :], ck, ck, ALU.mult)))
                rsum(stat("ck_ss", 1)[0:NCMP], ckn[0:NCMP, 1, :], AXX).then_inc(sem("ck_ss"), 1)
                need.wait_ge(sem("ck_rs"), 1)
                need.wait_ge(stepped, step(ts(ck, ck, stat("ck_rs", 1)[0:NCMP], None, ALU.mult)))
                need.wait_ge(stepped, step(tt(ck, ck, rowp("cmp_gain")[0:NCMP], ALU.mult)))
                hd = DH // 2
                cC, sC = cst("cosC")[0:NCMP], cst("sinC")[0:NCMP]
                tA, tB = tmpA[0:NCMP, 0:hd], tmpB[0:NCMP, 0:hd]
                step(tt(tA, ck[:, 0:hd], cC, ALU.mult))
                step(tt(tB, ck[:, hd:DH], sC, ALU.mult))
                need.wait_ge(stepped, step.count)
                for d in range(2):
                    step(tt(ckr[0:NCMP, d, 0:hd], tA, tB, ALU.subtract))
                need.wait_ge(stepped, step.count)
                step(tt(tA, ck[:, hd:DH], cC, ALU.mult))
                step(tt(tB, ck[:, 0:hd], sC, ALU.mult))
                need.wait_ge(stepped, step.count)
                step(tt(ckr[0:NCMP, 0, hd:DH], tA, tB, ALU.add))
                tt(ckr[0:NCMP, 1, hd:DH], tA, tB, ALU.add).then_inc(sem("cmp_k"), 1)
                take(("kcT",), kcT[:, 0:NCMP], src=lambda ps: ps[:, 0:NCMP])
                need.wait_ge(sem("gate_exp"), 1)
                gt = small[:, :, 128:140]
                need.wait_ge(stepped, step(ts(gt, gt, 1.0, None, ALU.add)))
                need.wait_ge(stepped, step(e.reciprocal(gt, gt)))
                g0 = small[:, 0, 128:140].rearrange("p (h b) -> p b h", b=3)[:, 0, :]
                need.wait_ge(stepped, step(ts(g0, g0, cst("valid"), None, ALU.mult)))
                need.wait_ge(*J.freed(("nq", 0)))
                need.wait_ge(*J.freed(("nq", 1)))
                need.wait_ge(*J.freed(("ksvs", 1)))
                need.wait_ge(stepped, step.count)
                nXf = nX.rearrange("p t h d -> p (t h) d")
                nsq = view(14272, 24, DH)
                need.wait_ge(sem("cmp_k"), 1)
                need.wait_ge(stepped, step(tt(nsq, nXf, nXf, ALU.mult)))
                rsum(stat("n_ss", 24), nsq, AXX).then_inc(sem("n_ss"), 1)
                need.wait_ge(sem("n_rs"), 1)
                need.wait_ge(stepped, step(tt(nXf, nXf, stat("n_rs", 24).unsqueeze(2).broadcast_to([P, 24, DH]), ALU.mult)))
                nXt = nX.rearrange("p t h d -> p t (h d)")
                need.wait_ge(stepped, step(tt(nXt, nXt, rowp("nsa_gain").unsqueeze(1).broadcast_to([P, NT, 384]), ALU.mult)))
                tA = view(14272, NT, 6, hd)
                tB = view(15296, NT, 6, hd)
                cA = cst("cosA").rearrange("p (t d) -> p t d", t=NT).unsqueeze(2).broadcast_to([P, NT, 6, hd])
                sA = cst("sinA").rearrange("p (t d) -> p t d", t=NT).unsqueeze(2).broadcast_to([P, NT, 6, hd])
                al = slice(None)
                ins = rope(nX, nY, cA, sA, tA, tB, hd,
                           [((al, al, slice(0, 4)), (al, al, slice(0, 4))),
                            ((al, al, slice(4, 6)), (al, al, slice(4, 8, 2))),
                            ((al, al, slice(4, 6)), (al, al, slice(5, 8, 2)))])
                ins.then_inc(sem("nsa_rope"), 1)
                lam = rowp("lam").rearrange("p (a d) -> p a d", a=4)
                lt = stat("lamt", 64).rearrange("p (a d) -> p a d", a=2)
                need.wait_ge(stepped, step(tt(lt, lam[:, 0:4:2, :], lam[:, 1:4:2, :], ALU.mult)))
                rsum(stat("lamv", 2), lt, AXX).then_inc(sem("lam_dots"), 1)
                need.wait_ge(sem("lam_exp"), 1)
                lw, lv_ = stat("lamw", 2), stat("lamv", 2)
                need.wait_ge(stepped, step(tt(lw[:, 1:2], lv_[:, 1:2], lv_[:, 0:1], ALU.subtract)))
                need.wait_ge(stepped, step(tt(lw[:, 1:2], lw[:, 1:2], rowp("lam_init")[:, 0:1], ALU.subtract)))
                step(ts(lw[:, 0:1], lw[:, 1:2], 0.0, 1.0, ALU.mult, ALU.add))
                for pr in (1, 3):
                    take(("nT", pr), nTr[:, pr, :], mul=0.125 if pr == 1 else None)
                for w in range(3):
                    dst = dV[:, 2:4, :] if w == 2 else dX[:, 2:4, w * GW:(w + 1) * GW]
                    take(("dp", w, 1), dst, src=two)
                for w in range(2):
                    for tp in range(2):
                        need.wait_ge(*J.freed(("dp", w, tp)))
                need.wait_ge(sem("nsa_rope"), 1)
                dXf = dX.rearrange("p t (h d) -> p (t h) d", d=32)
                dsq = dY.rearrange("p t (h d) -> p (t h) d", d=32)
                need.wait_ge(stepped, step(tt(dsq, dXf, dXf, ALU.mult)))
                rsum(stat("d_ss", 64), dsq, AXX).then_inc(sem("d_ss"), 1)
                need.wait_ge(sem("d_rs"), 1)
                need.wait_ge(stepped, step(tt(dXf, dXf, stat("d_rs", 64).unsqueeze(2).broadcast_to([P, 64, 32]), ALU.mult)))
                need.wait_ge(stepped, step(tt(dX, dX, rowp("diff_gain").unsqueeze(1).broadcast_to([P, NT, 512]), ALU.mult)))
                qd = DH // 4
                dX4 = dX.rearrange("p t (h d) -> p t h d", d=32)
                dY4 = dY.rearrange("p t (h d) -> p t h d", d=32)
                tA = view(8128, NT, 16, qd)
                tB = view(9152, NT, 16, qd)
                cD = cst("cosD").rearrange("p (t d) -> p t d", t=NT).unsqueeze(2).broadcast_to([P, NT, 16, qd])
                sD = cst("sinD").rearrange("p (t d) -> p t d", t=NT).unsqueeze(2).broadcast_to([P, NT, 16, qd])
                ins = rope(dX4, dY4, cD, sD, tA, tB, qd, [((al, al, al), (al, al, al))])
                ins.then_inc(sem("diff_rope"), 1)
                for pr in (1, 3):
                    take(("dT", pr), dTr[:, pr, :], mul=float(32 ** -0.5) if pr == 1 else None)
                attention_out(ATT)
                e.drain().then_inc(sem("y_done"), 1)
                need.wait_ge(sem("y_done"), 2)
                post("diff", 3, "diff_norm")
                yd = ycol(3)
                ts(yd, yd, rowp("lam_init")[:, 1:2], None, ALU.mult).then_inc(sem("y_done"), 1)
                phase(e, need, 2)
                take(("mqk", 1), mkT)
                step(e.memset(mV[:, :, :, DH:DH + 1], 1.0))
                for tp in range(2):
                    need.wait_ge(psum_full, J.number(("mv", tp)))
                    ps = bank(("mv", tp)).rearrange("p (t h d) -> p t h d", t=2, h=H)
                    for q in range(2):
                        ins = e.tensor_copy(mV[:, 2 * tp + q, :, 0:DH], ps[:, q])
                        if q == 0:
                            step(ins)
                    ins.then_inc(psum_free, 1)
                mt1 = stat("mt1", 32)
                m1 = mt1.rearrange("p (w t h) -> p w t h", w=2, h=H)
                for w, nm in enumerate(("i_bias", "f_bias")):
                    step(tt(m1[:, w], small[:, :, 148 + 4 * w:152 + 4 * w], rb(nm), ALU.add))
                need.wait_ge(stepped, step.count)
                ts(mt1, mt1, 1.0 / 15.0, None, ALU.mult).then_inc(sem("m_gates"), 1)
                need.wait_ge(sem("m_exp"), 1)
                need.wait_ge(stepped, step(ts(mt1, mt1, 1.0, None, ALU.add)))
                need.wait_ge(stepped, step(e.reciprocal(mt1, mt1)))
                need.wait_ge(stepped, step(ts(mt1, mt1, 30.0, -15.0, ALU.mult, ALU.add)))
                mt2 = stat("mt2", 16)
                e.tensor_copy(mt2, mt1[:, 16:32]).then_inc(sem("m_capped"), 1)
                need.wait_ge(sem("m_exp"), 2)
                ts(mt2, mt2, 1.0, None, ALU.add).then_inc(sem("m_one_plus"), 1)
                need.wait_ge(sem("m_ln"), 1)
                ts(stat("lf", 16), mt2, -1.0, None, ALU.mult).then_inc(sem("m_logf"), 1)
                take(("mF",), stat("F", 16), src=lambda ps: ps[:, 0:16])
                need.wait_ge(*J.freed(("mF",)))
                tt(stat("ma", 16), mt1[:, 0:16], stat("F", 16), ALU.subtract).then_inc(sem("m_a"), 1)
                take(("aT",), aT[0:H, :], src=lambda ps: ps[0:H, :])
                need.wait_ge(*J.freed(("aT",)))
                need.wait_ge(stepped, step(e.tensor_tensor_scan(nMT[0:H, :], aT[0:H, :], aT[0:H, :], 0.0, ALU.max, ALU.max)))
                ts(nMT[0:H, :], nMT[0:H, :], -1.0, None, ALU.mult).then_inc(sem("m_negM"), 1)
                need.wait_ge(*J.freed(("MT",)))
                tt(stat("enm", 16), stat("nM", 16), stat("F", 16), ALU.subtract).then_inc(sem("m_negm"), 1)
                need.wait_ge(*J.freed(("mo", 1)))
                need.wait_ge(stepped, step(ts(mO, mO, 1.0, None, ALU.add)))
                step(e.reciprocal(mO, mO))
                need.wait_ge(sem("m_expm"), 1)
                enm = v3(stat("enm", 16))
                for hh in range(H):
                    need.wait_ge(*J.freed(("mD", hh)))
                    for j in range(NT):
                        need.wait_ge(psum_full, J.number(("mS", hh, j)))
                        ps = bank(("mS", hh, j))
                        w = Em[:, hh % 2, j, j * P:S]
                        tt(w, w, ps[:, j * P:S], ALU.mult).then_inc(psum_free, 1)
                    need.wait_ge(psum_full, J.number(("mO", hh)))
                    ps = bank(("mO", hh))[:, 0:4 * 65].rearrange("p (t n) -> p t n", t=NT)
                    dn = stat("den", 4)
                    need.wait_ge(stepped, step.count)
                    need.wait_ge(stepped, step(ts(dn.unsqueeze(2), ps[:, :, DH:DH + 1], -1.0, None, ALU.mult)))
                    need.wait_ge(stepped, step(tt(dn.unsqueeze(2), dn.unsqueeze(2), ps[:, :, DH:DH + 1], ALU.max)))
                    need.wait_ge(stepped, step(tt(dn, dn, enm[:, :, hh], ALU.max)))
                    need.wait_ge(stepped, step(e.reciprocal(dn, dn)))
                    tt(y[:, :, 2 * GW + hh * DH:2 * GW + (hh + 1) * DH], ps[:, :, 0:DH],
                              dn.unsqueeze(2).broadcast_to([P, NT, DH]), ALU.mult).then_inc(psum_free, 1)
                need.wait_ge(*J.freed(("mO", H - 1)))
                need.wait_ge(psum_full, J.number(("mO", H - 1)))
                post("mlstm", 2, "mlstm_norm")
                yc = ycol(2)
                tt(yc, yc, mO, ALU.mult).then_inc(sem("y_done"), 1)
                phase(e, need, 3)
                for k in range(1, KD, 2):
                    take(("yT", k), hnT[:, k, :])
                for u in range(4):
                    for tp in range(2):
                        hh_ = h_res[:, 2 * tp:2 * tp + 2, u * 256:(u + 1) * 256]
                        need.wait_ge(psum_full, J.number(("wo", u, tp)))
                        ps = bank(("wo", u, tp))
                        tt(hh_, hh_, two(ps), ALU.add).then_inc(psum_free, 1)
                need.wait_ge(sem("mem_rs"), 1)
                for t in range(NMT):
                    ts(memn[:, t, :], memn[:, t, :], stat("mem_rs", 2)[:, t:t + 1], None, ALU.mult)\
                        .then_inc(sem("mem_norm"), 1)
                for k in range(1, KD, 2):
                    take(("memT", k), memT[:, k, :], src=lambda ps: ps[:, 0:MEM],
                         mul=col[:, col_ln("mem") + k:col_ln("mem") + k + 1])
                take(("xk",), xK, src=two)
                need.wait_ge(*J.freed(("wo", 3, 1)))
                for k in (KD - 2, KD - 1):
                    need.wait_ge(*J.freed(("yT", k)))
                scale_norm("xa")
                hT("xa")
                take(("xq", 1), xQ[:, 2:4, :], src=two)
                need.wait_ge(*J.freed(("xk",)))
                need.wait_ge(*J.freed(("xq", 0)))
                need.wait_ge(*J.freed(("xq", 1)))
                need.wait_ge(sem("hn_xa"), 4)
                for nm, X, nt in (("xk", xK, NMT), ("xq", xQ, NT)):
                    n_ = nt * H
                    Xf = X.rearrange("p t (h d) -> p (t h) d", d=DH)
                    sqx = xtmp[:, 0:n_ * DH].rearrange("p (a d) -> p a d", d=DH)
                    need.wait_ge(stepped, step(tt(sqx, Xf, Xf, ALU.mult)))
                    rsum(stat(nm + "_ss", n_), sqx, AXX).then_inc(sem(nm + "_ss"), 1)
                    need.wait_ge(sem(nm + "_rs"), 1)
                    need.wait_ge(stepped, step(tt(Xf, Xf, stat(nm + "_rs", n_).unsqueeze(2).broadcast_to([P, n_, DH]), ALU.mult)))
                    tt(X, X, rowp(nm + "_gain").unsqueeze(1).broadcast_to([P, nt, GW]), ALU.mult)\
                        .then_inc(sem("x_qk"), 1)
                for hp in range(2):
                    take(("xkT", hp), xkT[:, hp, :], src=lambda ps: ps[:, 0:MEM])
                attention_out(XATT)
                take(("xoT", 1), xoT[:, 1, :])
                for t in range(NT):
                    for c in range(2):
                        hh_ = h_res[:, t, c * 512:(c + 1) * 512]
                        need.wait_ge(psum_full, J.number(("xo", t, c)))
                        ps = bank(("xo", t, c))
                        tt(hh_, hh_, ps, ALU.add).then_inc(psum_free, 1)
                need.wait_ge(*J.freed(("xo", 3, 1)))
                scale_norm("moe")
                phase(e, need, 4)
                hT("moe")
                lg = stat("logits", NT * 36).rearrange("p (t n) -> p t n", t=NT)
                for t in range(NT):
                    take(("route", t), lg[:, t, :], src=lambda ps: ps[:, 0:36])
                need.wait_ge(*J.freed(("route", NT - 1)))
                bias = row[:, ROW["b_group"][0]:ROW["b_expert"][1]].unsqueeze(1).broadcast_to([P, NT, 36])
                need.wait_ge(stepped, step(tt(lg, lg, bias, ALU.add)))
                gp = stat("gpad", NT * 8).rearrange("p (t n) -> p t n", t=NT)
                step(e.memset(gp, NEG))
                need.wait_ge(stepped, step.count)
                need.wait_ge(stepped, step(e.tensor_copy(gp[:, :, 0:4], lg[:, :, 0:4])))
                m8 = stat("m8", NT * 8).rearrange("p (t n) -> p t n", t=NT)
                i8 = stat("i8", NT * 8).rearrange("p (t n) -> p t n", t=NT).bitcast(U32)
                for t in range(NT):
                    step(e.max(m8[:, t, :], gp[:, t, :]))
                need.wait_ge(stepped, step.count)
                for t in range(NT):
                    step(e.max_index(i8[:, t, :], m8[:, t, :], gp[:, t, :]))
                need.wait_ge(stepped, step.count)
                rexp = stat("r_exp", 20)
                gi = stat("gidx", NT)
                step(e.tensor_copy(gi.unsqueeze(2), i8[:, :, 0:1]))
                need.wait_ge(stepped, step(tt(rexp[:, 0:16].rearrange("p (t n) -> p t n", t=NT), lg[:, :, 0:4],
                          m8[:, :, 0:1].broadcast_to([P, NT, 4]), ALU.subtract)))
                io = stat("iota8", 8)
                io4 = io[:, 0:4].unsqueeze(1).broadcast_to([P, NT, 4])
                goh = stat("goh", 16).rearrange("p (t n) -> p t n", t=NT)
                need.wait_ge(sem("iota"), 1)
                need.wait_ge(stepped, step(tt(goh, io4, gi.unsqueeze(2).broadcast_to([P, NT, 4]), ALU.is_equal)))
                tmp = stat("etmp", NT * 32).rearrange("p (t n) -> p t n", t=NT)
                for t in range(NT):
                    step(tt(tmp[:, t, :].rearrange("p (g x) -> p g x", g=4),
                              lg[:, t, 4:36].rearrange("p (g x) -> p g x", g=4),
                              goh[:, t, :].unsqueeze(2).broadcast_to([P, 4, 8]), ALU.mult))
                need.wait_ge(stepped, step.count)
                for t in range(NT):
                    step(rsum(gp[:, t, :], tmp[:, t, :].rearrange("p (g x) -> p x g", g=4), AXX))
                need.wait_ge(stepped, step.count)
                for t in range(NT):
                    step(e.max(m8[:, t, :], gp[:, t, :]))
                need.wait_ge(stepped, step.count)
                for t in range(NT):
                    step(e.max_index(i8[:, t, :], m8[:, t, :], gp[:, t, :]))
                need.wait_ge(stepped, step.count)
                tt(rexp[:, 16:20].unsqueeze(2), m8[:, :, 1:2], m8[:, :, 0:1], ALU.subtract).then_inc(sem("route_arg"), 1)
                ei = stat("eidx", 2 * NT).rearrange("p (t n) -> p t n", t=NT)
                need.wait_ge(stepped, step(e.tensor_copy(ei, i8[:, :, 0:2])))
                need.wait_ge(sem("route_exp"), 1)
                gpr = stat("gpr", NT)
                wt = stat("wt", 2 * NT).rearrange("p (t n) -> p t n", t=NT)
                need.wait_ge(stepped, step(rsum(gpr, rexp[:, 0:16].rearrange("p (t n) -> p t n", t=NT), AXX)))
                r1 = stat("r1", NT)
                need.wait_ge(stepped, step(ts(r1, rexp[:, 16:20], 1.0, None, ALU.add)))
                need.wait_ge(stepped, step(tt(r1, r1, gpr, ALU.mult)))
                need.wait_ge(stepped, step(e.reciprocal(r1, r1)))
                step(e.tensor_copy(wt[:, :, 0:1], r1.unsqueeze(2)))
                step(tt(wt[:, :, 1:2], r1.unsqueeze(2), rexp[:, 16:20].unsqueeze(2), ALU.mult))
                need.wait_ge(stepped, step.count)
                one = [stat(f"one{n}", NT * NE) for n in range(2)]
                for n, o8 in enumerate((gp, m8)):
                    step(tt(o8, io.unsqueeze(1).broadcast_to([P, NT, 8]),
                            ei[:, :, n:n + 1].broadcast_to([P, NT, 8]), ALU.is_equal))
                need.wait_ge(stepped, step.count)
                for n, o8 in enumerate((gp, m8)):
                    step(tt(one[n].rearrange("p (t g x) -> p t g x", t=NT, g=E_GROUPS),
                            o8.unsqueeze(2).broadcast_to([P, NT, E_GROUPS, E_PER]),
                            goh.unsqueeze(3).broadcast_to([P, NT, E_GROUPS, E_PER]), ALU.mult))
                need.wait_ge(stepped, step.count)
                tt(stat("chosen", NT * NE), one[0], one[1], ALU.add).then_inc(sem("chosen"), 1)
                need.wait_ge(psum_full, J.number(("rank",)))
                ps = bank(("rank",))
                rank, rint, row_ = stat("rank", NT * NE), stat("rint", NT * NE).bitcast(I32), stat("etmp", NT * NE)
                step(e.tensor_copy(rint, ps[:, 0:NT * NE]))
                mx = stat("mx", 1)
                step(e.tensor_reduce(mx, ps[:, NT * NE:(NT + 1) * NE], AXX, ALU.max))
                ts(rank, ps[:, 0:NT * NE], float(NPAIR), None, ALU.mult).then_inc(psum_free, 1)
                need.wait_ge(stepped, step.count)
                need.wait_ge(stepped, step(ts(rint, rint, 6, 10, ALU.logical_shift_right, ALU.logical_shift_left)))
                need.wait_ge(*J.freed(("rank",)))
                need.wait_ge(stepped, step(tt(row_, rint, rank, ALU.add)))
                need.wait_ge(stepped, step(tt(row_.rearrange("p (t n) -> p t n", t=NT),
                                              row_.rearrange("p (t n) -> p t n", t=NT),
                                              cst("place").unsqueeze(1).broadcast_to([P, NT, NE]), ALU.add)))
                posf = stat("posf", 2 * NT)
                for n in range(2):
                    step(tt(one[n], one[n], row_, ALU.mult))
                c7 = stat("c7", ROUNDS - 1)
                step(ts(c7, cst("c64"), mx, None, ALU.is_lt))
                need.wait_ge(stepped, step.count)
                for n in range(2):
                    step(rsum(posf[:, n * NT:(n + 1) * NT], one[n].rearrange("p (t n) -> p t n", t=NT), AXX))
                step(rsum(stat("nr", 1), c7, AXX))
                need.wait_ge(stepped, step.count)
                e.tensor_copy(pos[:], posf).then_inc(sem("placed"), 1)
                ts(rounds[:], stat("nr", 1), 1.0, None, ALU.add).then_inc(sem("routed"), 1)
                need.wait_ge(sem("routed"), 1)
                nr = e.value_load(rounds[0:1, 0:1], min_val=1, max_val=ROUNDS)
                e.drain().then_inc(sem("rowsT_dve"), 1)
                e.drain().then_inc(sem("moe_gated"), 2)
                e.drain().then_inc(sem("y_dve"), 2)
                with e.Fori(0, nr) as r:
                    with e.Fori(0, NE // QE) as i:
                        for b in range(2):
                            e.wait_ge(sem("moe_T"), 16 * r + 2 * i + b + 3)
                            e.tensor_copy(X2T[:, b, 4:8, :], psum[:, 3, :].rearrange("p (k n) -> p k n", k=4))\
                                .then_inc(sem("rowsT_dve"), 1)
                            for x in range(2):
                                e.wait_ge(sem("moe_silu"), 32 * r + 4 * i + 2 * b + x + 1)
                                tt(aTm[:, x], sgl[:, x],
                                   psum[:, x, 2 * CAP:4 * CAP].rearrange("p (m n) -> p m n", m=2), ALU.mult)\
                                    .then_inc(sem("moe_gated"), 1)
                            e.wait_ge(sem("moe_down"), 32 * r + 4 * i + 2 * b + 2)
                            e.wait_ge(sem("y_out"), 256 * r + 32 * i + 16 * b + 16)
                            e.tensor_copy(Ye[:, 512:1024], psum[:, 5 + 2 * b, :]).then_inc(sem("y_dve"), 1)
                for t in range(NT):
                    need.wait_ge(sem("y_rows_in"), 16 * NT)
                    for n in range(2):
                        if n:
                            need.wait_ge(sem("h_added"), 2 * t + 1)
                        stt(h_res[:, t, :], Yg[:, t, n, :], wt[:, t, n:n + 1], h_res[:, t, :],
                            ALU.mult, ALU.add).then_inc(sem("h_added"), 1)
                layer_end(e, "dve")

        @block.gpsimd
        def _(e):
            need = Waits(e)
            e.iota(stat("iota8", 8), pattern=[[1, 8]], base=0, channel_multiplier=0,
                   allow_small_or_imprecise_dtypes=True).then_inc(sem("iota_once"), 1)
            e.wait_ge(sem("iota_once"), 1)
            tok4 = tok[:].rearrange("p (n t) o -> p n t o", n=2)
            e.iota(tok4[:, :, :, 0], pattern=[[0, 2], [P, NT]], base=0, channel_multiplier=1)                .then_inc(sem("iota_once"), 1)
            e.iota(tok4[:, :, :, 1], pattern=[[1, 2], [2 * P, NT]], base=0, channel_multiplier=2)                .then_inc(sem("iota_once"), 1)
            e.memset(unused[:, :, 0:1], 0).then_inc(sem("iota_once"), 1)
            e.iota(unused[:, :, 1:2], pattern=[[0, NPAIR], [0, 1]], base=2 * S, channel_multiplier=1)                .then_inc(sem("iota_once"), 1)
            e.wait_ge(sem("iota_once"), 5)
            keep = {"const_in", "out_done", "iota_once"}
            with e.Fori(0, L) as l:
                need.new_layer()
                e.drain().then_inc(sem("iota"), 1)
                need.wait_ge(sem("rstd_mix"), 1)
                e.memset(raw[:, :, 0:3], 0.0).then_inc(sem("raw_zero"), 1)
                for r in range(ROUNDS):
                    e.dma_start(table[r * P * NPAIR:(r + 1) * P * NPAIR, :].rearrange("(p i) o -> p i o", p=P),
                                unused[:]).then_inc(sem("table_reset"), 16)
                e.dma_start(y_rows[2 * S:2 * S + P, 0:NPAIR * 2].bitcast(U32),
                            unused[:].rearrange("p i o -> p (i o)")).then_inc(sem("y_out"), 16)
                for n in (1, 2, 3, 4):
                    phase(e, need, n)
                e.wait_ge(sem("table_reset"), 16 * ROUNDS)
                e.wait_ge(sem("placed"), 1)
                for j in range(2 * NT):
                    e.indirect_dma_start(table, bass.IndirectOffsetOnAxis(ap=pos[:, j:j + 1], axis=0),
                                         tok[:, j, :], None).then_inc(sem("table_out"), 16)

                def pick(c, j, o):
                    e.tensor_tensor(idx[:, c:c + 1], ids[:, bass.ds(j, 1), o], unused[:, 0, 0:1], ALU.add)                        .then_inc(sem("picked"), 1)
                    e.wait_ge(sem("picked"), 1)
                    e.sem_clear(sem("picked"))

                def gather(r, j, b):
                    e.wait_ge(sem("moe_T"), 16 * r + j + 1)
                    pick(b, j, 0)
                    e.indirect_dma_start(X2[:, b, :], None, hn_rows,
                                         bass.IndirectOffsetOnAxis(ap=idx[:, b:b + 1], axis=0))                        .then_inc(sem(f"rows_in{b}"), 16)

                def scatter(r, j):
                    e.wait_ge(sem("y_act"), 16 * r + j + 3)
                    e.wait_ge(sem("y_dve"), 16 * r + j + 3)
                    pick(2, j, 1)
                    e.indirect_dma_start(y_rows, bass.IndirectOffsetOnAxis(ap=idx[:, 2:3], axis=0),
                                         Ye, None).then_inc(sem("y_out"), 16)

                e.wait_ge(sem("routed"), 1)
                nr = e.value_load(rounds[0:1, 0:1], min_val=1, max_val=ROUNDS)
                e.wait_ge(sem("table_out"), 16 * 2 * NT)
                e.wait_ge(sem("hn_rows_out"), 16 * NT)
                with e.Fori(0, nr) as r:
                    e.dma_start(ids, table[bass.ds(r * P * NPAIR, P * NPAIR), :].rearrange("(p i) o -> p i o", p=P))                        .then_inc(sem("ids_in"), 16)
                    e.wait_ge(sem("ids_in"), 16 * r + 16)
                    gather(r, 0, 0)
                    with e.Fori(0, NPAIR // 2 - 1) as i:
                        gather(r, 2 * i + 1, 1)
                        scatter(r, 2 * i)
                        gather(r, 2 * i + 2, 0)
                        scatter(r, 2 * i + 1)
                    gather(r, NPAIR - 1, 1)
                    scatter(r, NPAIR - 2)
                    scatter(r, NPAIR - 1)
                e.wait_ge(sem("layer_done"), 4)
                e.dma_reset()
                for name in list(sems):
                    if name not in keep and not name.startswith("layer_go"):
                        e.sem_clear(sems[name])
                for name in ("sp", "pe", "act", "dve"):
                    e.drain().then_inc(sem("layer_go_" + name), 1)
    return nc


_OUT = (1, S, D)


def kernel(**inputs):
    import math

    import concourse.bacc as _bacc
    import ml_dtypes
    from concourse.bass_utils import run_bass_kernel_spmd as _run

    a = {k: np.ascontiguousarray(v) for k, v in inputs.items()}
    f, b = const_tables()
    g = a["nsa_qk_gain"]
    dg, xg = a["diff_qk_gain"], a["xattn_qk_gain"]
    init = np.array([[0.8 - 0.6 * math.exp(-0.3 * l) for _ in range(1)] for l in range(L)], np.float32)
    init = np.concatenate([init, np.array([[1.0 - (0.8 - 0.6 * math.exp(-0.3 * l))] for l in range(L)], np.float32)], 1)
    rows = np.concatenate([
        np.tile(g[:, 0], (1, 4)), g[:, 2], g[:, 3], g[:, 1], np.tile(dg[:, 0], (1, 8)), np.tile(dg[:, 1], (1, 8)),
        np.tile(xg[:, 0], (1, 4)), np.tile(xg[:, 1], (1, 4)), a["gdn_norm"], a["mlstm_norm"], a["diff_norm"],
        a["mlstm_i_bias"], a["mlstm_f_bias"], a["gdn_a_log"], a["gdn_dt_bias"], a["diff_lambda"].reshape(L, -1),
        a["moe_b_group"], a["moe_b_expert"], init], axis=1)
    rows = np.ascontiguousarray(np.broadcast_to(rows[:, None, :], (L, P, NROW)))
    cols = np.concatenate([a[n].reshape(L, P, KD) for n in ("ln_mix", "ln_xattn", "ln_moe", "ln_mem")]
                          + [a["gdn_conv"].reshape(L, 4, 6, P).transpose(0, 3, 2, 1).reshape(L, P, 24)], axis=2)
    arrays = {"x": a["x"], "mem": a["mem"], "rows": rows, "cols": np.ascontiguousarray(cols),
              "const_f": f, "const_b": b.astype(ml_dtypes.bfloat16),
              "pe_t": np.ascontiguousarray(a["nsa_cmp_pe"].transpose(0, 1, 3, 2).reshape(L, P, 32)),
              "ln_moe_rows": np.ascontiguousarray(np.broadcast_to(a["ln_moe"][:, None, :], (L, P, D))),
              "w_route": np.concatenate([a["moe_w_group"], a["moe_w_expert"]], axis=2)}
    for n in ("w_in", "w_out", "nsa_cmp_w1", "nsa_cmp_w2", "xattn_wq", "xattn_wkv", "xattn_wo",
              "moe_w1", "moe_w3", "moe_w2"):
        arrays[n] = a[n]
    nc = _bacc.Bacc("TRN2", target_bir_lowering=False, num_devices=1)
    t_in = {n: nc.dram_tensor(n, v.shape, mybir.dt.from_np(v.dtype), kind="ExternalInput").ap()
            for n, v in arrays.items()}
    out = nc.dram_tensor("out_h", _OUT, F32, kind="ExternalOutput").ap()
    build(nc, t_in, out)
    r = _run(nc, [arrays], core_ids=[0])
    return r.results[0]["out_h"]
```

```python
from contextlib import ExitStack

import numpy as np

import concourse.bass as bass
from concourse import mybir

F32 = mybir.dt.float32
BF16 = mybir.dt.bfloat16
U32 = mybir.dt.uint32
I32 = mybir.dt.int32
ALU = mybir.AluOpType
ACT = mybir.ActivationFunctionType
AXX = mybir.AxisListType.X

P = 128
L = 2
S = 512
NT = S // P
D = 1024
KD = D // P
H = 4
DH = 64
GW = H * DH
MEM = 256
NMT = MEM // P
NCMP = (S - 32) // 16 + 1
EPS = 1e-6
E_GROUPS, E_PER = 4, 8
NE = E_GROUPS * E_PER
FF = D // 4
NEG = -1e30
LEVELS = 7
SLOT = 2048
R = 4
CAP = 64
ROUNDS = S // CAP
NPAIR = NE // 2
QE = 4
NSMALL = 156

C_Q, C_KCVC, C_KSVS, C_KW, C_GQ = 0, 256, 384, 512, 652
C_AB, C_Z, C_MQ, C_MV, C_IF, C_MO, C_DQ, C_DK, C_DV = 1420, 1428, 1684, 1940, 2196, 2204, 2460, 2716, 2972

ROW = {}
_at = 0
for _n, _w in (("nsa_gain", 384), ("cmp_gain", 64), ("diff_gain", 512), ("xq_gain", 256), ("xk_gain", 256), ("gdn_norm", 64),
               ("mlstm_norm", 64), ("diff_norm", 64), ("i_bias", 4), ("f_bias", 4), ("a_log", 4),
               ("dt_bias", 4), ("lam", 128), ("b_group", 4), ("b_expert", 32), ("lam_init", 2)):
    ROW[_n] = (_at, _at + _w)
    _at += _w
NROW = _at
NCOL = 4 * KD + 24

CONST_F = {}
_at = 0
for _n, _w in (("ident", 128), ("triu", 128), ("ones", 128), ("sel4", 512), ("cosA", 128), ("sinA", 128),
               ("cosD", 64), ("sinD", 64), ("cosC", 32), ("sinC", 32), ("valid", 1), ("eps", 1),
               ("striu", 128), ("place", NE), ("c64", ROUNDS - 1)):
    CONST_F[_n] = (_at, _at + _w)
    _at += _w
NCF = _at
CONST_B = {}
_at = 0
for _n, _w in (("identb", 128), ("mask", 128), ("maskT", 128), ("maskC", 4 * 32), ("lvl", LEVELS * 128)):
    CONST_B[_n] = (_at, _at + _w)
    _at += _w
NCB = _at


def const_tables():
    f = np.zeros((P, NCF), np.float32)
    b = np.zeros((P, NCB), np.float32)
    p = np.arange(P)

    def put(a, table, name, v):
        lo, hi = table[name]
        a[:v.shape[0], lo:lo + v.shape[1]] = v
    put(f, CONST_F, "ident", np.eye(P, dtype=np.float32))
    put(f, CONST_F, "triu", (p[:, None] <= p[None, :]).astype(np.float32))
    put(f, CONST_F, "ones", np.ones((P, P), np.float32))
    put(f, CONST_F, "sel4", np.repeat(np.eye(4, dtype=np.float32), P, axis=1))

    def rope(pos, dim):
        inv = (1.0 / (np.float32(10000.0) ** (np.arange(0, dim, 2, dtype=np.float32) / np.float32(dim)))).astype(np.float32)
        ang = pos.astype(np.float32)[:, None] * inv[None, :]
        return np.cos(ang).astype(np.float32), np.sin(ang).astype(np.float32)
    for d, c, s in ((DH, "cosA", "sinA"), (DH // 2, "cosD", "sinD")):
        cos, sin = rope(np.arange(S), d)
        put(f, CONST_F, c, cos.reshape(NT, P, -1).transpose(1, 0, 2).reshape(P, -1))
        put(f, CONST_F, s, sin.reshape(NT, P, -1).transpose(1, 0, 2).reshape(P, -1))
    end = 16 * np.arange(NCMP) + 31
    cos, sin = rope(end, DH)
    put(f, CONST_F, "cosC", cos)
    put(f, CONST_F, "sinC", sin)
    put(f, CONST_F, "valid", (p[:, None] >= 31).astype(np.float32))
    put(f, CONST_F, "eps", np.full((P, 1), EPS, np.float32))
    put(f, CONST_F, "striu", (p[:, None] < p[None, :]).astype(np.float32))
    ex = np.arange(NE)
    put(f, CONST_F, "place", np.tile((ex % 2) * CAP * NPAIR + ex // 2, (P, 1)).astype(np.float32))
    put(f, CONST_F, "c64", np.tile(CAP * np.arange(1, ROUNDS), (P, 1)).astype(np.float32))
    put(b, CONST_B, "identb", np.eye(P))
    put(b, CONST_B, "mask", np.where(p[None, :] > p[:, None], NEG, 0.0))
    put(b, CONST_B, "maskT", np.where(p[None, :] < p[:, None], NEG, 0.0))
    tok = np.arange(S).reshape(NT, P)
    mc = np.zeros((P, 4, 32))
    mc[:, :, :NCMP] = np.where(end[None, None, :] <= tok.T[:, :, None], 0.0, NEG)
    put(b, CONST_B, "maskC", mc.reshape(P, -1))
    lv = np.zeros((P, LEVELS, P))
    for n in range(LEVELS):
        w = 1 << n
        j, i = p[:, None], p[None, :]
        lv[:, n] = (j // (2 * w) == i // (2 * w)) & (j // w % 2 == 0) & (i // w % 2 == 1)
    put(b, CONST_B, "lvl", lv.reshape(P, -1))
    return f, b


def job_list():
    jobs = []

    def add(name, banks, eng):
        jobs.append((name, banks, eng))
    for k in range(KD):
        add(("hT", "mix", k), 1, "AD"[k % 2])
    for c in range(6):
        add(("gp", c), 1, "AD"[c % 2])
    for tp in range(2):
        add(("small", tp), 1, "D")
    for tp in range(2):
        add(("z", tp), 1, "A")
    for w in range(3):
        for tp in range(2):
            add(("gn", w, tp), 1, "AD"[tp])
    add(("nq", 0), 1, "A")
    add(("gc",), 1, "A")
    add(("nq", 1), 1, "A")
    for w in range(4):
        for hp in range(2):
            add(("gT", w, hp), 1, "AD"[hp])
        if w == 1:
            add(("kcvc",), 1, "A")
    for h in range(H):
        add(("gD", h), 1, "A")
        add(("gA", h), 1, "D")
        add(("gQ", h), 1, "D")
    for h in range(H):
        add(("T0", h), 1, "A")
    for n in range(1, LEVELS):
        for h in range(H):
            add(("X", n, h), 1, "A")
        if n == 1:
            for tp in range(2):
                add(("ksvs", tp), 1, "A")
        for h in range(H):
            if n < LEVELS - 1:
                add(("T", n, h), 1, "D")
            add(("U", n, h), 1, "D")
    for hp in range(2):
        add(("wT", hp), 1, "A")
    for t in range(NT):
        add(("vn", t), 1, "A")
        add(("go", t), 1, "A")
        add(("gS", t), 1, "D")
        add(("dp", t // 2, t % 2), 1, "A")
    for tp in range(2):
        add(("dp", 2, tp), 1, "AD"[tp])
    for w in range(2):
        add(("mqk", w), 1, "AD"[w])
    for tp in range(2):
        add(("mv", tp), 1, "D")
    for j in range(2):
        add(("hid", j), 1, "D")
    for pr in range(4):
        add(("nT", pr), 1, "AD"[pr % 2])
    for pr in range(4):
        add(("dT", pr), 1, "AD"[pr % 2])
    add(("hidT",), 1, "D")
    for j in range(2):
        add(("cmp", j), 1, "D")
    for tp in range(2):
        add(("mo", tp), 1, "A")
    add(("kcT",), 1, "D")
    items = attention_items()
    attention_jobs(add, list(enumerate(items)), GATE_STEPS)
    for h in range(H + 1):
        if h < H:
            add(("mB", h), 1, "A")
            add(("mD", h), 1, "A")
            for j in range(NT):
                add(("mS", h, j), 1, "D")
        if h:
            add(("mO", h - 1), 1, "D")
        if h == 1:
            for k in range(KD):
                add(("memT", k), 1, "AD"[k % 2])
        if h == 2:
            for k in YT_EARLY:
                add(("yT", k), 1, "AD"[k % 2])
    add(("xk",), 1, "D")
    add(("xv",), 1, "A")
    for k in YT_LATE:
        add(("yT", k), 1, "AD"[k % 2])
    for u in range(4):
        for tp in range(2):
            add(("wo", u, tp), 1, "D")
    for k in range(KD):
        add(("hT", "xa", k), 1, "AD"[k % 2])
    for tp in range(2):
        add(("xq", tp), 1, "AD"[tp])
    for hp in range(2):
        add(("xqT", hp), 1, "A")
        add(("xkT", hp), 1, "D")
    attention_jobs(add, [(100 + n, it) for n, it in enumerate(cross_items())])
    for hp in range(2):
        add(("xoT", hp), 1, "AD"[hp])
    for t in range(NT):
        for c in range(2):
            add(("xo", t, c), 1, "D")
    for k in range(KD):
        add(("hT", "moe", k), 1, "AD"[k % 2])
    for t in range(NT):
        add(("route", t), 1, "D")
    add(("rank",), 1, "D")
    return jobs


YT_LATE = (4, 5)
YT_EARLY = (0, 1, 2, 3, 6, 7)


def attention_items():
    items = []
    for br in ("cmp", "sel", "win"):
        for t in range(NT):
            for pr in range(2):
                items.append((br, pr, t, NCMP if br == "cmp" else (t + 1) * P))
    for t in range(NT):
        for h in range(H):
            items.append(("diff", h, t, (t + 1) * P))
    return items


def cross_items():
    return [("cross", pr, t, MEM) for t in range(NT) for pr in range(2)]


def staggered(items):
    pad = [None, None]
    return zip(items + pad, [None] + items + [None], pad + items)


GATE_STEPS = {6: ("mF",), 10: ("aT",), 14: ("MT",)}


def attention_jobs(add, items, beside={}):
    for n, (a, b, c) in enumerate(staggered(items)):
        if a:
            add(("S", a[0]), 2, "A")
        if b:
            add(("PT", b[0]), 2, "AD"[b[0] % 2])
        if c:
            add(("O", c[0]), 1, "D")
        if n in beside:
            add(beside[n], 1, "A" if beside[n] == ("MT",) else "D")


class Jobs:

    def __init__(self, full, free):
        self.full, self.free = full, free
        self.info = {}
        owner = [None] * 8
        at = 0
        count = {"A": 0, "D": 0}
        for n, (name, banks, eng) in enumerate(job_list()):
            if banks == 2 and at % 2:
                at = (at + 1) % 8
            before = {owner[at + j] for j in range(banks)} - {None}
            count[eng] += 1
            assert name not in self.info, name
            self.info[name] = (n + 1, at, banks, eng, count[eng], before)
            for j in range(banks):
                owner[at + j] = name
            at = (at + banks) % 8

    def number(self, name):
        return self.info[name][0]

    def freed(self, name):
        _, _, _, eng, c, _ = self.info[name]
        return self.free[eng], c


def build(nc, t_in, out, dbg=None):
    ctx = ExitStack()
    with ctx:
        def sb(name, shape, dt=F32):
            return ctx.enter_context(nc.sbuf_tensor(name, shape, dt))

        sems = {}

        def sem(name):
            if name not in sems:
                sems[name] = ctx.enter_context(nc.semaphore(name))
            return sems[name]

        keep = ["const_in", "x_squared", "out_done", "iota_once"] + [f"x_in{t}" for t in range(NT)]
        keep += ["layer_go_" + n for n in ("sp", "pe", "act", "dve")]
        for name in keep:
            sem(name)
        psum = ctx.enter_context(nc.psum_tensor("psum", [P, 8, 512], F32))
        h_res = sb("h_res", [P, NT, D])
        hnT = sb("hnT", [P, KD, S])
        y = sb("y", [P, NT, D])
        ring = sb("ring", [P, R + 2, SLOT])
        cf = sb("cf", [P, NCF])
        cb = sb("cb", [P, NCB], BF16)
        row = sb("row", [P, NROW])
        col = sb("col", [P, NCOL])
        cw2 = sb("cw2", [P, 2, DH])
        pe_c = sb("pe_c", [P, 32])
        wr = sb("wr", [P, KD, 36])
        small = sb("small", [P, NT, NSMALL])
        st = sb("st", [P, 2100])
        rounds = sb("rounds", [P, 1], I32)
        pos = sb("pos", [P, 2 * NT], U32)
        tok = sb("tok", [P, 2 * NT, 2], U32)
        unused = sb("unused", [P, NPAIR, 2], U32)
        AW = 20000
        arena = sb("arena", [P, AW])

        def cst(name):
            lo, hi = CONST_F[name]
            return cf[:, lo:hi]

        def cbt(name):
            lo, hi = CONST_B[name]
            return cb[:, lo:hi]

        def rowp(name):
            lo, hi = ROW[name]
            return row[:, lo:hi]

        def col_ln(n):
            return {"mix": 0, "xa": 1, "moe": 2, "mem": 3}[n] * KD

        stat_at = {}
        used = [0]

        def stat(name, n):
            if name not in stat_at:
                stat_at[name] = (used[0], n)
                used[0] += n
                assert used[0] <= 2100, used[0]
            lo, k = stat_at[name]
            assert k == n
            return st[:, lo:lo + n]

        def view(off, *dims):
            n = int(np.prod(dims))
            assert off + n <= AW, (off, n)
            v = arena[:, off:off + n]
            if len(dims) == 1:
                return v
            names = "abcd"[:len(dims)]
            return v.rearrange(f"p ({' '.join(names)}) -> p {' '.join(names)}", **dict(zip(names, dims)))

        raw = view(0, 6, 515)
        conv = view(3090, 6, 512)
        gT_, gU, gX = view(0, H, NT, P), view(2048, H, NT, P), view(4096, H, NT, P)
        G0 = 6162
        gnat = view(G0, 4, NT, H, DH)
        gtr = view(G0 + 4096, 4, 2, S)
        AT = view(G0 + 8192, H, NT, P)
        atT = view(G0 + 10240, H, NT, P)
        vnew = view(G0 + 12288, 2, H, DH)
        state = view(G0 + 12800, H, DH)
        assert G0 + 13056 <= AW
        ycol = lambda a: y[:, :, a * GW:(a + 1) * GW]
        zgate = ycol(2)
        dec = ycol(0)
        Bm = ycol(3)
        dec_v = dec.rearrange("p t (b i) -> p b t i", b=2)
        Bm_v = Bm.rearrange("p t (b i) -> p b t i", b=2)
        late = ring[:, R:R + 2, :].rearrange("p a b -> p (a b)")
        nX = late[:, 0:1536].rearrange("p (t h d) -> p t h d", t=NT, h=6)
        nV = late[:, 1536:2048].rearrange("p (t w d) -> p t w d", t=NT, w=2)
        dX = late[:, 2048:4096].rearrange("p (t n) -> p t n", t=NT)
        kcvcT = view(19400, S)
        mqT, mkT = view(0, S), view(512, S)
        mV = view(1024, NT, H, 65)
        mO = view(2064, NT, GW)
        nY = view(3088, NT, 8, DH)
        nTr = view(5136, 4, S)
        blk = view(7184, 32, NCMP)
        ckn = view(8176, 2, DH)
        cvn = view(8304, DH)
        kcT = view(8368, 32)
        hidb = view(8400, 2, 32)
        hid_n, hid_t = view(7184, 2, P), view(7184 + 2 * P, 2, P)
        ckr = view(8528, 2, DH)
        Pm = view(8656, 2, 2, 512)
        PTm = view(10704, 2, 2, 512)
        tmpA, tmpB = view(8656, 1024), view(9680, 1024)
        dY = view(12752, NT, 512)
        dV = view(14800, NT, GW)
        dTr = view(15824, 4, S)
        aT = view(17872, S)
        nMT = view(18384, S)
        Em = [view(3088, NT, S), view(12752, NT, S)]
        memn = late[:, 2048:4096].rearrange("p (t n) -> p t n", t=NMT)
        memT = view(5136, KD, MEM)
        xK = view(15824, NMT, GW)
        xV = view(16336, NMT, GW)
        mtmp = view(8656, 1024)
        ktmp = view(9680, NMT * H, DH)
        xQ = view(16848, NT, GW)
        xqT = view(6144, 2, S)
        xkT = view(7168, 2, MEM)
        xtmp = view(12224, 2048)
        xoT = view(14272, 2, S)
        xO = y[:, :, 0:GW]
        ring2 = view(0, 6, SLOT)
        X2 = view(12288, 2, D)
        X2T = view(14336, 2, KD, P)
        sgl = view(16384, FF)
        am = view(16384 + FF, FF)
        aTm = view(16384 + 2 * FF, 2, P)
        Ye = view(17408, D)
        gmoe = view(18432, D)
        ids = view(19456, NPAIR, 2).bitcast(U32)
        Yg = view(0, NT, 2, D)
        idx = sb("idx", [P, 3], U32)
        table = nc.dram_tensor("table", (ROUNDS * P * NPAIR, 2), U32, kind="Internal").ap()
        hn_rows = nc.dram_tensor("hn_rows", (S, D), F32, kind="Internal").ap()
        y_rows = nc.dram_tensor("y_rows", (2 * S + P, D), F32, kind="Internal").ap()

        def expert_slot(q, n):
            return ring[:, 3 * q + n, :] if q < 2 else ring2[:, 3 * (q - 2) + n, :]

        def each_pair(e, nr, first, pair):
            with e.Fori(0, nr) as r:
                h = NPAIR // 2 * r
                first(h, 0)
                with e.Fori(0, NPAIR // 2 - 1) as i:
                    h = NPAIR // 2 * r + i
                    pair(h, 0, lambda: first(h, 1))
                    pair(h, 1, lambda: first(h + 1, 0))
                h = NPAIR // 2 * r + NPAIR // 2 - 1
                pair(h, 0, lambda: first(h, 1))
                pair(h, 1, lambda: None)

        J = Jobs(sem("psum_full"), {"A": sem("psum_free_act"), "D": sem("psum_free_dve")})
        ATT = [(n, it) for n, it in enumerate(attention_items())]
        XATT = [(100 + n, it) for n, it in enumerate(cross_items())]
        block = ctx.enter_context(nc.Block())

        psum_full = J.full

        def bank(name):
            _, at, banks, _, _, _ = J.info[name]
            return psum[:, at, :] if banks == 1 else psum[:, at:at + 2, :]

        class Waits:

            def __init__(self, e):
                self.e, self.seen = e, {}

            def new_layer(self):
                self.seen = {}

            def wait_ge(self, s, v):
                if self.seen.get(s.name, 0) < v:
                    self.e.wait_ge(s, v)
                    self.seen[s.name] = v

        class Steps:

            def __init__(self, s):
                self.sem, self.count = s, 0

            def __call__(self, ins):
                ins.then_inc(self.sem, 1)
                self.count += 1
                return self.count

        def phase(e, need, n):
            e.drain().then_inc(sem(f"phase{n}"), 1)
            need.wait_ge(sem(f"phase{n}"), 4)

        def layer_end(e, name):
            e.drain().then_inc(sem("layer_done"), 1)
            e.wait_ge(sem("layer_go_" + name), 1)
            e.sem_clear(sem("layer_go_" + name))

        units = ["gq", "gk", "gv", "small", "z", "nq", "kv", "dq", "dk", "dv", "mqk", "mv", "cw1a",
                 "cw1b", "mo", "xkw", "xvw", "wo0", "wo1", "wo2", "wo3", "xqw", "xow", "pad"]
        upos = {u: n for n, u in enumerate(units)}
        assert len(units) % R == 0
        last_job = {"gq": ("gp", 1), "gk": ("gp", 3), "gv": ("gp", 5), "small": ("small", 1), "z": ("z", 1),
                    "nq": ("nq", 1), "kv": ("ksvs", 1), "cw1a": ("hid", 1), "cw1b": ("hid", 1),
                    "dq": ("dp", 0, 1), "dk": ("dp", 1, 1), "dv": ("dp", 2, 1), "mqk": ("mqk", 1),
                    "mv": ("mv", 1), "mo": ("mo", 1), "wo0": ("wo", 0, 1), "wo1": ("wo", 1, 1),
                    "wo2": ("wo", 2, 1), "wo3": ("wo", 3, 1), "xkw": ("xk",), "xvw": ("xv",),
                    "xqw": ("xq", 1), "xow": ("xo", 3, 1)}
        ndma = {u: 1 for u in units}
        ndma.update(kv=1, small=3, cw1a=2, cw1b=2, pad=0)
        landed = {}
        tot = [0] * R
        for n, u in enumerate(units):
            tot[n % R] += 16 * ndma[u]
            landed[u] = tot[n % R]
        slot_base = list(tot)

        def slot(u):
            return ring[:, upos[u] % R, :]

        def weights_in(u):
            return sem(f"weights{upos[u] % R}"), landed[u]

        def operands(it):
            br, pr, t, kl = it
            q = slice(t * P, (t + 1) * P)
            nk = -(-kl // P)
            lo, hi = slice(0, DH), slice(DH, P)
            if br == "cmp":
                return [nTr[s, pr, q] for s in (lo, hi)], [kcT[s, 0:NCMP] for s in (lo, hi)], [[cvn[0:NCMP, :]]] * 2, None
            if br in ("sel", "win"):
                w = ("sel", "win").index(br)
                return ([nTr[s, pr, q] for s in (lo, hi)], [nTr[s, 2 + w, 0:kl] for s in (lo, hi)],
                        [[nV[:, k, w, :] for k in range(nk)]] * 2, None)
            if br == "diff":
                ss = [slice(32 * (2 * (pr % 2) + m), 32 * (2 * (pr % 2) + m) + 32) for m in range(2)]
                return ([dTr[s, pr // 2, q] for s in ss], [dTr[s, 2 + pr // 2, 0:kl] for s in ss],
                        [[dV[:, k, pr * DH:(pr + 1) * DH] for k in range(nk)]] * 2, None)
            return ([xqT[s, pr, q] for s in (lo, hi)], [xkT[s, pr, :] for s in (lo, hi)],
                    [[xV[:, k, (2 * pr + m) * DH:(2 * pr + m + 1) * DH] for k in range(nk)] for m in range(2)], None)

        def item_count(n):
            return n + 1 if n < 100 else len(ATT) + n - 100 + 1

        def prev_item(n):
            seq = [k for k, _ in ATT] + [k for k, _ in XATT]
            return seq[seq.index(n) - 2]

        @block.sync
        def _(e):
            for t in range(NT):
                e.dma_start(h_res[:, t, :], t_in["x"].rearrange("b (t p) d -> t p (b d)", p=P)[t])\
                    .then_inc(sem(f"x_in{t}"), 16)
            e.dma_start(cf[:], t_in["const_f"]).then_inc(sem("const_in"), 16)
            e.dma_start(cb[:], t_in["const_b"]).then_inc(sem("const_in"), 16)
            need = Waits(e)
            with e.Fori(0, L) as l:
                need.new_layer()

                def lay(name, pat, **kw):
                    return t_in[name][bass.ds(l, 1)].rearrange(pat, **kw)
                e.dma_start(row[:], lay("rows", "a p n -> p (a n)")).then_inc(sem("params_in"), 16)
                e.dma_start(col[:], lay("cols", "a p n -> p (a n)")).then_inc(sem("params_in"), 16)
                e.dma_start(cw2[:], lay("nsa_cmp_w2", "a j p n -> p (a j) n")).then_inc(sem("params_in"), 16)
                e.dma_start(pe_c[:], lay("pe_t", "a p n -> p (a n)")).then_inc(sem("params_in"), 16)
                e.dma_start(wr[:], lay("w_route", "a (p k) n -> p (a k) n", p=P)).then_inc(sem("params_in"), 16)
                win = lay("w_in", "a (p k) n -> p (a k) n", p=P)
                wout = lay("w_out", "a (k p) n -> p (a k) n", p=P)
                for n, u in enumerate(units):
                    if u == "pad":
                        continue
                    if u == "xkw":
                        need.wait_ge(sem("diff_rope"), 1)
                        e.dma_start(memn, t_in["mem"].rearrange("b (t p) d -> p (b t) d", p=P))\
                            .then_inc(sem("mem_in"), 16)
                    if n >= R:
                        need.wait_ge(psum_full, J.number(last_job[units[n - R]]))
                    s = sem(f"weights{n % R}")
                    sl = slot(u)
                    s8 = sl.rearrange("p (k n) -> p k n", k=KD)

                    def cols(c0, dst=s8):
                        e.dma_start(dst, win[:, :, c0:c0 + 256]).then_inc(s, 16)
                    if u in ("gq", "gk", "gv"):
                        cols(C_GQ + 256 * ("gq", "gk", "gv").index(u))
                    elif u == "small":
                        sm = sl[:, 0:KD * NSMALL].rearrange("p (k n) -> p k n", k=KD)
                        e.dma_start(sm[:, :, 0:140], win[:, :, C_KW:C_KW + 140]).then_inc(s, 16)
                        e.dma_start(sm[:, :, 140:148], win[:, :, C_AB:C_AB + 8]).then_inc(s, 16)
                        e.dma_start(sm[:, :, 148:156], win[:, :, C_IF:C_IF + 8]).then_inc(s, 16)
                    elif u in ("cw1a", "cw1b"):
                        half = ("cw1a", "cw1b").index(u)
                        for j in range(2):
                            src = t_in["nsa_cmp_w1"][bass.ds(l, 1), j].rearrange("a (l d) m -> d (a l) m", d=DH)
                            e.dma_start(sl[j * DH:(j + 1) * DH, :].rearrange("p (l m) -> p l m", m=P),
                                        src[:, 16 * half:16 * half + 16, :]).then_inc(s, 16)
                    elif u.startswith("wo"):
                        e.dma_start(s8, wout[:, :, int(u[2]) * 256:int(u[2]) * 256 + 256]).then_inc(s, 16)
                    elif u in ("xkw", "xvw"):
                        w = lay("xattn_wkv", "a (p k) n -> p (a k) n", p=P)
                        c0 = 0 if u == "xkw" else 256
                        e.dma_start(s8, w[:, :, c0:c0 + 256]).then_inc(s, 16)
                    elif u == "xqw":
                        e.dma_start(s8, lay("xattn_wq", "a (p k) n -> p (a k) n", p=P)).then_inc(s, 16)
                    elif u == "xow":
                        e.dma_start(sl.rearrange("p (k n) -> p k n", k=2),
                                    lay("xattn_wo", "a (k p) n -> p (a k) n", p=P)).then_inc(s, 16)
                    else:
                        cols({"z": C_Z, "nq": C_Q, "kv": C_KCVC, "mqk": C_MQ, "mv": C_MV, "mo": C_MO,
                              "dq": C_DQ, "dk": C_DK, "dv": C_DV}[u])
                need.wait_ge(sem("phase3"), 4)
                e.dma_start(gmoe, lay("ln_moe_rows", "a p n -> p (a n)")).then_inc(sem("gmoe_in"), 16)
                w1, w3, w2 = (t_in[n][bass.ds(l, 1)] for n in ("moe_w1", "moe_w3", "moe_w2"))

                def load_expert(ex, q, turn=None):
                    if turn is not None:
                        e.wait_ge(sem("moe_down"), QE * turn + q + 1 - QE)
                    e.dma_start(expert_slot(q, 0).rearrange("p (k f) -> p k f", k=KD),
                                w1[:, ex].rearrange("a b (p k) f -> p (a b k) f", p=P)).then_inc(sem(f"w1_in{q}"), 16)
                    if turn is not None:
                        before = 16 * turn + (16 if q else 0)
                        e.wait_ge(sem(f"w3_in{(q - 1) % QE}"), before)
                    e.dma_start(expert_slot(q, 1).rearrange("p (k f) -> p k f", k=KD),
                                w3[:, ex].rearrange("a b (p k) f -> p (a b k) f", p=P)).then_inc(sem(f"w3_in{q}"), 16)
                    if turn is not None:
                        e.wait_ge(sem(f"w2_in{(q - 1) % QE}"), before)
                    e.dma_start(expert_slot(q, 2).rearrange("p (k n) -> p k n", k=2),
                                w2[:, ex].rearrange("a b (k p) n -> p (a b k) n", p=P)).then_inc(sem(f"w2_in{q}"), 16)

                for n, q in enumerate((1, 2, 0, 3)):
                    e.wait_ge(sem("place_free"), n + 1)
                    load_expert(bass.ds(q, 1), q)
                    if n == 1:
                        for t in range(NT):
                            e.wait_ge(sem("hn_moe"), t + 1)
                            e.dma_start(hn_rows[t * P:(t + 1) * P, :], y[:, t, :]).then_inc(sem("hn_rows_out"), 16)
                with e.Fori(0, NE // QE - 1) as i:
                    for q in range(QE):
                        load_expert(bass.ds(QE * i + QE + q, 1), q, i + 1)
                e.wait_ge(sem("routed"), 1)
                nr = e.value_load(rounds[0:1, 0:1], min_val=1, max_val=ROUNDS)
                with e.If(nr > 1):
                    with e.Fori(1, nr) as r:
                        with e.Fori(0, NE // QE) as i:
                            for q in range(QE):
                                load_expert(bass.ds(QE * i + q, 1), q, NE // QE * r + i)
                layer_end(e, "sp")
            e.dma_start(out.rearrange("b (t p) d -> p (b t) d", p=P), h_res[:]).then_inc(sem("out_done"), 16)
            if dbg is not None:
                e.dma_start(dbg["y"], y[:]).then_inc(sem("out_done"), 16)
            e.wait_ge(sem("out_done"), 16 if dbg is None else 32)

        @block.tensor
        def _(e):
            need = Waits(e)

            def begin(name):
                _, at, banks, _, _, before = J.info[name]
                for b in sorted(before, key=str):
                    need.wait_ge(*J.freed(b))
                return psum[:, at, :] if banks == 1 else psum[:, at:at + 2, :]

            def tpose(out_, in_, n=P):
                return e.transpose(out_, in_, cst("ident")[0:n, 0:n])

            def transposed_norm(nm):
                for k in range(KD):
                    o = begin(("hT", nm, k))
                    for t in range(NT):
                        need.wait_ge(sem(f"hn_{nm}"), t + 1)
                        ins = tpose(o[:, t * P:(t + 1) * P], y[:, t, :].rearrange("p (c k) -> p k c", k=KD)[:, k, :])
                    ins.then_inc(psum_full, 1)

            def got_hnT(nm):
                for k in (KD - 2, KD - 1):
                    need.wait_ge(*J.freed(("hT", nm, k)))

            def proj_T(name, u, c0):
                need.wait_ge(*weights_in(u))
                o = begin(name)
                w = slot(u).rearrange("p (k n) -> p k n", k=KD)
                for k in range(KD):
                    ins = e.matmul(o, w[:, k, c0:c0 + P], hnT[:, k, :], start=(k == 0), stop=(k == KD - 1))
                ins.then_inc(psum_full, 1)

            def proj_N(name, u, tp, n, c0=0, lhs=None, nk=KD, width=None):
                need.wait_ge(*weights_in(u))
                o = begin(name)
                w = slot(u)[:, 0:nk * (width or n)].rearrange("p (k n) -> p k n", k=nk)
                src = hnT if lhs is None else lhs
                for q in range(2):
                    t = 2 * tp + q
                    for k in range(nk):
                        ins = e.matmul(o[:, q * n:(q + 1) * n], src[:, k, t * P:(t + 1) * P], w[:, k, c0:c0 + n],
                                       start=(k == 0), stop=(k == nk - 1))
                ins.then_inc(psum_full, 1)

            def attention(items, beside={}):
                def scores(n, it):
                    br, pr, t, kl = it
                    qs, ks, vs, used = operands(it)
                    o = begin(("S", n))
                    for m in range(2):
                        e.matmul(o[:, m, 0:kl], qs[m], ks[m], start=True, stop=False, skip_group_check=True)
                    for m in range(2):
                        if br == "cmp":
                            ins = e.matmul(o[:, m, 0:kl], cbt("identb"), cbt("maskC")[:, t * 32:t * 32 + kl],
                                           start=False, stop=True, skip_group_check=True)
                        else:
                            ins = e.matmul(o[:, m, t * P:kl], cbt("identb"), cbt("mask"),
                                           start=False, stop=True, skip_group_check=True)
                    ins.then_inc(psum_full, 1)

                def scores_x(n, it):
                    br, pr, t, kl = it
                    qs, ks, vs, used = operands(it)
                    o = begin(("S", n))
                    for m in range(2):
                        ins = e.matmul(o[:, m, 0:kl], qs[m], ks[m], start=True, stop=True)
                    ins.then_inc(psum_full, 1)

                def weighted(n, it):
                    br, pr, t, kl = it
                    qs, ks, vs, used = operands(it)
                    nk = -(-kl // P)
                    need.wait_ge(*J.freed(("S", n)))
                    o = begin(("PT", n))
                    for m in range(2):
                        for k in range(nk):
                            w = min(P, kl - k * P)
                            ins = tpose(o[0:w, m, k * P:(k + 1) * P], Pm[:, n % 2, m, k * P:k * P + w])
                    ins.then_inc(psum_full, 1)

                def product(n, it):
                    br, pr, t, kl = it
                    qs, ks, vs, used = operands(it)
                    nk = -(-kl // P)
                    need.wait_ge(*J.freed(("PT", n)))
                    o = begin(("O", n))
                    for m in range(2):
                        for k in range(nk):
                            w = min(P, kl - k * P)
                            ins = e.matmul(o[:, m * DH:(m + 1) * DH], PTm[0:w, n % 2, m, k * P:(k + 1) * P],
                                           vs[m][k], start=(k == 0), stop=(k == nk - 1))
                    ins.then_inc(psum_full, 1)

                for n, (a, b, c) in enumerate(staggered(items)):
                    if a:
                        (scores_x if a[1][0] == "cross" else scores)(*a)
                    if b:
                        weighted(*b)
                    if c:
                        product(*c)
                    if n in beside:
                        beside[n]()

            def gdn():
                for c in range(6):
                    proj_T(("gp", c), ("gq", "gk", "gv")[c // 2], (c % 2) * P)
                for tp in range(2):
                    proj_N(("small", tp), "small", tp, NSMALL)
                for tp in range(2):
                    proj_N(("z", tp), "z", tp, GW)
                for w in range(3):
                    need.wait_ge(sem("g_silu"), 2 * w + 2)
                    for tp in range(2):
                        o = begin(("gn", w, tp))
                        for q in range(2):
                            for c in range(2):
                                ins = tpose(o[:, q * GW + c * P:q * GW + (c + 1) * P],
                                            conv[:, 2 * w + c, (2 * tp + q) * P:(2 * tp + q + 1) * P])
                        ins.then_inc(psum_full, 1)
                proj_N(("nq", 0), "nq", 0, GW)
                need.wait_ge(sem("g_logdecay"), 1)
                o = begin(("gc",))
                g = stat("g", 16)
                e.matmul(o[:, 0:16], cst("triu"), g, start=True, stop=True)
                e.matmul(o[:, 16:32], cst("ones"), g, start=True, stop=True).then_inc(psum_full, 1)
                proj_N(("nq", 1), "nq", 1, GW)
                for w in range(4):
                    need.wait_ge(sem(("g_qk", "g_qk", "g_kbeta", "g_qd")[w]), 1)
                    src = (0, 1, 3, 0)[w]
                    for hp in range(2):
                        o = begin(("gT", w, hp))
                        for t in range(NT):
                            ins = tpose(o[:, t * P:(t + 1) * P],
                                        gnat[:, src, t, 2 * hp:2 * hp + 2, :].rearrange("p a b -> p (a b)"))
                        ins.then_inc(psum_full, 1)
                    if w == 1:
                        proj_T(("kcvc",), "kv", 0)
                for hh in range(H):
                    pp = slice(DH * (hh % 2), DH * (hh % 2) + DH)
                    o = begin(("gD", hh))
                    for t in range(NT):
                        e.matmul(o[:, t * P:(t + 1) * P], g[:, t * H + hh:t * H + hh + 1].broadcast_to([P, P]),
                                 cst("triu"), start=True, stop=False, skip_group_check=True)
                        ins = e.matmul(o[:, t * P:(t + 1) * P], cbt("identb"), cbt("maskT"), start=False, stop=True,
                                       skip_group_check=True)
                    ins.then_inc(psum_full, 1)
                    if hh == 0:
                        for w in range(3):
                            for hp in range(2):
                                need.wait_ge(*J.freed(("gT", w, hp)))
                    for nm, r in (("gA", 2), ("gQ", 0)):
                        o = begin((nm, hh))
                        for t in range(NT):
                            c = slice(t * P, (t + 1) * P)
                            ins = e.matmul(o[:, c], gtr[pp, 1, hh // 2, c], gtr[pp, r, hh // 2, c],
                                           start=True, stop=True)
                        ins.then_inc(psum_full, 1)
                for hh in range(H):
                    need.wait_ge(sem("g_U0"), hh + 1)
                    o = begin(("T0", hh))
                    for t in range(NT):
                        ins = tpose(o[:, t * P:(t + 1) * P], gU[:, hh, t, :])
                    ins.then_inc(psum_full, 1)
                for n in range(1, LEVELS):
                    for hh in range(H):
                        need.wait_ge(sem("g_B"), (n - 1) * H + hh + 1)
                        need.wait_ge(*J.freed(("T0", hh) if n == 1 else ("T", n - 1, hh)))
                        o = begin(("X", n, hh))
                        for t in range(NT):
                            ins = e.matmul(o[:, t * P:(t + 1) * P], Bm_v[:, hh % 2, t, :], gT_[:, hh, t, :],
                                           start=True, stop=True)
                        ins.then_inc(psum_full, 1)
                    if n == 1:
                        for tp in range(2):
                            proj_N(("ksvs", tp), "kv", tp, P, c0=P, width=256)
                    for hh in range(H):
                        need.wait_ge(*J.freed(("X", n, hh)))
                        if n > 1:
                            need.wait_ge(*J.freed(("U", n - 1, hh)))
                        if n < LEVELS - 1:
                            o = begin(("T", n, hh))
                            for t in range(NT):
                                ins = e.matmul(o[:, t * P:(t + 1) * P], gU[:, hh, t, :], gX[:, hh, t, :],
                                               start=True, stop=True)
                            ins.then_inc(psum_full, 1)
                        o = begin(("U", n, hh))
                        for t in range(NT):
                            ins = e.matmul(o[:, t * P:(t + 1) * P], gX[:, hh, t, :], gU[:, hh, t, :],
                                           start=True, stop=True)
                        ins.then_inc(psum_full, 1)
                need.wait_ge(sem("g_kbe"), 1)
                for hh in range(H):
                    need.wait_ge(*J.freed(("U", LEVELS - 1, hh)))
                for hp in range(2):
                    o = begin(("wT", hp))
                    for q in range(2):
                        for t in range(NT):
                            ins = e.matmul(o[q * DH:(q + 1) * DH, t * P:(t + 1) * P], gnat[:, 3, t, 2 * hp + q, :],
                                           gU[:, 2 * hp + q, t, :], start=True, stop=True)
                    ins.then_inc(psum_full, 1)
                need.wait_ge(sem("g_vbeta"), 1)
                need.wait_ge(sem("g_kend"), 1)
                for hp in range(2):
                    need.wait_ge(*J.freed(("wT", hp)))
                    need.wait_ge(*J.freed(("gT", 3, hp)))
                for t in range(NT):
                    c = slice(t * P, (t + 1) * P)
                    if t:
                        need.wait_ge(*J.freed(("gS", t - 1)))
                    o = begin(("vn", t))
                    for hh in range(H):
                        pp = slice(DH * (hh % 2), DH * (hh % 2) + DH)
                        oo = o[:, hh * DH:(hh + 1) * DH]
                        ins = e.matmul(oo, gU[:, hh, t, :], gnat[:, 2, t, hh, :], start=True, stop=(t == 0))
                        if t:
                            ins = e.matmul(oo, gtr[:, 2, hh // 2, c], state[:, hh, :], start=False, stop=True)
                    ins.then_inc(psum_full, 1)
                    need.wait_ge(*J.freed(("vn", t)))
                    o = begin(("go", t))
                    for hh in range(H):
                        pp = slice(DH * (hh % 2), DH * (hh % 2) + DH)
                        oo = o[:, hh * DH:(hh + 1) * DH]
                        ins = e.matmul(oo, atT[:, hh, t, :], vnew[:, t % 2, hh, :], start=True, stop=(t == 0))
                        if t:
                            ins = e.matmul(oo, gtr[:, 3, hh // 2, c], state[:, hh, :], start=False, stop=True)
                    ins.then_inc(psum_full, 1)
                    o = begin(("gS", t))
                    for hh in range(H):
                        q = hh % 2
                        ins = e.matmul(o[q * DH:(q + 1) * DH, (hh // 2) * DH:(hh // 2 + 1) * DH],
                                       gnat[:, 1, t, hh, :], vnew[:, t % 2, hh, :], start=True, stop=True)
                    ins.then_inc(psum_full, 1)
                    proj_N(("dp", t // 2, t % 2), ("dq", "dk")[t // 2], t % 2, GW)

            def nsa_diff():
                for tp in range(2):
                    proj_N(("dp", 2, tp), "dv", tp, GW)
                for w in range(2):
                    proj_T(("mqk", w), "mqk", w * P)
                for tp in range(2):
                    proj_N(("mv", tp), "mv", tp, GW)
                need.wait_ge(sem("phase1"), 4)
                need.wait_ge(*weights_in("cw1a"))
                need.wait_ge(*weights_in("cw1b"))
                need.wait_ge(sem("blocks"), 2)
                hid = [begin(("hid", j)) for j in range(2)]
                for i in range(32):
                    for j in range(2):
                        pp = slice(j * DH, (j + 1) * DH)
                        w = slot("cw1a" if i < 16 else "cw1b").rearrange("p (l m) -> p l m", m=P)[pp, i % 16, :]
                        ins = e.matmul(hid[j][0:NCMP, 0:P], blk[pp, i, :], w, start=(i == 0), stop=(i == 31))
                        if i == 31:
                            ins.then_inc(psum_full, 1)
                need.wait_ge(sem("nsa_rope"), 1)
                for pr in range(4):
                    o = begin(("nT", pr))
                    for t in range(NT):
                        ins = tpose(o[:, t * P:(t + 1) * P], nY[:, t, 2 * pr:2 * pr + 2, :].rearrange("p a b -> p (a b)"))
                    ins.then_inc(psum_full, 1)
                need.wait_ge(sem("diff_rope"), 1)
                for pr in range(4):
                    o = begin(("dT", pr))
                    for t in range(NT):
                        ins = tpose(o[:, t * P:(t + 1) * P], dY[:, t, pr * P:(pr + 1) * P])
                    ins.then_inc(psum_full, 1)
                need.wait_ge(sem("cmp_hidden"), 1)
                o = begin(("hidT",))
                for j in range(2):
                    ins = tpose(o[:, j * 32:j * 32 + NCMP], hid_n[0:NCMP, j, :], NCMP)
                ins.then_inc(psum_full, 1)
                need.wait_ge(*J.freed(("hidT",)))
                for j in range(2):
                    o = begin(("cmp", j))
                    e.matmul(o[0:NCMP, 0:DH], hidb[:, j, 0:NCMP], cw2[:, j, :], start=True, stop=True).then_inc(psum_full, 1)
                for tp in range(2):
                    proj_N(("mo", tp), "mo", tp, GW)
                need.wait_ge(sem("cmp_k"), 1)
                o = begin(("kcT",))
                tpose(o[:, 0:NCMP], ckr[0:NCMP, :, :].rearrange("p a b -> p (a b)"), NCMP).then_inc(psum_full, 1)
                need.wait_ge(*J.freed(("kcT",)))
                need.wait_ge(*J.freed(("cmp", 1)))
                for pr in range(4):
                    need.wait_ge(*J.freed(("nT", pr)))
                    need.wait_ge(*J.freed(("dT", pr)))
                for w in range(3):
                    for tp in range(2):
                        need.wait_ge(*J.freed(("dp", w, tp)))
                attention(ATT, dict(zip(GATE_STEPS, (log_decay_sums, gates_T, maxima_T))))

            def log_decay_sums():
                need.wait_ge(sem("m_logf"), 1)
                lf = stat("lf", 16).rearrange("p (t h) -> p t h", h=H)
                o = begin(("mF",))
                for t in range(NT):
                    for s in range(t + 1):
                        ins = e.matmul(o[:, t * H:(t + 1) * H], cst("triu" if s == t else "ones"), lf[:, s, :],
                                       start=(s == 0), stop=(s == t))
                ins.then_inc(psum_full, 1)

            def gates_T():
                need.wait_ge(sem("m_a"), 1)
                a = stat("ma", 16).rearrange("p (t h) -> p t h", h=H)
                o = begin(("aT",))
                for t in range(NT):
                    ins = tpose(o[0:H, t * P:(t + 1) * P], a[:, t, :])
                ins.then_inc(psum_full, 1)

            def maxima_T():
                need.wait_ge(sem("m_negM"), 1)
                o = begin(("MT",))
                for t in range(NT):
                    ins = tpose(o[:, t * H:(t + 1) * H], nMT[0:H, t * P:(t + 1) * P], H)
                ins.then_inc(psum_full, 1)

            def y_T(ks):
                for k in ks:
                    o = begin(("yT", k))
                    for t in range(NT):
                        ins = tpose(o[:, t * P:(t + 1) * P], y[:, t, k * P:(k + 1) * P])
                    ins.then_inc(psum_full, 1)

            def memory_T():
                need.wait_ge(sem("mem_norm"), 2)
                for k in range(KD):
                    o = begin(("memT", k))
                    for t in range(NMT):
                        ins = tpose(o[:, t * P:(t + 1) * P], memn[:, t, :].rearrange("p (c k) -> p k c", k=KD)[:, k, :])
                    ins.then_inc(psum_full, 1)

            def mlstm():
                for w in range(2):
                    need.wait_ge(*J.freed(("mqk", w)))
                need.wait_ge(*J.freed(("mv", 1)))
                def weights(hh):
                    pp = slice(32 * hh, 32 * hh + 32)
                    sl = cst("sel4")[0:H, hh * P:(hh + 1) * P]
                    o = begin(("mB", hh))
                    e.matmul(o, sl, nMT[0:H, :], start=True, stop=True).then_inc(psum_full, 1)
                    o = begin(("mD", hh))
                    e.matmul(o, sl, nMT[0:H, :], start=True, stop=False, skip_group_check=True)
                    for t in range(NT):
                        ins = e.matmul(o[:, t * P:(t + 1) * P], cbt("identb"), cbt("maskT"), start=False,
                                       stop=(t == NT - 1), skip_group_check=True)
                    ins.then_inc(psum_full, 1)
                    for j in range(NT):
                        o = begin(("mS", hh, j))
                        e.matmul(o[:, j * P:S], mkT[pp, j * P:(j + 1) * P], mqT[pp, j * P:S],
                                      start=True, stop=True).then_inc(psum_full, 1)

                def values(hh):
                    for j in range(NT):
                        need.wait_ge(*J.freed(("mS", hh, j)))
                    o = begin(("mO", hh))
                    for t in range(NT):
                        for j in range(t + 1):
                            ins = e.matmul(o[:, t * 65:(t + 1) * 65], Em[hh % 2][:, j, t * P:(t + 1) * P],
                                           mV[:, j, hh, :], start=(j == 0), stop=(j == t))
                    ins.then_inc(psum_full, 1)

                for hh in range(H + 1):
                    if hh < H:
                        weights(hh)
                    if hh:
                        values(hh - 1)
                    if hh == 1:
                        memory_T()
                    if hh == 2:
                        need.wait_ge(sem("y_done"), 3)
                        y_T(YT_EARLY)
                for k in (KD - 2, KD - 1):
                    need.wait_ge(*J.freed(("memT", k)))
                proj_N(("xk",), "xkw", 0, GW, lhs=memT)
                proj_N(("xv",), "xvw", 0, GW, lhs=memT)

            def out_proj():
                need.wait_ge(sem("y_done"), 4)
                y_T(YT_LATE)
                for k in YT_LATE:
                    need.wait_ge(*J.freed(("yT", k)))
                for u in range(4):
                    for tp in range(2):
                        proj_N(("wo", u, tp), f"wo{u}", tp, 256)
                e.drain().then_inc(sem("place_free"), 2)

            def cross():
                transposed_norm("xa")
                got_hnT("xa")
                for tp in range(2):
                    proj_N(("xq", tp), "xqw", tp, GW)
                need.wait_ge(sem("x_qk"), 2)
                for hp in range(2):
                    o = begin(("xqT", hp))
                    for t in range(NT):
                        ins = tpose(o[:, t * P:(t + 1) * P], xQ[:, t, hp * P:(hp + 1) * P])
                    ins.then_inc(psum_full, 1)
                    o = begin(("xkT", hp))
                    for t in range(NMT):
                        ins = tpose(o[:, t * P:(t + 1) * P], xK[:, t, hp * P:(hp + 1) * P])
                    ins.then_inc(psum_full, 1)
                for hp in range(2):
                    need.wait_ge(*J.freed(("xqT", hp)))
                    need.wait_ge(*J.freed(("xkT", hp)))
                need.wait_ge(*J.freed(("xv",)))
                attention(XATT)
                need.wait_ge(*J.freed(("O", 107)))
                for hp in range(2):
                    o = begin(("xoT", hp))
                    for t in range(NT):
                        ins = tpose(o[:, t * P:(t + 1) * P], xO[:, t, hp * P:(hp + 1) * P])
                    ins.then_inc(psum_full, 1)
                for hp in range(2):
                    need.wait_ge(*J.freed(("xoT", hp)))
                need.wait_ge(*weights_in("xow"))
                w = slot("xow").rearrange("p (k n) -> p k n", k=2)
                for t in range(NT):
                    for c in range(2):
                        o = begin(("xo", t, c))
                        for k in range(2):
                            ins = e.matmul(o, xoT[:, k, t * P:(t + 1) * P], w[:, k, c * 512:(c + 1) * 512],
                                           start=(k == 0), stop=(k == 1))
                        ins.then_inc(psum_full, 1)

            def moe():
                transposed_norm("moe")
                got_hnT("moe")
                for t in range(NT):
                    o = begin(("route", t))
                    for k in range(KD):
                        ins = e.matmul(o[:, 0:36], hnT[:, k, t * P:(t + 1) * P], wr[:, k, :],
                                       start=(k == 0), stop=(k == KD - 1))
                    ins.then_inc(psum_full, 1)
                need.wait_ge(sem("chosen"), 1)
                ch = stat("chosen", NT * NE).rearrange("p (t n) -> p t n", t=NT)
                o = begin(("rank",))
                for t in range(NT):
                    for a in range(t + 1):
                        e.matmul(o[:, t * NE:(t + 1) * NE], cst("striu" if a == t else "ones"), ch[:, a, :],
                                 start=(a == 0), stop=(a == t))
                for a in range(NT):
                    ins = e.matmul(o[:, NT * NE:(NT + 1) * NE], cst("ones"), ch[:, a, :],
                                   start=(a == 0), stop=(a == NT - 1))
                ins.then_inc(psum_full, 1)
                for b in [n for n in J.info if n[0] in ("hT", "xo", "route", "rank")]:
                    need.wait_ge(*J.freed(b))
                need.wait_ge(sem("routed"), 1)
                nr = e.value_load(rounds[0:1, 0:1], min_val=1, max_val=ROUNDS)
                e.drain().then_inc(sem("moe_T"), 2)
                e.drain().then_inc(sem("moe_aT"), 1)

                def rows_T(h, b):
                    e.wait_ge(sem(f"rows_in{b}"), 16 * h + 16)
                    e.wait_ge(sem("rowsT_act"), 2 * h + b + 1)
                    e.wait_ge(sem("rowsT_dve"), 2 * h + b + 1)
                    for k in range(KD):
                        ins = tpose(psum[:, 2 + k // 4, (k % 4) * P:(k % 4 + 1) * P],
                                    X2[:, b, :].rearrange("p (c k) -> p k c", k=KD)[:, k, :])
                    ins.then_inc(sem("moe_T"), 1)

                def pair(h, b, ahead):
                    e.wait_ge(sem("rowsT_act"), 2 * h + b + 2)
                    e.wait_ge(sem("rowsT_dve"), 2 * h + b + 2)
                    e.wait_ge(sem("moe_gated"), 2 * h + b + 1)
                    for x in range(2):
                        q = 2 * b + x
                        area, at = (ring, 3 * q) if q < 2 else (ring2, 3 * (q - 2))
                        w13 = area[:, at:at + 2, :].rearrange("p g (k f) -> p g k f", k=KD)
                        e.wait_ge(sem(f"w1_in{q}"), 16 * h + 16)
                        e.wait_ge(sem(f"w3_in{q}"), 16 * h + 16)
                        for k in range(KD):
                            ins = e.matmul(psum[x * CAP:(x + 1) * CAP, b, :], X2T[:, b, k, x * CAP:(x + 1) * CAP],
                                           w13[:, :, k, :], start=(k == 0), stop=(k == KD - 1))
                    ins.then_inc(sem("moe_up"), 1)
                    ahead()
                    e.wait_ge(sem("moe_gated"), 2 * h + b + 3)
                    e.wait_ge(sem("moe_aT_read"), 2 * h + b + 1)
                    for m in range(2):
                        ins = tpose(psum[:, 6, m * P:(m + 1) * P], am[:, m * P:(m + 1) * P])
                    ins.then_inc(sem("moe_aT"), 1)
                    e.wait_ge(sem("moe_aT_read"), 2 * h + b + 2)
                    e.wait_ge(sem("y_act"), 2 * h + b + 1)
                    e.wait_ge(sem("y_dve"), 2 * h + b + 1)
                    for x in range(2):
                        w2 = expert_slot(2 * b + x, 2).rearrange("p (m n) -> p m n", m=2)
                        e.wait_ge(sem(f"w2_in{2 * b + x}"), 16 * h + 16)
                        for c in range(2):
                            for m in range(2):
                                ins = e.matmul(psum[x * CAP:(x + 1) * CAP, 4 + c, :],
                                               aTm[:, m, x * CAP:(x + 1) * CAP], w2[:, m, c * 512:(c + 1) * 512],
                                               start=(m == 0), stop=(m == 1))
                        ins.then_inc(sem("moe_down"), 1)

                each_pair(e, nr, rows_T, pair)

            e.wait_ge(sem("const_in"), 32)
            with e.Fori(0, L) as l:
                need.new_layer()
                transposed_norm("mix")
                got_hnT("mix")
                gdn()
                e.drain().then_inc(sem("phase1"), 1)
                nsa_diff()
                mlstm()
                phase(e, need, 3)
                out_proj()
                cross()
                phase(e, need, 4)
                e.drain().then_inc(sem("place_free"), 2)
                moe()
                layer_end(e, "pe")

        @block.scalar
        def _(e):
            need = Waits(e)
            stepped = sem("act_stepped")
            step = Steps(stepped)
            psum_free = J.free["A"]
            act = e.activation
            epsc = cst("eps")

            def take(name, dst, scale=None, src=None, func=ACT.Copy):
                need.wait_ge(psum_full, J.number(name))
                ps = bank(name)
                ins = act(dst, ps if src is None else src(ps), func, **({} if scale is None else {"scale": scale}))
                ins.then_inc(psum_free, 1)

            def rsqrt(src, dst, n, signal, scale=None):
                p = src.shape[0]
                tmp = stat("rsq_tmp", 64)[0:p, 0:src.shape[1]]
                need.wait_ge(stepped, step(act(tmp, src, ACT.Ln, scale=1.0 / n, bias=epsc[0:p])))
                act(dst, tmp, ACT.Exp, scale=-0.5).then_inc(sem(signal), 1)

            def norm_stats(nm):
                ss = stat("h_ss", NT)
                for t in range(NT):
                    if nm == "xa":
                        for u in range(4):
                            need.wait_ge(*J.freed(("wo", u, t // 2)))
                    if nm == "moe":
                        for c in range(2):
                            need.wait_ge(*J.freed(("xo", t, c)))
                    need.wait_ge(stepped, step(act(junk, h_res[:, t, :], ACT.Square, accum_out=ss[:, t:t + 1])))
                need.wait_ge(stepped, step.count)
                rsqrt(ss, stat("h_rstd", NT), D, f"rstd_{nm}")

            def hT(nm):
                for k in range(0, KD, 2):
                    take(("hT", nm, k), hnT[:, k, :],
                         scale=None if nm == "moe" else col[:, col_ln(nm) + k:col_ln(nm) + k + 1])

            def exps(items, beside={}):
                def exp(n, it):
                    kl = it[3]
                    need.wait_ge(psum_full, J.number(("S", n)))
                    ps = bank(("S", n))
                    need.wait_ge(sem("neg_max"), item_count(n))
                    if n >= 2:
                        need.wait_ge(psum_full, J.number(("PT", prev_item(n))))
                    for m in range(2):
                        ins = act(Pm[:, n % 2, m, 0:kl], ps[:, m, 0:kl], ACT.Exp,
                                  bias=stat("nmax", 8)[:, 2 * (n % 4) + m:2 * (n % 4) + m + 1],
                                  accum_out=stat("psums", 8)[:, 2 * (n % 4) + m:2 * (n % 4) + m + 1])
                        if m == 0:
                            step(ins)
                    ins.then_inc(psum_free, 1)

                def copy_transposed(n, it):
                    kl = it[3]
                    w = (-(-kl // P)) * P
                    pk = min(P, kl)
                    need.wait_ge(psum_full, J.number(("PT", n)))
                    pt = bank(("PT", n))
                    if n >= 2:
                        need.wait_ge(psum_full, J.number(("O", prev_item(n))))
                    act(PTm[0:pk, n % 2, :, 0:w], pt[0:pk, :, 0:w], ACT.Copy).then_inc(psum_free, 1)

                for n, (a, b, _) in enumerate(staggered(items)):
                    if a:
                        exp(*a)
                    if b and b[0] % 2 == 0:
                        copy_transposed(*b)
                    if n in beside:
                        beside[n]()

            for t in range(NT):
                e.wait_ge(sem(f"x_in{t}"), 16)
                act(view(0, 1024), h_res[:, t, :], ACT.Square, accum_out=stat("h_ss", NT)[:, t:t + 1])\
                    .then_inc(sem("x_squared"), 1)
                e.wait_ge(sem("x_squared"), t + 1)
            e.wait_ge(sem("const_in"), 32)
            with e.Fori(0, L) as l:
                need.new_layer()
                step.count = 0
                need.wait_ge(sem("params_in"), 80)
                rsqrt(stat("h_ss", NT), stat("h_rstd", NT), D, "rstd_mix")
                hT("mix")
                for c in range(0, 6, 2):
                    if c == 0:
                        need.wait_ge(sem("raw_zero"), 1)
                    take(("gp", c), raw[:, c, 3:515])
                for tp in range(2):
                    need.wait_ge(psum_full, J.number(("z", tp)))
                    ps = bank(("z", tp))
                    act(zgate[:, 2 * tp:2 * tp + 2, :], ps.rearrange("p (t n) -> p t n", t=2), ACT.Silu).then_inc(psum_free, 1)
                for c in range(6):
                    need.wait_ge(sem("g_conv"), c + 1)
                    act(conv[:, c, :], conv[:, c, :], ACT.Silu).then_inc(sem("g_silu"), 1)
                for w in range(3):
                    take(("gn", w, 0), gnat[:, w, 0:2].rearrange("p t h d -> p t (h d)"),
                         src=lambda ps: ps.rearrange("p (t n) -> p t n", t=2))
                take(("nq", 0), nX[:, 0:2, 0:4, :].rearrange("p t h d -> p t (h d)"),
                     src=lambda ps: ps.rearrange("p (t n) -> p t n", t=2))
                need.wait_ge(sem("g_gates"), 1)
                t1, t2, t3 = stat("t1", 16), stat("t2", 16), stat("t3", 4)
                act(t1, t1, ACT.Exp, scale=-1.0).then_inc(sem("g_exp"), 1)
                bcol = small[:, :, 144:148]
                act(t2.rearrange("p (t h) -> p t h", h=H), bcol, ACT.Exp, scale=-1.0).then_inc(sem("g_exp"), 1)
                act(t3, rowp("a_log"), ACT.Exp).then_inc(sem("g_exp"), 1)
                need.wait_ge(sem("g_one_plus"), 1)
                act(stat("t4", 16), stat("t4", 16), ACT.Ln).then_inc(sem("g_ln"), 1)
                need.wait_ge(sem("g_ss"), 1)
                rsqrt(stat("g_ss", 32), stat("g_rs", 32), 1.0, "g_rs")
                need.wait_ge(psum_full, J.number(("gc",)))
                ps = bank(("gc",))
                act(stat("gcgl", 32), ps[:, 0:32], ACT.Copy).then_inc(psum_free, 1)
                need.wait_ge(*J.freed(("gc",)))
                act(stat("egcgl", 32), stat("gcgl", 32), ACT.Exp).then_inc(sem("g_egc"), 1)
                need.wait_ge(sem("g_gend"), 1)
                act(stat("gend", 16), stat("gend", 16), ACT.Exp).then_inc(sem("g_egend"), 1)
                take(("nq", 1), nX[:, 2:4, 0:4, :].rearrange("p t h d -> p t (h d)"),
                     src=lambda ps: ps.rearrange("p (t n) -> p t n", t=2))
                for w in range(4):
                    take(("gT", w, 0), gtr[:, w, 0, :])
                    if w == 1:
                        take(("kcvc",), kcvcT)
                for hh in range(H):
                    need.wait_ge(psum_full, J.number(("gD", hh)))
                    ps = bank(("gD", hh))
                    if hh >= 2:
                        need.wait_ge(*J.freed(("gQ", hh - 2)))
                    for t in range(NT):
                        ins = act(dec_v[:, hh % 2, t, :], ps[:, t * P:(t + 1) * P], ACT.Exp,
                                  bias=stat("ngc", 16)[:, t * H + hh:t * H + hh + 1])
                    ins.then_inc(psum_free, 1)
                for hh in range(H):
                    take(("T0", hh), gT_[:, hh].rearrange("p t n -> p (t n)"))
                for n in range(1, LEVELS):
                    for hh in range(H):
                        if n > 1:
                            need.wait_ge(psum_full, J.number(("U", n - 1, hh)))
                        take(("X", n, hh), gX[:, hh].rearrange("p t n -> p (t n)"))
                    if n == 1:
                        for tp in range(2):
                            need.wait_ge(psum_full, J.number(("ksvs", tp)))
                            ps = bank(("ksvs", tp))[:, 0:256].rearrange("p (t n) -> p t n", t=2)
                            step(act(nX[:, 2 * tp:2 * tp + 2, 4, :], ps[:, :, 0:DH], ACT.Copy))
                            act(nV[:, 2 * tp:2 * tp + 2, 0, :], ps[:, :, DH:P], ACT.Copy).then_inc(psum_free, 1)
                for hp in range(2):
                    need.wait_ge(psum_full, J.number(("gQ", H - 1)))
                    take(("wT", hp), gtr[:, 2, hp, :], scale=-1.0)
                for t in range(NT):
                    if t >= 2:
                        need.wait_ge(psum_full, J.number(("gS", t - 2)))
                    take(("vn", t), vnew[:, t % 2].rearrange("p h d -> p (h d)"), src=lambda ps: ps[:, 0:GW])
                    take(("go", t), y[:, t, GW:2 * GW], src=lambda ps: ps[:, 0:GW])
                    w, tp = t // 2, t % 2
                    take(("dp", w, tp), dX[:, 2 * tp:2 * tp + 2, w * GW:(w + 1) * GW],
                         src=lambda ps: ps.rearrange("p (t n) -> p t n", t=2))
                need.wait_ge(sem("post_ss_gdn"), 1)
                rsqrt(stat("post_ss", 16), stat("post_rs", 16), DH, "post_rs_gdn")
                phase(e, need, 1)
                take(("dp", 2, 0), dV[:, 0:2, :], src=lambda ps: ps.rearrange("p (t n) -> p t n", t=2))
                take(("mqk", 0), mqT[:, :], scale=float(32 ** -0.5))
                act(small[:, :, 128:140], small[:, :, 128:140], ACT.Exp, scale=-1.0).then_inc(sem("gate_exp"), 1)
                need.wait_ge(sem("n_ss"), 1)
                rsqrt(stat("n_ss", 24), stat("n_rs", 24), DH, "n_rs")
                need.wait_ge(sem("lam_dots"), 1)
                act(stat("lamv", 2), stat("lamv", 2), ACT.Exp).then_inc(sem("lam_exp"), 1)
                need.wait_ge(sem("d_ss"), 1)
                rsqrt(stat("d_ss", 64), stat("d_rs", 64), DH // 2, "d_rs")
                need.wait_ge(sem("gelu_arg"), 1)
                act(hid_t[0:NCMP], hid_t[0:NCMP], ACT.Exp, scale=-1.0).then_inc(sem("gelu_exp"), 1)
                for pr in (0, 2):
                    take(("nT", pr), nTr[:, pr, :], scale=0.125 if pr == 0 else None)
                for pr in (0, 2):
                    take(("dT", pr), dTr[:, pr, :], scale=float(32 ** -0.5) if pr == 0 else None)
                need.wait_ge(sem("ck_ss"), 1)
                rsqrt(stat("ck_ss", 1)[0:NCMP], stat("ck_rs", 1)[0:NCMP], DH, "ck_rs")
                need.wait_ge(sem("m_gates"), 1)
                mt1 = stat("mt1", 32)
                act(mt1, mt1, ACT.Exp, scale=-2.0).then_inc(sem("m_exp"), 1)
                need.wait_ge(sem("m_capped"), 1)
                mt2 = stat("mt2", 16)
                act(mt2, mt2, ACT.Exp, scale=-1.0).then_inc(sem("m_exp"), 1)
                need.wait_ge(sem("m_one_plus"), 1)
                act(mt2, mt2, ACT.Ln).then_inc(sem("m_ln"), 1)
                for tp in range(2):
                    need.wait_ge(psum_full, J.number(("mo", tp)))
                    ps = bank(("mo", tp))
                    act(mO[:, 2 * tp:2 * tp + 2, :], ps.rearrange("p (t n) -> p t n", t=2), ACT.Exp,
                               scale=-1.0).then_inc(psum_free, 1)
                def maxima():
                    take(("MT",), stat("nM", 16), src=lambda ps: ps[:, 0:16])

                def exp_maxima():
                    need.wait_ge(sem("m_negm"), 1)
                    act(stat("enm", 16), stat("enm", 16), ACT.Exp).then_inc(sem("m_expm"), 1)

                exps(ATT, {14: maxima, 18: exp_maxima})
                need.wait_ge(sem("post_ss_diff"), 1)
                rsqrt(stat("post_ss", 16), stat("post_rs", 16), DH, "post_rs_diff")
                need.wait_ge(sem("mem_in"), 16)
                need.wait_ge(psum_full, J.number(("O", len(ATT) - 1)))
                for t in range(NMT):
                    need.wait_ge(stepped, step(act(mtmp, memn[:, t, :], ACT.Square, accum_out=stat("mem_ss", 2)[:, t:t + 1])))
                need.wait_ge(stepped, step.count)
                rsqrt(stat("mem_ss", 2), stat("mem_rs", 2), D, "mem_rs")
                a = stat("ma", 16)
                for hh in range(H):
                    if hh >= 2:
                        need.wait_ge(psum_full, J.number(("mO", hh - 2)))
                    need.wait_ge(psum_full, J.number(("mB", hh)))
                    ps = bank(("mB", hh))
                    for j in range(NT - 1):
                        ins = act(Em[hh % 2][:, j, (j + 1) * P:S], ps[:, (j + 1) * P:S], ACT.Exp,
                                  bias=a[:, j * H + hh:j * H + hh + 1])
                    ins.then_inc(psum_free, 1)
                    need.wait_ge(psum_full, J.number(("mD", hh)))
                    ps = bank(("mD", hh))
                    for j in range(NT):
                        ins = act(Em[hh % 2][:, j, j * P:(j + 1) * P], ps[:, j * P:(j + 1) * P], ACT.Exp,
                                  bias=a[:, j * H + hh:j * H + hh + 1])
                    ins.then_inc(psum_free, 1)
                    if hh == 1:
                        for k in range(0, KD, 2):
                            take(("memT", k), memT[:, k, :], scale=col[:, col_ln("mem") + k:col_ln("mem") + k + 1],
                                 src=lambda ps: ps[:, 0:MEM])
                    if hh == 2:
                        for k in YT_EARLY[0::2]:
                            take(("yT", k), hnT[:, k, :])
                take(("xv",), xV, src=lambda ps: ps.rearrange("p (t n) -> p t n", t=2))
                need.wait_ge(sem("post_ss_mlstm"), 1)
                rsqrt(stat("post_ss", 16), stat("post_rs", 16), DH, "post_rs_mlstm")
                need.wait_ge(sem("xk_ss"), 1)
                rsqrt(stat("xk_ss", 8), stat("xk_rs", 8), DH, "xk_rs")
                phase(e, need, 3)
                take(("yT", 4), hnT[:, 4, :])
                junk = xtmp[:, 0:1024]
                norm_stats("xa")
                hT("xa")
                take(("xq", 0), xQ[:, 0:2, :], src=lambda ps: ps.rearrange("p (t n) -> p t n", t=2))
                need.wait_ge(sem("xq_ss"), 1)
                rsqrt(stat("xq_ss", 16), stat("xq_rs", 16), DH, "xq_rs")
                for hp in range(2):
                    take(("xqT", hp), xqT[:, hp, :], scale=0.125)
                exps(XATT)
                take(("xoT", 0), xoT[:, 0, :])
                norm_stats("moe")
                phase(e, need, 4)
                hT("moe")
                need.wait_ge(sem("route_arg"), 1)
                act(stat("r_exp", 20), stat("r_exp", 20), ACT.Exp).then_inc(sem("route_exp"), 1)
                need.wait_ge(sem("routed"), 1)
                nr = e.value_load(rounds[0:1, 0:1], min_val=1, max_val=ROUNDS)
                e.drain().then_inc(sem("rowsT_act"), 1)
                e.drain().then_inc(sem("moe_aT_read"), 1)
                e.drain().then_inc(sem("y_act"), 1)

                def rows_T(h, b):
                    e.wait_ge(sem("moe_T"), 2 * h + b + 3)
                    act(X2T[:, b, 0:4, :], psum[:, 2, :], ACT.Copy).then_inc(sem("rowsT_act"), 1)

                def pair(h, b, ahead):
                    e.wait_ge(sem("moe_up"), 2 * h + b + 1)
                    e.wait_ge(sem("moe_gated"), 2 * h + b + 2)
                    act(sgl, psum[:, b, 0:FF], ACT.Silu).then_inc(sem("moe_silu"), 1)
                    ahead()
                    e.wait_ge(sem("moe_aT"), 2 * h + b + 2)
                    act(aTm, psum[:, 6, 0:2 * P], ACT.Copy).then_inc(sem("moe_aT_read"), 1)
                    e.wait_ge(sem("moe_down"), 4 * h + 2 * b + 2)
                    e.wait_ge(sem("y_out"), 32 * h + 16 * b + 16)
                    act(Ye[:, 0:512], psum[:, 4, :], ACT.Copy).then_inc(sem("y_act"), 1)

                each_pair(e, nr, rows_T, pair)
                e.wait_ge(sem("y_out"), 256 * nr + 16)
                for t in range(NT):
                    e.dma_start(Yg[:, t], y_rows[2 * P * t:2 * P * (t + 1), :].rearrange("(p n) d -> p n d", n=2))\
                        .then_inc(sem(f"y_rows_in{t}"), 16)
                for t in range(NT):
                    need.wait_ge(sem("h_added"), 2 * t + 2)
                    need.wait_ge(stepped, step(act(view(14336, 1024), h_res[:, t, :], ACT.Square,
                                                   accum_out=stat("h_ss", NT)[:, t:t + 1])))
                layer_end(e, "act")

        @block.vector
        def _(e):
            need = Waits(e)
            stepped = sem("dve_stepped")
            step = Steps(stepped)
            psum_free = J.free["D"]
            tt, ts, stt = e.tensor_tensor, e.tensor_scalar, e.scalar_tensor_tensor
            rsum = e.reduce_sum

            def take(name, dst, src=None, mul=None):
                need.wait_ge(psum_full, J.number(name))
                ps = bank(name)
                ps = ps if src is None else src(ps)
                ins = e.tensor_copy(dst, ps) if mul is None else ts(dst, ps, mul, None, ALU.mult)
                ins.then_inc(psum_free, 1)

            two = lambda ps: ps.rearrange("p (t n) -> p t n", t=2)

            def scale_norm(nm):
                need.wait_ge(sem(f"rstd_{nm}"), 1)
                for t in range(NT):
                    rstd = stat("h_rstd", NT)[:, t:t + 1]
                    if nm == "moe":
                        need.wait_ge(sem("gmoe_in"), 16)
                        ins = stt(y[:, t, :], h_res[:, t, :], rstd, gmoe, ALU.mult, ALU.mult)
                    else:
                        ins = ts(y[:, t, :], h_res[:, t, :], rstd, None, ALU.mult)
                    ins.then_inc(sem(f"hn_{nm}"), 1)

            def hT(nm):
                for k in range(1, KD, 2):
                    take(("hT", nm, k), hnT[:, k, :],
                         mul=None if nm == "moe" else col[:, col_ln(nm) + k:col_ln(nm) + k + 1])

            def rope(X, Y, cos, sin, tA, tB, half, outs):
                x1, x2 = X[..., 0:half], X[..., half:2 * half]
                step(tt(tA, x1, cos, ALU.mult))
                step(tt(tB, x2, sin, ALU.mult))
                need.wait_ge(stepped, step.count)
                for a, b in outs:
                    step(tt(Y[b + (slice(0, half),)], tA[a], tB[a], ALU.subtract))
                need.wait_ge(stepped, step.count)
                step(tt(tA, x2, cos, ALU.mult))
                step(tt(tB, x1, sin, ALU.mult))
                need.wait_ge(stepped, step.count)
                for a, b in outs:
                    ins = tt(Y[b + (slice(half, 2 * half),)], tA[a], tB[a], ALU.add)
                    if (a, b) != outs[-1]:
                        step(ins)
                need.wait_ge(stepped, step.count)
                return ins

            def attention_out(items, beside={}):
                def largest(n, it):
                    need.wait_ge(psum_full, J.number(("S", n)))
                    ps = bank(("S", n))
                    k4 = 2 * (n % 4)
                    e.tensor_reduce(stat("nmax", 8)[:, k4:k4 + 2], ps[:, :, 0:it[3]], AXX, ALU.max, negate=True)\
                        .then_inc(sem("neg_max"), 1)

                def copy_transposed(n, it):
                    kl = it[3]
                    w = (-(-kl // P)) * P
                    pk = min(P, kl)
                    need.wait_ge(psum_full, J.number(("PT", n)))
                    pt = bank(("PT", n))
                    if n >= 2:
                        need.wait_ge(psum_full, J.number(("O", prev_item(n))))
                    e.tensor_copy(PTm[0:pk, n % 2, :, 0:w], pt[0:pk, :, 0:w]).then_inc(psum_free, 1)

                def finish(n, it):
                    br, pr, t, kl = it
                    k4 = 2 * (n % 4)
                    need.wait_ge(*J.freed(("S", n)))
                    rs = stat("rsum", 8)[:, k4:k4 + 2]
                    need.wait_ge(stepped, step(e.reciprocal(rs, stat("psums", 8)[:, k4:k4 + 2])))
                    if br in ("cmp", "sel", "win"):
                        b = ("cmp", "sel", "win").index(br)
                        g = small[:, t, 128:140].rearrange("p (h b) -> p b h", b=3)[:, b, 2 * pr:2 * pr + 2]
                        need.wait_ge(stepped, step(tt(rs, rs, g, ALU.mult)))
                    if br == "diff":
                        need.wait_ge(stepped, step(tt(rs, rs, stat("lamw", 2), ALU.mult)))
                    need.wait_ge(psum_full, J.number(("O", n)))
                    ps = bank(("O", n))
                    if br == "diff":
                        o = y[:, t, 3 * GW + pr * DH:3 * GW + (pr + 1) * DH]
                        need.wait_ge(stepped, step(ts(o, ps[:, 0:DH], rs[:, 0:1], None, ALU.mult)))
                        stt(o, ps[:, DH:2 * DH], rs[:, 1:2], o, ALU.mult, ALU.add).then_inc(psum_free, 1)
                        return
                    for m in range(2):
                        o = (xO if br == "cross" else y)[:, t, (2 * pr + m) * DH:(2 * pr + m + 1) * DH]
                        src = ps[:, m * DH:(m + 1) * DH]
                        if br in ("cmp", "cross"):
                            ins = ts(o, src, rs[:, m:m + 1], None, ALU.mult)
                        else:
                            if m == 0:
                                need.wait_ge(*J.freed(("O", n - 8)))
                            ins = stt(o, src, rs[:, m:m + 1], o, ALU.mult, ALU.add)
                        if m == 0:
                            step(ins)
                    ins.then_inc(psum_free, 1)

                for n, (a, b, c) in enumerate(staggered(items)):
                    if a:
                        largest(*a)
                    if b and b[0] % 2:
                        copy_transposed(*b)
                    if c:
                        finish(*c)
                    if n in beside:
                        beside[n]()

            def head_norm(nm, X, nt, sq):
                n_ = nt * H
                Xf = X.rearrange("p t (h d) -> p (t h) d", d=DH)
                need.wait_ge(stepped, step(tt(sq, Xf, Xf, ALU.mult)))
                rsum(stat(nm + "_ss", n_), sq, AXX).then_inc(sem(nm + "_ss"), 1)
                need.wait_ge(sem(nm + "_rs"), 1)
                need.wait_ge(stepped, step(tt(Xf, Xf, stat(nm + "_rs", n_).unsqueeze(2).broadcast_to([P, n_, DH]), ALU.mult)))
                tt(X, X, rowp(nm + "_gain").unsqueeze(1).broadcast_to([P, nt, GW]), ALU.mult)\
                    .then_inc(sem("x_qk"), 1)

            def post(nm, g, gain):
                yg = y[:, :, g * GW:(g + 1) * GW].rearrange("p t (h d) -> p t h d", h=H)
                tmp = view({"gdn": 0, "diff": 7184, "mlstm": 3088}[nm], NT, H, DH)
                need.wait_ge(stepped, step.count)
                need.wait_ge(stepped, step(tt(tmp, yg, yg, ALU.mult)))
                rsum(stat("post_ss", 16).rearrange("p (t h) -> p t h", h=H), tmp, AXX)\
                    .then_inc(sem("post_ss_" + nm), 1)
                need.wait_ge(sem("post_rs_" + nm), 1)
                rs = stat("post_rs", 16).rearrange("p (t h) -> p t h", h=H)
                need.wait_ge(stepped, step(tt(yg, yg, rs.unsqueeze(3).broadcast_to([P, NT, H, DH]), ALU.mult)))
                gn = rowp(gain).unsqueeze(1).broadcast_to([P, NT * H, DH])
                ygf = y[:, :, g * GW:(g + 1) * GW].rearrange("p t (h d) -> p t h d", h=H)
                need.wait_ge(stepped, step(tt(ygf, ygf, rowp(gain).unsqueeze(1).unsqueeze(1).broadcast_to([P, NT, H, DH]), ALU.mult)))

            e.wait_ge(sem("const_in"), 32)
            for t in range(NT):
                e.wait_ge(sem(f"x_in{t}"), 16)
            with e.Fori(0, L) as l:
                need.new_layer()
                step.count = 0
                need.wait_ge(sem("params_in"), 80)
                scale_norm("mix")
                hT("mix")
                for c in range(1, 6, 2):
                    if c == 1:
                        need.wait_ge(sem("raw_zero"), 1)
                    take(("gp", c), raw[:, c, 3:515])
                for tp in range(2):
                    take(("small", tp), small[:, 2 * tp:2 * tp + 2, :],
                         src=lambda ps: ps[:, 0:2 * NSMALL].rearrange("p (t n) -> p t n", t=2))
                taps = col[:, 4 * KD:4 * KD + 24].rearrange("p (c j) -> p c j", j=4)
                for c in range(6):
                    need.wait_ge(*J.freed(("gp", c)))
                for c in range(0, 6, 2):
                    for j in range(4):
                        for cc in (c, c + 1):
                            src = raw[:, cc, j:j + 512]
                            if j == 0:
                                ins = ts(conv[:, cc, :], src, taps[:, cc, 0:1], None, ALU.mult)
                            else:
                                ins = stt(conv[:, cc, :], src, taps[:, cc, j:j + 1], conv[:, cc, :], ALU.mult, ALU.add)
                            if j < 3:
                                step(ins)
                            else:
                                ins.then_inc(sem("g_conv"), 1)
                        need.wait_ge(stepped, step.count)
                need.wait_ge(*J.freed(("small", 1)))
                t1, t2, t3, t4, t5 = stat("t1", 16), stat("t2", 16), stat("t3", 4), stat("t4", 16), stat("t5", 16)
                v3 = lambda s: s.rearrange("p (t h) -> p t h", h=H)
                rb = lambda n: rowp(n).unsqueeze(1).broadcast_to([P, NT, H])
                need.wait_ge(stepped, step(tt(v3(t5), small[:, :, 140:144], rb("dt_bias"), ALU.add)))
                step(ts(t4, t5, -1.0, None, ALU.mult))
                need.wait_ge(stepped, step.count)
                tt(t1, t5, t4, ALU.max).then_inc(sem("g_gates"), 1)
                need.wait_ge(sem("g_gates"), 1)
                need.wait_ge(sem("g_exp"), 3)
                step(ts(t5, t5, 0.0, None, ALU.max))
                need.wait_ge(stepped, step.count)
                ts(t4, t1, 1.0, None, ALU.add).then_inc(sem("g_one_plus"), 1)
                beta = stat("beta", 16)
                need.wait_ge(stepped, step(ts(t2, t2, 1.0, None, ALU.add)))
                need.wait_ge(stepped, step(e.reciprocal(beta, t2)))
                need.wait_ge(sem("g_ln"), 1)
                need.wait_ge(stepped, step(tt(t5, t5, t4, ALU.add)))
                need.wait_ge(stepped, step(ts(t3, t3, -1.0, None, ALU.mult)))
                g = stat("g", 16)
                tt(v3(g), v3(t5), t3.unsqueeze(1).broadcast_to([P, NT, H]), ALU.mult).then_inc(sem("g_logdecay"), 1)
                for w in range(3):
                    take(("gn", w, 1), gnat[:, w, 2:4].rearrange("p t h d -> p t (h d)"), src=two)
                for w in range(3):
                    need.wait_ge(*J.freed(("gn", w, 0)))
                    need.wait_ge(*J.freed(("gn", w, 1)))
                sq = view(0, 2 * NT * H, DH)
                gf = gnat[:, 0:2].rearrange("p w t h d -> p (w t h) d")
                need.wait_ge(sem("g_silu"), 6)
                need.wait_ge(stepped, step(tt(sq, gf, gf, ALU.mult)))
                rsum(stat("g_ss", 32), sq, AXX).then_inc(sem("g_ss"), 1)
                need.wait_ge(sem("g_rs"), 1)
                rs = stat("g_rs", 32)
                need.wait_ge(stepped, step(ts(rs[:, 0:16], rs[:, 0:16], DH ** -0.5, None, ALU.mult)))
                tt(gf, gf, rs.unsqueeze(2).broadcast_to([P, 32, DH]), ALU.mult).then_inc(sem("g_qk"), 1)
                need.wait_ge(sem("g_qk"), 1)

                def heads(w):
                    return gnat[:, w].rearrange("p t h d -> p (t h) d")

                def per(s):
                    return s.unsqueeze(2).broadcast_to([P, 16, DH])
                tt(heads(3), heads(1), per(beta), ALU.mult).then_inc(sem("g_kbeta"), 1)
                tt(heads(2), heads(2), per(beta), ALU.mult).then_inc(sem("g_vbeta"), 1)
                need.wait_ge(*J.freed(("gc",)))
                gcgl = stat("gcgl", 32)
                tt(stat("gend", 16), gcgl[:, 16:32], gcgl[:, 0:16], ALU.subtract).then_inc(sem("g_gend"), 1)
                step(ts(stat("ngc", 16), gcgl[:, 0:16], -1.0, None, ALU.mult))
                need.wait_ge(stepped, step.count)
                e.sem_inc(sem("g_ngc"), 1)
                need.wait_ge(sem("g_egc"), 1)
                take(("gT", 0, 1), gtr[:, 0, 1, :])
                tt(heads(0), heads(0), per(stat("egcgl", 32)[:, 0:16]), ALU.mult).then_inc(sem("g_qd"), 1)
                take(("gT", 1, 1), gtr[:, 1, 1, :])
                need.wait_ge(sem("g_egend"), 1)
                tt(heads(1), heads(1), per(stat("gend", 16)), ALU.mult).then_inc(sem("g_kend"), 1)
                take(("gT", 2, 1), gtr[:, 2, 1, :])
                tt(heads(3), heads(3), per(stat("egcgl", 32)[:, 0:16]), ALU.mult).then_inc(sem("g_kbe"), 1)
                take(("gT", 3, 1), gtr[:, 3, 1, :])
                for hh in range(H):
                    need.wait_ge(*J.freed(("gD", hh)))
                    dd = dec_v[:, hh % 2]
                    for nm, dst in (("gA", AT), ("gQ", atT)):
                        need.wait_ge(psum_full, J.number((nm, hh)))
                        ps = bank((nm, hh))
                        tt(dst[:, hh], ps.rearrange("p (t i) -> p t i", t=NT), dd, ALU.mult).then_inc(psum_free, 1)
                lv = lambda n: cbt("lvl")[:, n * P:(n + 1) * P].unsqueeze(1).broadcast_to([P, NT, P])
                ident = cst("ident").unsqueeze(1).broadcast_to([P, NT, P])
                for hh in range(H):
                    need.wait_ge(*J.freed(("gA", hh)))
                    need.wait_ge(stepped, step(tt(Bm_v[:, hh % 2], AT[:, hh], lv(0), ALU.mult)))
                    tt(gU[:, hh], ident, Bm_v[:, hh % 2], ALU.subtract).then_inc(sem("g_U0"), 1)
                for n in range(1, LEVELS):
                    for hh in range(H):
                        if n == 1 and hh < 2:
                            need.wait_ge(sem("g_U0"), 4)
                        if n > 1 or hh >= 2:
                            k = (n - 1) * H + hh - 2
                            need.wait_ge(psum_full, J.number(("X", k // H + 1, k % H)))
                        tt(Bm_v[:, hh % 2], AT[:, hh], lv(n), ALU.mult).then_inc(sem("g_B"), 1)
                    for hh in range(H):
                        for nm, dst in (("T", gT_), ("U", gU)):
                            if nm == "T" and n == LEVELS - 1:
                                continue
                            need.wait_ge(psum_full, J.number((nm, n, hh)))
                            ps = bank((nm, n, hh)).rearrange("p (t i) -> p t i", t=NT)
                            if nm == "T":
                                need.wait_ge(*J.freed(("T0", hh)))
                            tt(dst[:, hh], dst[:, hh], ps, ALU.subtract).then_inc(psum_free, 1)
                egl = stat("egcgl", 32)[:, 16:32]
                need.wait_ge(stepped, step(e.memset(state, 0.0)))
                for t in range(NT):
                    need.wait_ge(psum_full, J.number(("gS", t)))
                    ps = bank(("gS", t))
                    for hh in range(H):
                        q = hh % 2
                        pp = slice(q * DH, (q + 1) * DH)
                        s_ = state[pp, hh, :]
                        src = ps[pp, (hh // 2) * DH:(hh // 2 + 1) * DH]
                        if t == 0:
                            ins = e.tensor_copy(s_, src)
                        else:
                            if hh == 0:
                                need.wait_ge(*J.freed(("gS", t - 1)))
                            ins = stt(s_, s_, egl[pp, t * H + hh:t * H + hh + 1], src, ALU.mult, ALU.add)
                        if hh < H - 1:
                            step(ins)
                    need.wait_ge(stepped, step.count)
                    ins.then_inc(psum_free, 1)
                for t in range(NT):
                    need.wait_ge(*J.freed(("go", t)))
                post("gdn", 1, "gdn_norm")
                yb = ycol(1)
                tt(yb, yb, zgate, ALU.mult).then_inc(sem("y_done"), 1)
                phase(e, need, 1)
                need.wait_ge(*J.freed(("kcvc",)))
                for half in range(2):
                    i0 = 16 * half
                    src = kcvcT[:, i0:i0 + 16 * NCMP].rearrange("p (n i) -> p i n", i=16)
                    tt(blk[:, i0:i0 + 16, :], src,
                       pe_c[:, i0:i0 + 16].unsqueeze(2).broadcast_to([P, 16, NCMP]), ALU.add)\
                        .then_inc(sem("blocks"), 1)
                step(e.tensor_copy(nX[:, :, 5, :], small[:, :, 0:DH]))
                step(e.tensor_copy(nV[:, :, 1, :], small[:, :, DH:P]))
                need.wait_ge(sem("gate_exp"), 1)
                gt = small[:, :, 128:140]
                need.wait_ge(stepped, step(ts(gt, gt, 1.0, None, ALU.add)))
                need.wait_ge(stepped, step(e.reciprocal(gt, gt)))
                g0 = small[:, 0, 128:140].rearrange("p (h b) -> p b h", b=3)[:, 0, :]
                need.wait_ge(stepped, step(ts(g0, g0, cst("valid"), None, ALU.mult)))
                hd = DH // 2
                need.wait_ge(*J.freed(("nq", 0)))
                need.wait_ge(*J.freed(("nq", 1)))
                need.wait_ge(*J.freed(("ksvs", 1)))
                need.wait_ge(stepped, step.count)
                nXf = nX.rearrange("p t h d -> p (t h) d")
                nsq = view(12752, 24, DH)
                need.wait_ge(stepped, step(tt(nsq, nXf, nXf, ALU.mult)))
                rsum(stat("n_ss", 24), nsq, AXX).then_inc(sem("n_ss"), 1)
                need.wait_ge(sem("n_rs"), 1)
                need.wait_ge(stepped, step(tt(nXf, nXf, stat("n_rs", 24).unsqueeze(2).broadcast_to([P, 24, DH]), ALU.mult)))
                nXt = nX.rearrange("p t h d -> p t (h d)")
                need.wait_ge(stepped, step(tt(nXt, nXt, rowp("nsa_gain").unsqueeze(1).broadcast_to([P, NT, 384]), ALU.mult)))
                tA = view(12752, NT, 6, hd)
                tB = view(13776, NT, 6, hd)
                cA = cst("cosA").rearrange("p (t d) -> p t d", t=NT).unsqueeze(2).broadcast_to([P, NT, 6, hd])
                sA = cst("sinA").rearrange("p (t d) -> p t d", t=NT).unsqueeze(2).broadcast_to([P, NT, 6, hd])
                al = slice(None)
                ins = rope(nX, nY, cA, sA, tA, tB, hd,
                           [((al, al, slice(0, 4)), (al, al, slice(0, 4))),
                            ((al, al, slice(4, 6)), (al, al, slice(4, 8, 2))),
                            ((al, al, slice(4, 6)), (al, al, slice(5, 8, 2)))])
                ins.then_inc(sem("nsa_rope"), 1)
                lam = rowp("lam").rearrange("p (a d) -> p a d", a=4)
                lt = stat("lamt", 64).rearrange("p (a d) -> p a d", a=2)
                need.wait_ge(stepped, step(tt(lt, lam[:, 0:4:2, :], lam[:, 1:4:2, :], ALU.mult)))
                rsum(stat("lamv", 2), lt, AXX).then_inc(sem("lam_dots"), 1)
                need.wait_ge(sem("lam_exp"), 1)
                lw, lv_ = stat("lamw", 2), stat("lamv", 2)
                need.wait_ge(stepped, step(tt(lw[:, 1:2], lv_[:, 1:2], lv_[:, 0:1], ALU.subtract)))
                need.wait_ge(stepped, step(tt(lw[:, 1:2], lw[:, 1:2], rowp("lam_init")[:, 0:1], ALU.subtract)))
                step(ts(lw[:, 0:1], lw[:, 1:2], 0.0, 1.0, ALU.mult, ALU.add))
                for w in range(2):
                    for tp in range(2):
                        need.wait_ge(*J.freed(("dp", w, tp)))
                need.wait_ge(sem("nsa_rope"), 1)
                dXf = dX.rearrange("p t (h d) -> p (t h) d", d=32)
                dsq = dY.rearrange("p t (h d) -> p (t h) d", d=32)
                need.wait_ge(stepped, step(tt(dsq, dXf, dXf, ALU.mult)))
                rsum(stat("d_ss", 64), dsq, AXX).then_inc(sem("d_ss"), 1)
                need.wait_ge(sem("d_rs"), 1)
                need.wait_ge(stepped, step(tt(dXf, dXf, stat("d_rs", 64).unsqueeze(2).broadcast_to([P, 64, 32]), ALU.mult)))
                need.wait_ge(stepped, step(tt(dX, dX, rowp("diff_gain").unsqueeze(1).broadcast_to([P, NT, 512]), ALU.mult)))
                qd = DH // 4
                dX4 = dX.rearrange("p t (h d) -> p t h d", d=32)
                dY4 = dY.rearrange("p t (h d) -> p t h d", d=32)
                tA = tmpA.rearrange("p (t h d) -> p t h d", t=NT, d=qd)
                tB = tmpB.rearrange("p (t h d) -> p t h d", t=NT, d=qd)
                cD = cst("cosD").rearrange("p (t d) -> p t d", t=NT).unsqueeze(2).broadcast_to([P, NT, 16, qd])
                sD = cst("sinD").rearrange("p (t d) -> p t d", t=NT).unsqueeze(2).broadcast_to([P, NT, 16, qd])
                ins = rope(dX4, dY4, cD, sD, tA, tB, qd, [((al, al, al), (al, al, al))])
                ins.then_inc(sem("diff_rope"), 1)
                take(("dp", 2, 1), dV[:, 2:4, :], src=two)
                take(("mqk", 1), mkT)
                step(e.memset(mV[:, :, :, DH:DH + 1], 1.0))
                for tp in range(2):
                    need.wait_ge(psum_full, J.number(("mv", tp)))
                    ps = bank(("mv", tp)).rearrange("p (t h d) -> p t h d", t=2, h=H)
                    for q in range(2):
                        ins = e.tensor_copy(mV[:, 2 * tp + q, :, 0:DH], ps[:, q])
                        if q == 0:
                            step(ins)
                    ins.then_inc(psum_free, 1)
                for j in range(2):
                    take(("hid", j), hid_n[0:NCMP, j, :], src=lambda ps: ps[0:NCMP, 0:P])
                c2 = 2.0 * float(np.sqrt(2.0 / np.pi))
                hb, ht = hid_n[0:NCMP], hid_t[0:NCMP]
                need.wait_ge(*J.freed(("hid", 1)))
                need.wait_ge(stepped, step(tt(ht, hb, hb, ALU.mult)))
                need.wait_ge(stepped, step(ts(ht, ht, 0.044715 * c2, c2, ALU.mult, ALU.add)))
                tt(ht, ht, hb, ALU.mult).then_inc(sem("gelu_arg"), 1)
                need.wait_ge(sem("gelu_exp"), 1)
                need.wait_ge(stepped, step(ts(ht, ht, 1.0, None, ALU.add)))
                need.wait_ge(stepped, step(e.reciprocal(ht, ht)))
                tt(hb, hb, ht, ALU.mult).then_inc(sem("cmp_hidden"), 1)
                for pr in (1, 3):
                    take(("nT", pr), nTr[:, pr, :], mul=0.125 if pr == 1 else None)
                for pr in (1, 3):
                    take(("dT", pr), dTr[:, pr, :], mul=float(32 ** -0.5) if pr == 1 else None)
                take(("hidT",), hidb[:, :, 0:NCMP],
                     src=lambda ps: ps[:, 0:64].rearrange("p (j n) -> p j n", j=2)[:, :, 0:NCMP])
                take(("cmp", 0), ckn[0:NCMP, 0, :], src=lambda ps: ps[0:NCMP, 0:DH])
                take(("cmp", 1), cvn[0:NCMP, :], src=lambda ps: ps[0:NCMP, 0:DH])
                need.wait_ge(*J.freed(("cmp", 0)))
                ck = ckn[0:NCMP, 0, :]
                need.wait_ge(stepped, step(tt(ckn[0:NCMP, 1, :], ck, ck, ALU.mult)))
                rsum(stat("ck_ss", 1)[0:NCMP], ckn[0:NCMP, 1, :], AXX).then_inc(sem("ck_ss"), 1)
                need.wait_ge(sem("ck_rs"), 1)
                need.wait_ge(stepped, step(ts(ck, ck, stat("ck_rs", 1)[0:NCMP], None, ALU.mult)))
                need.wait_ge(stepped, step(tt(ck, ck, rowp("cmp_gain")[0:NCMP], ALU.mult)))
                cC, sC = cst("cosC")[0:NCMP], cst("sinC")[0:NCMP]
                tA, tB = tmpA[0:NCMP, 0:hd], tmpB[0:NCMP, 0:hd]
                step(tt(tA, ck[:, 0:hd], cC, ALU.mult))
                step(tt(tB, ck[:, hd:DH], sC, ALU.mult))
                need.wait_ge(stepped, step.count)
                for d in range(2):
                    step(tt(ckr[0:NCMP, d, 0:hd], tA, tB, ALU.subtract))
                need.wait_ge(stepped, step.count)
                step(tt(tA, ck[:, hd:DH], cC, ALU.mult))
                step(tt(tB, ck[:, 0:hd], sC, ALU.mult))
                need.wait_ge(stepped, step.count)
                step(tt(ckr[0:NCMP, 0, hd:DH], tA, tB, ALU.add))
                tt(ckr[0:NCMP, 1, hd:DH], tA, tB, ALU.add).then_inc(sem("cmp_k"), 1)
                mt1 = stat("mt1", 32)
                m1 = mt1.rearrange("p (w t h) -> p w t h", w=2, h=H)
                for w, nm in enumerate(("i_bias", "f_bias")):
                    step(tt(m1[:, w], small[:, :, 148 + 4 * w:152 + 4 * w], rb(nm), ALU.add))
                need.wait_ge(stepped, step.count)
                ts(mt1, mt1, 1.0 / 15.0, None, ALU.mult).then_inc(sem("m_gates"), 1)
                need.wait_ge(sem("m_exp"), 1)
                need.wait_ge(stepped, step(ts(mt1, mt1, 1.0, None, ALU.add)))
                need.wait_ge(stepped, step(e.reciprocal(mt1, mt1)))
                need.wait_ge(stepped, step(ts(mt1, mt1, 30.0, -15.0, ALU.mult, ALU.add)))
                mt2 = stat("mt2", 16)
                e.tensor_copy(mt2, mt1[:, 16:32]).then_inc(sem("m_capped"), 1)
                need.wait_ge(sem("m_exp"), 2)
                ts(mt2, mt2, 1.0, None, ALU.add).then_inc(sem("m_one_plus"), 1)
                need.wait_ge(sem("m_ln"), 1)
                ts(stat("lf", 16), mt2, -1.0, None, ALU.mult).then_inc(sem("m_logf"), 1)
                take(("kcT",), kcT[:, 0:NCMP], src=lambda ps: ps[:, 0:NCMP])
                def gate_sums():
                    take(("mF",), stat("F", 16), src=lambda ps: ps[:, 0:16])
                    need.wait_ge(*J.freed(("mF",)))
                    tt(stat("ma", 16), mt1[:, 0:16], stat("F", 16), ALU.subtract).then_inc(sem("m_a"), 1)

                def gate_maxima():
                    take(("aT",), aT[0:H, :], src=lambda ps: ps[0:H, :])
                    need.wait_ge(*J.freed(("aT",)))
                    need.wait_ge(stepped, step(e.tensor_tensor_scan(nMT[0:H, :], aT[0:H, :], aT[0:H, :], 0.0, ALU.max, ALU.max)))
                    ts(nMT[0:H, :], nMT[0:H, :], -1.0, None, ALU.mult).then_inc(sem("m_negM"), 1)

                def negative_maxima():
                    need.wait_ge(*J.freed(("MT",)))
                    tt(stat("enm", 16), stat("nM", 16), stat("F", 16), ALU.subtract).then_inc(sem("m_negm"), 1)

                def output_gate():
                    need.wait_ge(*J.freed(("mo", 1)))
                    need.wait_ge(stepped, step(ts(mO, mO, 1.0, None, ALU.add)))
                    step(e.reciprocal(mO, mO))

                attention_out(ATT, {6: gate_sums, 10: gate_maxima, 15: negative_maxima, 20: output_gate})
                e.drain().then_inc(sem("y_done"), 1)
                need.wait_ge(sem("y_done"), 2)
                post("diff", 3, "diff_norm")
                yd = ycol(3)
                ts(yd, yd, rowp("lam_init")[:, 1:2], None, ALU.mult).then_inc(sem("y_done"), 1)
                need.wait_ge(sem("mem_rs"), 1)
                for t in range(NMT):
                    ts(memn[:, t, :], memn[:, t, :], stat("mem_rs", 2)[:, t:t + 1], None, ALU.mult)\
                        .then_inc(sem("mem_norm"), 1)
                need.wait_ge(sem("m_expm"), 1)
                enm = v3(stat("enm", 16))
                def weights(hh):
                    need.wait_ge(*J.freed(("mD", hh)))
                    for j in range(NT):
                        need.wait_ge(psum_full, J.number(("mS", hh, j)))
                        ps = bank(("mS", hh, j))
                        w = Em[hh % 2][:, j, j * P:S]
                        tt(w, w, ps[:, j * P:S], ALU.mult).then_inc(psum_free, 1)

                def values(hh):
                    if hh:
                        need.wait_ge(*J.freed(("mO", hh - 1)))
                    need.wait_ge(psum_full, J.number(("mO", hh)))
                    ps = bank(("mO", hh))[:, 0:4 * 65].rearrange("p (t n) -> p t n", t=NT)
                    dn = stat("den", 4)
                    need.wait_ge(stepped, step.count)
                    need.wait_ge(stepped, step(ts(dn.unsqueeze(2), ps[:, :, DH:DH + 1], -1.0, None, ALU.mult)))
                    need.wait_ge(stepped, step(tt(dn.unsqueeze(2), dn.unsqueeze(2), ps[:, :, DH:DH + 1], ALU.max)))
                    need.wait_ge(stepped, step(tt(dn, dn, enm[:, :, hh], ALU.max)))
                    need.wait_ge(stepped, step(e.reciprocal(dn, dn)))
                    tt(y[:, :, 2 * GW + hh * DH:2 * GW + (hh + 1) * DH], ps[:, :, 0:DH],
                              dn.unsqueeze(2).broadcast_to([P, NT, DH]), ALU.mult).then_inc(psum_free, 1)

                for hh in range(H + 1):
                    if hh < H:
                        weights(hh)
                    if hh:
                        values(hh - 1)
                    if hh == 1:
                        for k in range(1, KD, 2):
                            take(("memT", k), memT[:, k, :], src=lambda ps: ps[:, 0:MEM],
                                 mul=col[:, col_ln("mem") + k:col_ln("mem") + k + 1])
                    if hh == 2:
                        for k in YT_EARLY[1::2]:
                            take(("yT", k), hnT[:, k, :])
                need.wait_ge(*J.freed(("mO", H - 1)))
                take(("xk",), xK, src=two)
                post("mlstm", 2, "mlstm_norm")
                yc = ycol(2)
                tt(yc, yc, mO, ALU.mult).then_inc(sem("y_done"), 1)
                need.wait_ge(*J.freed(("xk",)))
                head_norm("xk", xK, NMT, ktmp)
                phase(e, need, 3)
                take(("yT", 5), hnT[:, 5, :])
                for u in range(4):
                    for tp in range(2):
                        hh_ = h_res[:, 2 * tp:2 * tp + 2, u * 256:(u + 1) * 256]
                        need.wait_ge(psum_full, J.number(("wo", u, tp)))
                        ps = bank(("wo", u, tp))
                        tt(hh_, hh_, two(ps), ALU.add).then_inc(psum_free, 1)
                need.wait_ge(*J.freed(("wo", 3, 1)))
                for k in YT_LATE:
                    need.wait_ge(*J.freed(("yT", k)))
                scale_norm("xa")
                hT("xa")
                take(("xq", 1), xQ[:, 2:4, :], src=two)
                need.wait_ge(*J.freed(("xq", 0)))
                need.wait_ge(*J.freed(("xq", 1)))
                need.wait_ge(sem("hn_xa"), 4)
                head_norm("xq", xQ, NT, xtmp[:, 0:NT * H * DH].rearrange("p (a d) -> p a d", d=DH))
                for hp in range(2):
                    take(("xkT", hp), xkT[:, hp, :], src=lambda ps: ps[:, 0:MEM])
                attention_out(XATT)
                take(("xoT", 1), xoT[:, 1, :])
                for t in range(NT):
                    for c in range(2):
                        hh_ = h_res[:, t, c * 512:(c + 1) * 512]
                        need.wait_ge(psum_full, J.number(("xo", t, c)))
                        ps = bank(("xo", t, c))
                        tt(hh_, hh_, ps, ALU.add).then_inc(psum_free, 1)
                need.wait_ge(*J.freed(("xo", 3, 1)))
                scale_norm("moe")
                phase(e, need, 4)
                hT("moe")
                lg = stat("logits", NT * 36).rearrange("p (t n) -> p t n", t=NT)
                for t in range(NT):
                    take(("route", t), lg[:, t, :], src=lambda ps: ps[:, 0:36])
                need.wait_ge(*J.freed(("route", NT - 1)))
                bias = row[:, ROW["b_group"][0]:ROW["b_expert"][1]].unsqueeze(1).broadcast_to([P, NT, 36])
                need.wait_ge(stepped, step(tt(lg, lg, bias, ALU.add)))
                gp = stat("gpad", NT * 8).rearrange("p (t n) -> p t n", t=NT)
                step(e.memset(gp, NEG))
                need.wait_ge(stepped, step.count)
                need.wait_ge(stepped, step(e.tensor_copy(gp[:, :, 0:4], lg[:, :, 0:4])))
                m8 = stat("m8", NT * 8).rearrange("p (t n) -> p t n", t=NT)
                i8 = stat("i8", NT * 8).rearrange("p (t n) -> p t n", t=NT).bitcast(U32)
                for t in range(NT):
                    step(e.max(m8[:, t, :], gp[:, t, :]))
                need.wait_ge(stepped, step.count)
                for t in range(NT):
                    step(e.max_index(i8[:, t, :], m8[:, t, :], gp[:, t, :]))
                need.wait_ge(stepped, step.count)
                rexp = stat("r_exp", 20)
                gi = stat("gidx", NT)
                step(e.tensor_copy(gi.unsqueeze(2), i8[:, :, 0:1]))
                need.wait_ge(stepped, step(tt(rexp[:, 0:16].rearrange("p (t n) -> p t n", t=NT), lg[:, :, 0:4],
                          m8[:, :, 0:1].broadcast_to([P, NT, 4]), ALU.subtract)))
                io = stat("iota8", 8)
                io4 = io[:, 0:4].unsqueeze(1).broadcast_to([P, NT, 4])
                goh = stat("goh", 16).rearrange("p (t n) -> p t n", t=NT)
                need.wait_ge(sem("iota"), 1)
                need.wait_ge(stepped, step(tt(goh, io4, gi.unsqueeze(2).broadcast_to([P, NT, 4]), ALU.is_equal)))
                tmp = stat("etmp", NT * 32).rearrange("p (t n) -> p t n", t=NT)
                for t in range(NT):
                    step(tt(tmp[:, t, :].rearrange("p (g x) -> p g x", g=4),
                              lg[:, t, 4:36].rearrange("p (g x) -> p g x", g=4),
                              goh[:, t, :].unsqueeze(2).broadcast_to([P, 4, 8]), ALU.mult))
                need.wait_ge(stepped, step.count)
                for t in range(NT):
                    step(rsum(gp[:, t, :], tmp[:, t, :].rearrange("p (g x) -> p x g", g=4), AXX))
                need.wait_ge(stepped, step.count)
                for t in range(NT):
                    step(e.max(m8[:, t, :], gp[:, t, :]))
                need.wait_ge(stepped, step.count)
                for t in range(NT):
                    step(e.max_index(i8[:, t, :], m8[:, t, :], gp[:, t, :]))
                need.wait_ge(stepped, step.count)
                tt(rexp[:, 16:20].unsqueeze(2), m8[:, :, 1:2], m8[:, :, 0:1], ALU.subtract).then_inc(sem("route_arg"), 1)
                ei = stat("eidx", 2 * NT).rearrange("p (t n) -> p t n", t=NT)
                need.wait_ge(stepped, step(e.tensor_copy(ei, i8[:, :, 0:2])))
                need.wait_ge(sem("route_exp"), 1)
                gpr = stat("gpr", NT)
                wt = stat("wt", 2 * NT).rearrange("p (t n) -> p t n", t=NT)
                need.wait_ge(stepped, step(rsum(gpr, rexp[:, 0:16].rearrange("p (t n) -> p t n", t=NT), AXX)))
                r1 = stat("r1", NT)
                need.wait_ge(stepped, step(ts(r1, rexp[:, 16:20], 1.0, None, ALU.add)))
                need.wait_ge(stepped, step(tt(r1, r1, gpr, ALU.mult)))
                need.wait_ge(stepped, step(e.reciprocal(r1, r1)))
                step(e.tensor_copy(wt[:, :, 0:1], r1.unsqueeze(2)))
                step(tt(wt[:, :, 1:2], r1.unsqueeze(2), rexp[:, 16:20].unsqueeze(2), ALU.mult))
                need.wait_ge(stepped, step.count)
                one = [stat(f"one{n}", NT * NE) for n in range(2)]
                for n, o8 in enumerate((gp, m8)):
                    step(tt(o8, io.unsqueeze(1).broadcast_to([P, NT, 8]),
                            ei[:, :, n:n + 1].broadcast_to([P, NT, 8]), ALU.is_equal))
                need.wait_ge(stepped, step.count)
                for n, o8 in enumerate((gp, m8)):
                    step(tt(one[n].rearrange("p (t g x) -> p t g x", t=NT, g=E_GROUPS),
                            o8.unsqueeze(2).broadcast_to([P, NT, E_GROUPS, E_PER]),
                            goh.unsqueeze(3).broadcast_to([P, NT, E_GROUPS, E_PER]), ALU.mult))
                need.wait_ge(stepped, step.count)
                tt(stat("chosen", NT * NE), one[0], one[1], ALU.add).then_inc(sem("chosen"), 1)
                need.wait_ge(psum_full, J.number(("rank",)))
                ps = bank(("rank",))
                rank, rint, row_ = stat("rank", NT * NE), stat("rint", NT * NE).bitcast(I32), stat("etmp", NT * NE)
                step(e.tensor_copy(rint, ps[:, 0:NT * NE]))
                mx = stat("mx", 1)
                step(e.tensor_reduce(mx, ps[:, NT * NE:(NT + 1) * NE], AXX, ALU.max))
                ts(rank, ps[:, 0:NT * NE], float(NPAIR), None, ALU.mult).then_inc(psum_free, 1)
                need.wait_ge(stepped, step.count)
                need.wait_ge(stepped, step(ts(rint, rint, 6, 10, ALU.logical_shift_right, ALU.logical_shift_left)))
                need.wait_ge(*J.freed(("rank",)))
                need.wait_ge(stepped, step(tt(row_, rint, rank, ALU.add)))
                need.wait_ge(stepped, step(tt(row_.rearrange("p (t n) -> p t n", t=NT),
                                              row_.rearrange("p (t n) -> p t n", t=NT),
                                              cst("place").unsqueeze(1).broadcast_to([P, NT, NE]), ALU.add)))
                posf = stat("posf", 2 * NT)
                for n in range(2):
                    step(tt(one[n], one[n], row_, ALU.mult))
                c7 = stat("c7", ROUNDS - 1)
                step(ts(c7, cst("c64"), mx, None, ALU.is_lt))
                need.wait_ge(stepped, step.count)
                for n in range(2):
                    step(rsum(posf[:, n * NT:(n + 1) * NT], one[n].rearrange("p (t n) -> p t n", t=NT), AXX))
                step(rsum(stat("nr", 1), c7, AXX))
                need.wait_ge(stepped, step.count)
                e.tensor_copy(pos[:], posf).then_inc(sem("placed"), 1)
                ts(rounds[:], stat("nr", 1), 1.0, None, ALU.add).then_inc(sem("routed"), 1)
                need.wait_ge(sem("routed"), 1)
                nr = e.value_load(rounds[0:1, 0:1], min_val=1, max_val=ROUNDS)
                e.drain().then_inc(sem("rowsT_dve"), 1)
                e.drain().then_inc(sem("moe_gated"), 2)
                e.drain().then_inc(sem("y_dve"), 1)

                def rows_T(h, b):
                    e.wait_ge(sem("moe_T"), 2 * h + b + 3)
                    e.tensor_copy(X2T[:, b, 4:8, :], psum[:, 3, :].rearrange("p (k n) -> p k n", k=4))\
                        .then_inc(sem("rowsT_dve"), 1)

                def pair(h, b, ahead):
                    e.wait_ge(sem("moe_silu"), 2 * h + b + 1)
                    e.wait_ge(sem("moe_aT"), 2 * h + b + 1)
                    tt(am, sgl, psum[:, b, FF:2 * FF], ALU.mult).then_inc(sem("moe_gated"), 1)
                    ahead()
                    e.wait_ge(sem("moe_down"), 4 * h + 2 * b + 2)
                    e.wait_ge(sem("y_out"), 32 * h + 16 * b + 16)
                    e.tensor_copy(Ye[:, 512:1024], psum[:, 5, :]).then_inc(sem("y_dve"), 1)

                each_pair(e, nr, rows_T, pair)
                for t in range(NT):
                    need.wait_ge(sem(f"y_rows_in{t}"), 16)
                    for n in range(2):
                        if n:
                            need.wait_ge(sem("h_added"), 2 * t + 1)
                        stt(h_res[:, t, :], Yg[:, t, n, :], wt[:, t, n:n + 1], h_res[:, t, :],
                            ALU.mult, ALU.add).then_inc(sem("h_added"), 1)
                layer_end(e, "dve")

        @block.gpsimd
        def _(e):
            need = Waits(e)
            e.iota(stat("iota8", 8), pattern=[[1, 8]], base=0, channel_multiplier=0,
                   allow_small_or_imprecise_dtypes=True).then_inc(sem("iota_once"), 1)
            e.wait_ge(sem("iota_once"), 1)
            tok4 = tok[:].rearrange("p (n t) o -> p n t o", n=2)
            e.iota(tok4[:, :, :, 0], pattern=[[0, 2], [P, NT]], base=0, channel_multiplier=1)\
                        .then_inc(sem("iota_once"), 1)
            e.iota(tok4[:, :, :, 1], pattern=[[1, 2], [2 * P, NT]], base=0, channel_multiplier=2)\
                        .then_inc(sem("iota_once"), 1)
            e.memset(unused[:, :, 0:1], 0).then_inc(sem("iota_once"), 1)
            e.iota(unused[:, :, 1:2], pattern=[[0, NPAIR], [0, 1]], base=2 * S, channel_multiplier=1)\
                        .then_inc(sem("iota_once"), 1)
            e.wait_ge(sem("iota_once"), 5)
            with e.Fori(0, L) as l:
                need.new_layer()
                e.drain().then_inc(sem("iota"), 1)
                need.wait_ge(sem("rstd_mix"), 1)
                e.memset(raw[:, :, 0:3], 0.0).then_inc(sem("raw_zero"), 1)
                for r in range(ROUNDS):
                    e.dma_start(table[r * P * NPAIR:(r + 1) * P * NPAIR, :].rearrange("(p i) o -> p i o", p=P),
                                unused[:]).then_inc(sem("table_reset"), 16)
                e.dma_start(y_rows[2 * S:2 * S + P, 0:NPAIR * 2].bitcast(U32),
                            unused[:].rearrange("p i o -> p (i o)")).then_inc(sem("y_out"), 16)
                for n in (1, 3, 4):
                    phase(e, need, n)
                e.wait_ge(sem("table_reset"), 16 * ROUNDS)
                e.wait_ge(sem("placed"), 1)
                for j in range(2 * NT):
                    e.indirect_dma_start(table, bass.IndirectOffsetOnAxis(ap=pos[:, j:j + 1], axis=0),
                                         tok[:, j, :], None).then_inc(sem("table_out"), 16)

                def pick(c, j, o):
                    e.tensor_tensor(idx[:, c:c + 1], ids[:, bass.ds(j, 1), o], unused[:, 0, 0:1], ALU.add)\
                        .then_inc(sem("picked"), 1)
                    e.wait_ge(sem("picked"), 1)
                    e.sem_clear(sem("picked"))

                def gather(r, j, b):
                    e.wait_ge(sem("moe_T"), 16 * r + j + 1)
                    pick(b, j, 0)
                    e.indirect_dma_start(X2[:, b, :], None, hn_rows,
                                         bass.IndirectOffsetOnAxis(ap=idx[:, b:b + 1], axis=0))\
                        .then_inc(sem(f"rows_in{b}"), 16)

                def scatter(r, j):
                    e.wait_ge(sem("y_act"), 16 * r + j + 2)
                    e.wait_ge(sem("y_dve"), 16 * r + j + 2)
                    pick(2, j, 1)
                    e.indirect_dma_start(y_rows, bass.IndirectOffsetOnAxis(ap=idx[:, 2:3], axis=0),
                                         Ye, None).then_inc(sem("y_out"), 16)

                e.wait_ge(sem("routed"), 1)
                nr = e.value_load(rounds[0:1, 0:1], min_val=1, max_val=ROUNDS)
                e.wait_ge(sem("table_out"), 16 * 2 * NT)
                e.wait_ge(sem("hn_rows_out"), 16 * NT)
                with e.Fori(0, nr) as r:
                    e.dma_start(ids, table[bass.ds(r * P * NPAIR, P * NPAIR), :].rearrange("(p i) o -> p i o", p=P))\
                        .then_inc(sem("ids_in"), 16)
                    e.wait_ge(sem("ids_in"), 16 * r + 16)
                    gather(r, 0, 0)
                    gather(r, 1, 1)
                    with e.Fori(0, NPAIR // 2 - 1) as i:
                        gather(r, 2 * i + 2, 0)
                        scatter(r, 2 * i)
                        gather(r, 2 * i + 3, 1)
                        scatter(r, 2 * i + 1)
                    scatter(r, NPAIR - 2)
                    scatter(r, NPAIR - 1)
                e.wait_ge(sem("layer_done"), 4)
                e.dma_reset()
                layer_sems = [sems[name].num for name in sems if name not in keep]
                assert layer_sems == list(range(layer_sems[0], layer_sems[0] + len(layer_sems)))
                e.sem_clear(range(layer_sems[0], layer_sems[0] + len(layer_sems)))
                for name in ("sp", "pe", "act", "dve"):
                    e.drain().then_inc(sem("layer_go_" + name), 1)
    return nc


_OUT = (1, S, D)


def kernel(**inputs):
    import math

    import concourse.bacc as _bacc
    import ml_dtypes
    from concourse.bass_utils import run_bass_kernel_spmd as _run

    a = {k: np.ascontiguousarray(v) for k, v in inputs.items()}
    f, b = const_tables()
    g = a["nsa_qk_gain"]
    dg, xg = a["diff_qk_gain"], a["xattn_qk_gain"]
    init = np.array([[0.8 - 0.6 * math.exp(-0.3 * l) for _ in range(1)] for l in range(L)], np.float32)
    init = np.concatenate([init, np.array([[1.0 - (0.8 - 0.6 * math.exp(-0.3 * l))] for l in range(L)], np.float32)], 1)
    rows = np.concatenate([
        np.tile(g[:, 0], (1, 4)), g[:, 2], g[:, 3], g[:, 1], np.tile(dg[:, 0], (1, 8)), np.tile(dg[:, 1], (1, 8)),
        np.tile(xg[:, 0], (1, 4)), np.tile(xg[:, 1], (1, 4)), a["gdn_norm"], a["mlstm_norm"], a["diff_norm"],
        a["mlstm_i_bias"], a["mlstm_f_bias"], a["gdn_a_log"], a["gdn_dt_bias"], a["diff_lambda"].reshape(L, -1),
        a["moe_b_group"], a["moe_b_expert"], init], axis=1)
    rows = np.ascontiguousarray(np.broadcast_to(rows[:, None, :], (L, P, NROW)))
    cols = np.concatenate([a[n].reshape(L, P, KD) for n in ("ln_mix", "ln_xattn", "ln_moe", "ln_mem")]
                          + [a["gdn_conv"].reshape(L, 4, 6, P).transpose(0, 3, 2, 1).reshape(L, P, 24)], axis=2)
    arrays = {"x": a["x"], "mem": a["mem"], "rows": rows, "cols": np.ascontiguousarray(cols),
              "const_f": f, "const_b": b.astype(ml_dtypes.bfloat16),
              "pe_t": np.ascontiguousarray(a["nsa_cmp_pe"].transpose(0, 1, 3, 2).reshape(L, P, 32)),
              "ln_moe_rows": np.ascontiguousarray(np.broadcast_to(a["ln_moe"][:, None, :], (L, P, D))),
              "w_route": np.concatenate([a["moe_w_group"], a["moe_w_expert"]], axis=2)}
    for n in ("w_in", "w_out", "nsa_cmp_w1", "nsa_cmp_w2", "xattn_wq", "xattn_wkv", "xattn_wo",
              "moe_w1", "moe_w3", "moe_w2"):
        arrays[n] = a[n]
    nc = _bacc.Bacc("TRN2", target_bir_lowering=False, num_devices=1)
    t_in = {n: nc.dram_tensor(n, v.shape, mybir.dt.from_np(v.dtype), kind="ExternalInput").ap()
            for n, v in arrays.items()}
    out = nc.dram_tensor("out_h", _OUT, F32, kind="ExternalOutput").ap()
    build(nc, t_in, out)
    r = _run(nc, [arrays], core_ids=[0])
    return r.results[0]["out_h"]
```
